# Optimizing a Trainium2 kernel written in Bass

```python
import jax, jax.numpy as jnp
from jax import lax
import numpy as np

D_MODEL = 1024
BATCH = 1
SEQ = 512
DEPTH = 2

GRID_W = 64
CTX_LEN = 256
HEAD_DIM = 64
A_HEADS = 8
A_KV_HEADS = 2
A_GROUP = A_HEADS // A_KV_HEADS
A_BLOCK = 128
ROPE_THETA = 10000.0
B_HEADS = 8
NA_ROWS = 8
NA_COLS = 16
C_GROUPS = 4
C_GROUP_W = 128
BRANCH_W = 512
N_BRANCH = 3
D_FF = -(-8 * D_MODEL // (3 * 256)) * 256
IN_SIZES = (A_HEADS * HEAD_DIM, A_KV_HEADS * HEAD_DIM, A_KV_HEADS * HEAD_DIM,
            B_HEADS * HEAD_DIM, B_HEADS * HEAD_DIM, B_HEADS * HEAD_DIM,
            C_GROUPS * C_GROUP_W, N_BRANCH * D_MODEL)
IN_SPLITS = tuple(sum(IN_SIZES[:i + 1]) for i in range(len(IN_SIZES) - 1))
D_IN = sum(IN_SIZES)
DEEPNORM_ALPHA = (2.0 * DEPTH) ** 0.25
DEEPNORM_BETA = (8.0 * DEPTH) ** -0.25
LN_EPS = 1e-6
RMS_EPS = 1e-6

kernel_name = 'hybrid_gqa_natten_fnet_dit_block'

def _layernorm(x, g=None, b=None):
    xf = x.astype(jnp.float32)
    mu = xf.mean(-1, keepdims=True)
    var = jnp.square(xf - mu).mean(-1, keepdims=True)
    y = (xf - mu) * lax.rsqrt(var + LN_EPS)
    if g is not None:
        y = y * g.astype(jnp.float32) + b.astype(jnp.float32)
    return y.astype(x.dtype)

def _rmsnorm(x, g):
    xf = x.astype(jnp.float32)
    y = xf * lax.rsqrt(jnp.mean(jnp.square(xf), -1, keepdims=True) + RMS_EPS)
    return (y * g.astype(jnp.float32)).astype(x.dtype)

def _modulate(h, shift, scale):
    return h * (1.0 + scale) + shift

def _rope_2d(x, rows, cols):
    quarter = HEAD_DIM // 4
    half = HEAD_DIM // 2
    freqs = ROPE_THETA ** (-jnp.arange(quarter, dtype=jnp.float32) / quarter)

    def rot(xa, pos):
        ang = pos.astype(jnp.float32)[:, None] * freqs
        cos = jnp.cos(ang)[None, :, None, :].astype(x.dtype)
        sin = jnp.sin(ang)[None, :, None, :].astype(x.dtype)
        x1, x2 = xa[..., :quarter], xa[..., quarter:]
        return jnp.concatenate([x1 * cos - x2 * sin, x1 * sin + x2 * cos], axis=-1)

    return jnp.concatenate([rot(x[..., :half], rows), rot(x[..., half:], cols)], axis=-1)

def _gqa(q, k, v):
    s = jnp.einsum('bqkgd,bskd->bkgqs', q, k).astype(jnp.float32) * (HEAD_DIM ** -0.5)
    p = jax.nn.softmax(s, axis=-1).astype(v.dtype)
    return jnp.einsum('bkgqs,bskd->bqkgd', p, v)

def _mha(q, k, v):
    s = jnp.einsum('bqhd,bshd->bhqs', q, k).astype(jnp.float32) * (HEAD_DIM ** -0.5)
    p = jax.nn.softmax(s, axis=-1).astype(v.dtype)
    return jnp.einsum('bhqs,bshd->bqhd', p, v)

def _neighbourhood_attn(q, k, v, kc, vc, rpb, rows_n):
    B, L, H, dh = q.shape
    kr = min(NA_ROWS, rows_n)
    kcn = NA_COLS
    cols = jnp.arange(GRID_W)
    col_start = jnp.clip(cols - kcn // 2, 0, GRID_W - kcn)
    col_idx = col_start[:, None] + jnp.arange(kcn)[None, :]
    dc = col_idx - cols[:, None] + (NA_COLS - 1)
    k_grid = k.reshape(B, rows_n, GRID_W, H, dh)
    v_grid = v.reshape(B, rows_n, GRID_W, H, dh)
    q_rows = q.reshape(B, rows_n, GRID_W, H, dh).transpose(1, 0, 2, 3, 4)
    scale = HEAD_DIM ** -0.5

    def row_fn(args):
        r, q_r = args
        r0 = jnp.clip(r - kr // 2, 0, rows_n - kr)
        k_band = lax.dynamic_slice_in_dim(k_grid, r0, kr, axis=1)
        v_band = lax.dynamic_slice_in_dim(v_grid, r0, kr, axis=1)
        k_win = k_band[:, :, col_idx]
        v_win = v_band[:, :, col_idx]
        s_nb = jnp.einsum('bqhd,brqjhd->bhqrj', q_r, k_win).astype(jnp.float32) * scale
        dr = r0 + jnp.arange(kr) - r + (NA_ROWS - 1)
        bias = rpb[:, dr][:, :, dc].transpose(0, 2, 1, 3)
        s_nb = s_nb + bias[None].astype(jnp.float32)
        s_ctx = jnp.einsum('bqhd,bshd->bhqs', q_r, kc).astype(jnp.float32) * scale
        s = jnp.concatenate([s_nb.reshape(B, H, GRID_W, kr * kcn), s_ctx], axis=-1)
        p = jax.nn.softmax(s, axis=-1).astype(v.dtype)
        p_nb = p[..., :kr * kcn].reshape(B, H, GRID_W, kr, kcn)
        p_ctx = p[..., kr * kcn:]
        return (jnp.einsum('bhqrj,brqjhd->bqhd', p_nb, v_win)
                + jnp.einsum('bhqs,bshd->bqhd', p_ctx, vc))

    out = lax.map(row_fn, (jnp.arange(rows_n), q_rows))
    return out.transpose(1, 0, 2, 3, 4).reshape(B, L, H * dh)

def _fourier_mix(u):
    B, L, _ = u.shape
    uf = u.astype(jnp.float32).reshape(B, L, C_GROUPS, C_GROUP_W)
    y = jnp.fft.fft2(uf, axes=(1, 3), norm='ortho').real
    return y.reshape(B, L, C_GROUPS * C_GROUP_W).astype(u.dtype)

def _merge(gz, oa, ob, oc, w_branch, w_out):
    ga, gb, gf = jnp.split(jax.nn.sigmoid(gz), N_BRANCH, axis=-1)
    y = ga * (oa @ w_branch[0]) + gb * (ob @ w_branch[1]) + gf * (oc @ w_branch[2])
    return y @ w_out

def _token_mixers(h, hc, w_in, q_norm, k_norm, rpb, w_branch, w_out, rows, cols, rows_n, with_ctx_out):
    B, L, _ = h.shape
    Lc = hc.shape[1]
    qa, ka, va, qb, kb, vb, uc, gz = jnp.split(h @ w_in, IN_SPLITS, axis=-1)
    qac, kac, vac, qbc, kbc, vbc, ucc, gzc = jnp.split(hc @ w_in, IN_SPLITS, axis=-1)

    qa = _rope_2d(_rmsnorm(qa.reshape(B, L, A_HEADS, HEAD_DIM), q_norm), rows, cols)
    ka = _rope_2d(_rmsnorm(ka.reshape(B, L, A_KV_HEADS, HEAD_DIM), k_norm), rows, cols)
    va = va.reshape(B, L, A_KV_HEADS, HEAD_DIM)
    kac = _rmsnorm(kac.reshape(B, Lc, A_KV_HEADS, HEAD_DIM), k_norm)
    vac = vac.reshape(B, Lc, A_KV_HEADS, HEAD_DIM)
    k_all = jnp.concatenate([kac, ka], axis=1)
    v_all = jnp.concatenate([vac, va], axis=1)
    n_blk = L // A_BLOCK
    q_blocks = qa.reshape(B, n_blk, A_BLOCK, A_KV_HEADS, A_GROUP, HEAD_DIM).transpose(1, 0, 2, 3, 4, 5)
    oa = lax.map(lambda qq: _gqa(qq, k_all, v_all), q_blocks)
    oa = oa.transpose(1, 0, 2, 3, 4, 5).reshape(B, L, BRANCH_W)

    kbc = kbc.reshape(B, Lc, B_HEADS, HEAD_DIM)
    vbc = vbc.reshape(B, Lc, B_HEADS, HEAD_DIM)
    ob = _neighbourhood_attn(qb.reshape(B, L, B_HEADS, HEAD_DIM), kb.reshape(B, L, B_HEADS, HEAD_DIM),
                             vb.reshape(B, L, B_HEADS, HEAD_DIM), kbc, vbc, rpb, rows_n)

    oc = _fourier_mix(uc)

    y = _merge(gz, oa, ob, oc, w_branch, w_out)
    if not with_ctx_out:
        return y, None

    qac = _rmsnorm(qac.reshape(B, Lc, A_HEADS, HEAD_DIM), q_norm).reshape(B, Lc, A_KV_HEADS, A_GROUP, HEAD_DIM)
    oac = _gqa(qac, kac, vac).reshape(B, Lc, BRANCH_W)
    obc = _mha(qbc.reshape(B, Lc, B_HEADS, HEAD_DIM), kbc, vbc).reshape(B, Lc, BRANCH_W)
    occ = _fourier_mix(ucc)
    yc = _merge(gzc, oac, obc, occ, w_branch, w_out)
    return y, yc

def _swiglu(h, w_gu, w_down):
    g, u = jnp.split(h @ w_gu, 2, axis=-1)
    return (jax.nn.silu(g) * u) @ w_down

def setup_inputs(seed: int = 0) -> dict:
    key = jax.random.key(seed)
    ks = jax.random.split(key, 18)

    def nrm(k, shape, s):
        return jax.random.normal(k, shape, jnp.float32) * s

    D = D_MODEL
    return {
        'x': nrm(ks[0], (BATCH, SEQ, D), 1.0),
        'c': nrm(ks[1], (BATCH, D), 1.0),
        'ctx': nrm(ks[2], (BATCH, CTX_LEN, D), 1.0),
        'c_ctx': nrm(ks[3], (D,), 1.0),
        'w_ada': nrm(ks[4], (DEPTH, D, 6 * D), 0.5 * D ** -0.5),
        'b_ada': nrm(ks[5], (DEPTH, 6 * D), 0.02),
        'w_in': nrm(ks[6], (DEPTH, D, D_IN), D ** -0.5),
        'q_norm': 1.0 + nrm(ks[7], (DEPTH, HEAD_DIM), 0.02),
        'k_norm': 1.0 + nrm(ks[8], (DEPTH, HEAD_DIM), 0.02),
        'rpb': nrm(ks[9], (DEPTH, B_HEADS, 2 * NA_ROWS - 1, 2 * NA_COLS - 1), 0.2),
        'w_branch': nrm(ks[10], (DEPTH, N_BRANCH, BRANCH_W, D), BRANCH_W ** -0.5),
        'w_out': nrm(ks[11], (DEPTH, D, D), D ** -0.5 * DEEPNORM_BETA),
        'ln1_g': 1.0 + nrm(ks[12], (DEPTH, D), 0.02),
        'ln1_b': nrm(ks[13], (DEPTH, D), 0.02),
        'w_gu': nrm(ks[14], (DEPTH, D, 2 * D_FF), D ** -0.5),
        'w_down': nrm(ks[15], (DEPTH, D_FF, D), D_FF ** -0.5 * DEEPNORM_BETA),
        'ln2_g': 1.0 + nrm(ks[16], (DEPTH, D), 0.02),
        'ln2_b': nrm(ks[17], (DEPTH, D), 0.02),
    }

def reference(x, c, ctx, c_ctx, w_ada, b_ada, w_in, q_norm, k_norm, rpb, w_branch, w_out,
              ln1_g, ln1_b, w_gu, w_down, ln2_g, ln2_b):
    L = x.shape[1]
    rows_n = L // GRID_W
    pos = jnp.arange(L, dtype=jnp.int32)
    rows = pos // GRID_W
    cols = pos % GRID_W
    xc = ctx
    c_act = jax.nn.silu(c)
    cc_act = jax.nn.silu(c_ctx)
    for l in range(DEPTH):
        with_ctx = l < DEPTH - 1
        mods = jnp.split(c_act @ w_ada[l] + b_ada[l], 6, axis=-1)
        sh1, sc1, g1, sh2, sc2, g2 = [t[:, None, :] for t in mods]
        shc1, scc1, gc1, shc2, scc2, gc2 = jnp.split(cc_act @ w_ada[l] + b_ada[l], 6, axis=-1)

        h = _modulate(_layernorm(x), sh1, sc1)
        hc = _modulate(_layernorm(xc), shc1, scc1)
        y, yc = _token_mixers(h, hc, w_in[l], q_norm[l], k_norm[l], rpb[l], w_branch[l], w_out[l],
                              rows, cols, rows_n, with_ctx)
        x = _layernorm(DEEPNORM_ALPHA * x + g1 * y, ln1_g[l], ln1_b[l])

        f = _swiglu(_modulate(_layernorm(x), sh2, sc2), w_gu[l], w_down[l])
        x = _layernorm(DEEPNORM_ALPHA * x + g2 * f, ln2_g[l], ln2_b[l])

        if with_ctx:
            xc = _layernorm(DEEPNORM_ALPHA * xc + gc1 * yc, ln1_g[l], ln1_b[l])
            fc = _swiglu(_modulate(_layernorm(xc), shc2, scc2), w_gu[l], w_down[l])
            xc = _layernorm(DEEPNORM_ALPHA * xc + gc2 * fc, ln2_g[l], ln2_b[l])
    return x


_drawn_inputs = setup_inputs


def setup_inputs(seed=0):
    import zlib

    import numpy as np

    out = dict(_drawn_inputs(seed))
    spreads = {}
    factors = {'ctx': 7.433,
     'c_ctx': 3.058,
     'b_ada': 5.739,
     'q_norm': 27.648,
     'k_norm': 26.454,
     'rpb': 24.152}
    for name, (base, spread) in spreads.items():
        noise = np.random.default_rng([zlib.crc32(name.encode()), seed]).standard_normal(out[name].shape)
        drawn = base * np.exp(spread * noise) if base else spread * noise
        out[name] = __import__('jax').numpy.asarray(drawn.astype(out[name].dtype))
    for name, factor in factors.items():
        out[name] = (out[name] * factor).astype(out[name].dtype)
    return out
```

```python
import concourse.bass as bass
from concourse import mybir
import numpy as np

F32 = mybir.dt.float32
F32R = mybir.dt.float32r
ALU = mybir.AluOpType
ACT = mybir.ActivationFunctionType
AX = mybir.AxisListType

DEPTH = 2
D = 1024
LAT, CTX = 512, 256
P = 128
KD = D // P
LT, CT = LAT // P, CTX // P
ALLT = LT + CT
TOK = LAT + CTX
HD = 64
HEADS = 8
KV_A = 2
GRID_W, ROWS, WIN = 64, 8, 16
BRANCH = 512
KB = BRANCH // P
D_FF = 2816
FF = D_FF // P
UNIT = 8
PARTS = ((0, 8), (8, 8), (16, 6))
ALPHA = (2.0 * DEPTH) ** 0.25
EPS = 1e-6
QSCALE = HD ** -0.5
MASKED = -1e30
BIAS_AT = (0, 256, 256, 640)
BIAS_KEYS = (256, 384, 384, 256)
FIRST_BLOCK = (0, 0, 1, 2)
BIAS_W = 896
ADA_UNITS = 6 * D // P
ADA_SLOTS = 4
ROUNDS = {ALLT: 4, LT: 3}
PRIME = 8


class Phase:

    def __init__(self, kind, layer, tiles, unit, part=None):
        self.kind, self.layer, self.tiles, self.unit, self.part = kind, layer, tiles, unit, part
        self.width = tiles * P
        self.at = {}


def plan():
    phases, unit = [], 0

    def add(kind, layer, tiles, units=0, part=None):
        nonlocal unit
        phases.append(Phase(kind, layer, tiles, unit, part))
        unit += units

    add("first_norm", 0, ALLT)
    for layer in range(DEPTH):
        t = ALLT if layer < DEPTH - 1 else LT
        add("modulate", layer, ALLT, part=0)
        add("fourier_in", layer, t, 4)
        add("tokens_a", layer, t, 6)
        add("fourier", layer, t)
        add("merge", layer, t, 12, part=2)
        add("attention", layer, t, part=0)
        add("merge", layer, t, 12, part=0)
        add("tokens_b", layer, t, 12)
        add("attention", layer, t, part=1)
        add("merge", layer, t, 12, part=1)
        add("project", layer, t, 8)
        add("residual", layer, t, part=0)
        add("modulate", layer, t, part=1)
        for part, (_, chunks) in enumerate(PARTS):
            add("gate_up", layer, t, 2 * chunks, part=part)
            add("down", layer, t, 8, part=part)
        add("residual", layer, t, part=1)
    counts = {}
    for ph in phases:
        ph.at = dict(counts)
        for name, n in increments(ph).items():
            counts[name] = counts.get(name, 0) + n
    return phases, unit


def increments(ph):
    t, k = ph.tiles, ph.kind
    if k == "first_norm":
        return {"norm_step": t * 3 + 8, "var_ready": 1, "std_ready": 1, "normed": t, "loaded": 16 * t}
    if k == "modulate":
        return {"turned": KD, "h_hi": KD, "h_val": KD, "h_lo": KD}
    if k == "fourier_in":
        return {"evacuated": 4}
    if k == "tokens_a":
        return {"evacuated": t + ALLT, "rope_step": 8 + 5 * ALLT, "var_ready": 1, "std_ready": 1}
    if k == "tokens_b":
        return {"evacuated": t + 2 * ALLT}
    if k == "fourier":
        return {"z_made": 2 * t, "evacuated": 2 * t, "mixed": KB, "o_hi": KB, "o_lo": KB}
    if k == "merge":
        return {"gated": KD, "branch_read": KD * (ph.part != 2), "merged": KD, "y_split": 2 * KD * (ph.part == 1)}
    if k == "attention":
        n, r = HEADS * t, HEADS * ROUNDS[t]
        return {"staged": 2 * HEADS, "piece": r, "piece_hi": r, "piece_lo": r, "scored": n, "max_part": n,
                "max_ready": n, "probs": n, "turned_p": n, "pt_act": n, "pt_dve": HEADS * wide_tiles(ph.part, t), "attended": n,
                "inverse": n, "o_norm": n, "o_turned": t, "o_hi": t, "o_lo": t}
    if k == "project":
        return {"projected": KD, "loaded": 16 * (t + 2)}
    if k == "residual":
        last = ph.layer == DEPTH - 1 and ph.part == 1
        return {"turned": t, "added": t, "norm_step": (t * 3 + 8) * (1 if last else 2), "var_ready": 1 if last else 2,
                "std_ready": 1 if last else 2, "normed": t if last else 2 * t, "scaled": t, "shifted": t,
                "stored": 16 * t}
    if k == "gate_up":
        n = PARTS[ph.part][1]
        return {"silu": n, "hidden": n, "hidden_hi": n, "hidden_lo": n}
    if k == "down":
        return {"summed": KD, "loaded": 16 * (t + 2) * (ph.part == len(PARTS) - 1)}
    raise ValueError(k)


def build(nc, x_in, ctx_in, cond, w_ada, b_ada, stream, qk_gain, norm_rows, bias, ident_in, rope_in, dft_ch, dft_lat,
          dft_ctx, scratch, out):
    phases, n_units = plan()

    base = (nc.sbuf_base + 63) // 64 * 64
    end = nc.sbuf_top
    cursor = [base]

    def sb(name, shape, dtype=F32, at=None):
        size = 4 * int(np.prod(shape[1:]))
        if at is None:
            at = cursor[0]
            cursor[0] += (size + 63) // 64 * 64
        assert at + size <= end, (name, at + size - end)
        return nc.alloc_sbuf_tensor_at(name, shape, dtype, offset=at)

    K = 1024
    raw = sb("raw", [P, 2, UNIT * P])
    w_hi = sb("w_hi", [P, 2, UNIT * P], F32R)
    w_lo = sb("w_lo", [P, 2, UNIT * P], F32R)
    h_hi = sb("h_hi", [P, KD, TOK], F32R)
    h_lo = sb("h_lo", [P, KD, TOK], F32R)
    acc = sb("acc", [P, KD, TOK])
    ident = sb("ident", [P, P])
    rope = sb("rope", [P, 2, ALLT, HD])
    rope_g = sb("rope_g", [P, 4, ALLT, HD])
    gain = sb("gain", [P, DEPTH, 4, HD])
    mods = sb("mods", [P, DEPTH * ADA_UNITS, 2])
    mods_v = mods[:, :, :].rearrange("p (l s k) c -> p l s k c", l=DEPTH, s=6)
    ada_bias = sb("ada_bias", [P, DEPTH * ADA_UNITS])
    cond_sb = sb("cond_sb", [P, KD, 2])
    cond_act = sb("cond_act", [P, KD, 2])
    stats = sb("stats", [P, ALLT, 2, 6])
    mean_var = sb("mean_var", [P, ALLT, 2])
    NH_A = HEADS + KV_A
    var_s = sb("var_s", [P, ALLT * NH_A])
    std_s = sb("std_s", [P, ALLT * NH_A])
    inv_s = sb("inv_s", [P, ALLT * NH_A])
    tmp_s = sb("tmp_s", [P, ALLT * NH_A])
    shift_s = sb("shift_s", [P, ALLT])
    max_c = sb("max_c", [P, 2])
    max_a = sb("max_a", [P, 2])
    neg_max = sb("neg_max", [P, 2])
    row_sum = sb("row_sum", [P, 4])
    row_inv = sb("row_inv", [P, 2])
    dft_c = sb("dft_c", [P, 2 * P])
    eps_c = sb("eps_c", [P, 1])
    R = cursor[0]

    o_hi = sb("o_hi", [P, KB, TOK], F32R, at=R)
    o_lo = sb("o_lo", [P, KB, TOK], F32R, at=R + 12 * K)
    u_cols = sb("u_cols", [P, KB, TOK], at=R)
    q_st = [sb(f"q_st{s}", [P, TOK], F32R, at=R + 3 * K * s) for s in range(2)]
    k_hh = [sb(f"k_hh{s}", [P, TOK], F32R, at=R + 6 * K + 3 * K * s) for s in range(2)]
    k_ll = [sb(f"k_ll{s}", [P, TOK], F32R, at=R + 12 * K + 3 * K * s) for s in range(2)]
    stage_q = [sb(f"stage_q{s}", [P, ALLT, 2, HD], at=R + 18 * K + 3 * K * s) for s in range(2)]
    stage_k = [sb(f"stage_k{s}", [P, ALLT, 2, HD], at=R + 81 * K + 3 * K * s) for s in range(2)]
    tok_a = sb("tok_a", [P, ALLT, NH_A * HD], at=R + 24 * K)
    v_a = sb("v_a", [P, ALLT, KV_A * HD], at=R + 39 * K)
    z_sb = sb("z_sb", [P, ALLT, KB, 2 * P], at=R + 42 * K)
    dft_l = sb("dft_l", [P, LT, 2, LAT], at=R + 66 * K)
    dft_x = sb("dft_x", [P, CT, 2, CTX], at=R + 82 * K)
    rope_t = [sb(f"rope_t{s}", [P, NH_A * HD], at=R + 86 * K + 2560 * s) for s in range(2)]
    tok_b = sb("tok_b", [P, ALLT, 2, BRANCH], at=R + 24 * K)
    v_b = sb("v_b", [P, ALLT, BRANCH], at=R + 48 * K)
    o_tok = sb("o_tok", [P, ALLT, BRANCH], at=R + 60 * K)
    p_sb = [sb(f"p_sb{s}", [P, TOK], at=R + 72 * K + 3 * K * s) for s in range(2)]
    pt_sb = sb("pt_sb", [P, TOK], at=R + 78 * K)
    bias_sb = [sb(f"bias_sb{s}", [P, BIAS_W], at=R + 87 * K + 3584 * s) for s in range(2)]
    gate = sb("gate", [P, 4, TOK], at=R + 72 * K)
    y_hi = sb("y_hi", [P, KD, TOK], F32R, at=R + 24 * K)
    y_lo = sb("y_lo", [P, KD, TOK], F32R, at=R + 48 * K)
    ln_rows = sb("ln_rows", [P, 2, D], at=R)
    xn = sb("xn", [P, ALLT, D], at=R + 24 * K)
    h_tmp = sb("h_tmp", [P, 2, TOK], at=R + 48 * K)
    xr = sb("xr", [P, ALLT, D], at=R + 72 * K)
    hid_hi = sb("hid_hi", [P, 8, TOK], F32R, at=R + 8 * K)
    hid_lo = sb("hid_lo", [P, 8, TOK], F32R, at=R + 32 * K)
    silu_g = sb("silu_g", [P, 2, TOK], at=R + 56 * K)
    hid = sb("hid", [P, 2, TOK], at=R + 62 * K)
    ada_raw = sb("ada_raw", [P, ADA_SLOTS, UNIT * P], at=R)

    ps = nc.alloc_psum_tensor("ps", [P, 8, 512], F32)

    def span(bank, width, start=0):
        n = (start + width + 511) // 512
        return ps[:, bank:bank + n, :].rearrange("p a b -> p (a b)")[:, start:start + width]

    sems = {}

    def S(name):
        if name not in sems:
            sems[name] = nc.alloc_semaphore(name)
        return sems[name]

    raw_ready = [nc.alloc_semaphore(f"raw_ready{s}") for s in range(2)]
    ada_ready = [nc.alloc_semaphore(f"ada_ready{s}") for s in range(ADA_SLOTS)]
    bias_ready = [nc.alloc_semaphore(f"bias_ready{s}") for s in range(2)]

    PRIMED = ("gated", "branch_read", "merged", "projected", "silu", "hidden", "summed", "probs", "piece", "piece_lo",
              "o_norm", "attended", "scored", "turned_p", "added", "evacuated", "pt_act", "pt_dve", "inverse")

    def at(ph, name):
        return ph.at.get(name, 0) + (PRIME if name in PRIMED else 0)

    def prime(eng, names):
        for name in names:
            eng.sem_inc(S(name), PRIME)

    TERMS = ("lo_hi", "hi_lo", "hi_hi")

    def term(name, slot, x_hi, x_lo):
        return {"lo_hi": (w_lo, x_hi), "hi_lo": (w_hi, x_lo), "hi_hi": (w_hi, x_hi)}[name]

    block = nc.Block()
    with block:

        @block.sync
        def _(sp):
            sp.dma_start(cond_sb[:, :, :], cond[:, :, :]).then_inc(S("cond_loaded"), 16)
            for s in range(2):
                sp.dma_start(raw[:, s, :], stream[s, :, :]).then_inc(raw_ready[s], 16)
            for s in range(ADA_SLOTS):
                sp.dma_start(ada_raw[:, s, :], w_ada[s, :, :]).then_inc(ada_ready[s], 16)
            with sp.Fori(0, DEPTH * ADA_UNITS // ADA_SLOTS - 1) as i:
                for s in range(ADA_SLOTS):
                    sp.wait_ge(S("ada_used"), ADA_SLOTS * i + s + 1)
                    sp.dma_start(ada_raw[:, s, :], w_ada[bass.ds(ADA_SLOTS * (i + 1) + s, 1), :, :]
                                 .rearrange("a p c -> p (a c)")).then_inc(ada_ready[s], 16)
            with sp.Fori(1, n_units // 2) as i:
                for s in range(2):
                    sp.wait_ge(S("lo_made"), 2 * i + s - 1)
                    sp.dma_start(raw[:, s, :], stream[bass.ds(2 * i + s, 1), :, :]
                                 .rearrange("a p c -> p (a c)")).then_inc(raw_ready[s], 16)

        @block.gpsimd
        def _(pool):
            def lo_parts(first, end):
                with pool.Fori(first // 2, end // 2) as i:
                    for s in range(2):
                        pool.wait_ge(S("hi_made"), 2 * i + s + 1)
                        nc.gpsimd.tensor_tensor(w_lo[:, s, :], raw[:, s, :], w_hi[:, s, :].bitcast(F32),
                                                ALU.subtract).then_inc(S("lo_made"), 1)

            done = 0
            for ph in phases:
                if ph.kind != "attention":
                    continue
                lo_parts(done, ph.unit + 2)
                done = ph.unit + 2
                if ph.part == 0:
                    pool.wait_ge(S("rope_step"), at(ph, "rope_step"))
                else:
                    pool.wait_ge(S("evacuated"), at(ph, "evacuated"))
                pool.wait_ge(S("merged"), at(ph, "merged"))
                pool.wait_ge(S("unit_done"), ph.unit)
                rounds = ROUNDS[ph.tiles]
                with pool.Fori(0, HEADS // 2) as i:
                    for s in range(2):
                        h = 2 * i + s
                        pool.wait_ge(S("piece"), at(ph, "piece") + rounds * (2 * i + s - 1))
                        if ph.part == 0:
                            q_src = tok_a[:, 0:ph.tiles, bass.ds(h * HD, HD)]
                            k_src = tok_a[:, :, bass.ds(HEADS * HD + (i // 2) * HD, HD)]
                        else:
                            q_src = tok_b[:, 0:ph.tiles, 0, bass.ds(h * HD, HD)]
                            k_src = tok_b[:, :, 1, bass.ds(h * HD, HD)]
                        nc.gpsimd.tensor_copy(stage_q[s][:, 0:ph.tiles, :, :],
                                              q_src.unsqueeze(2).broadcast_to([P, ph.tiles, 2, HD])
                                              ).then_inc(S("staged"), 1)
                        nc.gpsimd.tensor_copy(stage_k[s][:, :, :, :],
                                              k_src.unsqueeze(2).broadcast_to([P, ALLT, 2, HD])
                                              ).then_inc(S("staged"), 1)
            lo_parts(done, n_units)

        @block.scalar
        def _(act):
            prime(act, ("gated", "projected", "silu", "probs", "evacuated", "pt_act"))
            consts = [(ident[:, :], ident_in[:, :]), (rope[:, :, :, :], rope_in[:, :, :, :]),
                      (ada_bias[:, :], b_ada[:, :]), (dft_c[:, :], dft_ch[:, :])]
            for dst, src in consts:
                act.dma_start(dst, src).then_inc(S("consts"), 16)
            act.dma_start(gain[:, :, :, :].rearrange("p a b c -> p (a b c)"),
                          qk_gain.partition_broadcast(P)).then_inc(S("consts"), 16)
            act.wait_ge(S("cond_loaded"), 16)
            nc.scalar.activation(cond_act[:, :, :], cond_sb[:, :, :], ACT.Silu).then_inc(S("cond_ready"), 1)

            def split(u, s):
                act.wait_ge(raw_ready[s], 8 * (u - s) + 16)
                nc.scalar.activation(w_hi[:, s, :], raw[:, s, :], ACT.Copy).then_inc(S("hi_made"), 1)

            def unit_done(u, s, ahead=True):
                act.wait_ge(S("unit_done"), u + 1)
                if ahead:
                    split(u + 2, s)

            def root(ph, k, n):
                act.wait_ge(S("var_ready"), at(ph, "var_ready") + k + 1)
                nc.scalar.activation(std_s[:, 0:n], var_s[:, 0:n], ACT.Sqrt).then_inc(S("std_ready"), 1)

            def normalise(ph, k, dst, src):
                root(ph, k, ph.tiles)
                act.wait_ge(S("norm_step"), at(ph, "norm_step") + (k + 1) * (3 * ph.tiles + 8))
                for t in range(ph.tiles):
                    nc.scalar.activation(dst[:, t, :], src[:, t, :], ACT.Identity, scale=inv_s[:, t:t + 1],
                                         bias=shift_s[:, t:t + 1]).then_inc(S("normed"), 1)

            def rows_of_input(t):
                return x_in[t * P:(t + 1) * P, :] if t < LT else ctx_in[(t - LT) * P:(t - LT + 1) * P, :]

            def load_residual(ph):
                which = 0 if ph.kind == "project" else 1
                for t in range(ph.tiles):
                    src = rows_of_input(t) if ph.layer + which == 0 else scratch[ph.layer * 2 + which, t, :, :]
                    act.dma_start(xr[:, t, :], src).then_inc(S("loaded"), 16)
                for r in range(2):
                    act.dma_start(ln_rows[:, r, :], norm_rows[ph.layer, which, r, :].partition_broadcast(P)
                                  ).then_inc(S("loaded"), 16)

            for s in range(2):
                split(s, s)

            def first_norm(ph):
                for t in range(ALLT):
                    act.dma_start(xr[:, t, :], rows_of_input(t)).then_inc(S("loaded"), 16)
                normalise(ph, 0, xn, xr)

            def modulate(ph):
                act.wait_ge(S("mods_ready"), 3)
                act.wait_ge(S("unit_done"), ph.unit) if ph.unit else None
                m = 3 * ph.part
                for k in range(KD):
                    slot = 2 * (k % 4)
                    act.wait_ge(S("turned"), at(ph, "turned") + k + 1)
                    for c, (a, b) in enumerate(((0, LAT), (LAT, TOK))[:1 + (ph.tiles > LT)]):
                        last = nc.scalar.activation(h_hi[:, k, a:b], span(slot, b - a, a), ACT.Identity,
                                                    scale=mods_v[:, ph.layer, m + 1, k, c:c + 1],
                                                    bias=mods_v[:, ph.layer, m, k, c:c + 1])
                    last.then_inc(S("h_hi"), 1)
                if ph.part == 0:
                    act.dma_start(dft_l[:, :, :, :], dft_lat[:, :, :, :]).then_inc(S("dft_loaded"), 16)
                    act.dma_start(dft_x[:, :, :, :], dft_ctx[:, :, :, :]).then_inc(S("dft_loaded"), 16)

            def fourier_in(ph):
                with act.Fori(0, KB // 2) as i:
                    for s in range(2):
                        unit_done(ph.unit + 2 * i + s, s)
                        src = ps[:, bass.ds(4 * i + 2 * s, 2), :].rearrange("p a b -> p (a b)")[:, 0:ph.width]
                        nc.scalar.activation(u_cols[:, bass.ds(2 * i + s, 1), 0:ph.width].rearrange("p a b -> p (a b)"),
                                             src, ACT.Copy).then_inc(S("evacuated"), 1)

            def groups(ph):
                if ph.kind == "tokens_a":
                    return ((4, ph.tiles, 512, lambda t: ((tok_a[:, t, 0:512], 0, 512),), 1.0),
                            (2, ALLT, 256, lambda t: ((tok_a[:, t, 512:640], 0, 128), (v_a[:, t, :], 128, 256)), 1.0))
                return ((4, ph.tiles, 512, lambda t: ((tok_b[:, t, 0, :], 0, 512),), QSCALE),
                        (4, ALLT, 512, lambda t: ((tok_b[:, t, 1, :], 0, 512),), 1.0),
                        (4, ALLT, 512, lambda t: ((v_b[:, t, :], 0, 512),), 1.0))

            def tokens(ph):
                u, bank = ph.unit, 0
                for units, tiles, cols, dests, scale in groups(ph):
                    for j in range(units):
                        unit_done(u + j, j % 2)
                    u += units
                    for t in range(tiles):
                        for dst, a, b in dests(t):
                            last = nc.scalar.activation(dst, ps[:, bank % 8, a:b], ACT.Copy, scale=scale)
                        last.then_inc(S("evacuated"), 1)
                        bank += 1
                if ph.kind == "tokens_a":
                    root(ph, 0, ALLT * NH_A)

            def fourier(ph):
                for n in range(2 * ph.tiles):
                    t, g = n // 2, n % 2
                    act.wait_ge(S("z_made"), at(ph, "z_made") + n + 1)
                    nc.scalar.activation(z_sb[:, t, 2 * g:2 * g + 2, :].rearrange("p a b -> p (a b)"),
                                         ps[:, n % 8, :], ACT.Copy).then_inc(S("evacuated"), 1)
                for g in range(KB):
                    act.wait_ge(S("mixed"), at(ph, "mixed") + g + 1)
                    nc.scalar.activation(o_hi[:, g, 0:ph.width], span(2 * g, ph.width), ACT.Copy).then_inc(S("o_hi"), 1)

            def merge(ph):
                with act.Fori(0, 2) as i:
                    for half in range(2):
                        for j in range(3):
                            n = 3 * half + j
                            unit_done(ph.unit + 6 * i + n, n % 2)
                            if j < 2:
                                c = 2 * half + j
                                act.wait_ge(S("merged"), at(ph, "merged") + 4 * i + c - 3)
                                nc.scalar.activation(gate[:, c, 0:ph.width], span(2 * j, ph.width), ACT.Sigmoid
                                                     ).then_inc(S("gated"), 1)

            def attention(ph):
                t_n, rounds, branch = ph.tiles, ROUNDS[ph.tiles], ph.part

                def load_bias(h, s):
                    if branch == 1:
                        act.dma_start(bias_sb[s][:, :], bias[ph.layer, bass.ds(h, 1), :, :]
                                      .rearrange("a p c -> p (a c)")).then_inc(bias_ready[s], 16)

                def piece(h, s, r):
                    what, a, b = PIECES[r]
                    act.wait_ge(S("piece"), at(ph, "piece") + rounds * h + r + 1)
                    dst = q_st[s] if what == "q" else k_hh[s]
                    nc.scalar.activation(dst[:, a:b], ps[:, 7, 0:b - a], ACT.Copy).then_inc(S("piece_hi"), 1)

                def probs(n, s, t):
                    keys = P * len(key_tiles(branch, t))
                    act.wait_ge(S("max_ready"), at(ph, "max_ready") + n + 1)
                    act.wait_ge(S("inverse"), at(ph, "inverse") + n - 1)
                    act.wait_ge(S("turned_p"), at(ph, "turned_p") + n - 1)
                    nc.scalar.activation(p_sb[s][:, 0:keys], span(2 * s, keys), ACT.Exp, bias=neg_max[:, s:s + 1],
                                         accum_out=row_sum[:, s:s + 1]).then_inc(S("probs"), 1)

                def copy_turned(n, t):
                    keys = min(512, P * len(key_tiles(branch, t)))
                    act.wait_ge(S("turned_p"), at(ph, "turned_p") + n + 1)
                    nc.scalar.activation(pt_sb[:, 0:keys], span(4, keys), ACT.Copy).then_inc(S("pt_act"), 1)

                act.wait_ge(S("merged"), at(ph, "merged"))
                for s in range(2):
                    load_bias(s, s)
                for r in range(rounds):
                    piece(0, 0, r)
                probs(0, 0, 0)
                probs(1, 1, 1)

                def pair(i, last):
                    for m in range(2 * t_n):
                        n = 2 * t_n * i + m
                        for s, h, r in pieces_at(t_n, m, last):
                            piece(2 * i + h, s, r)
                        copy_turned(n, m % t_n)
                        if m + 2 < 2 * t_n or not last:
                            probs(n + 2, m % 2, (m + 2) % t_n)
                        if m == t_n and not last:
                            load_bias(2 * i + 2, 0)
                    if not last:
                        load_bias(2 * i + 3, 1)

                with act.Fori(0, HEADS // 2 - 1) as i:
                    pair(i, False)
                pair(HEADS // 2 - 1, True)
                for t in range(t_n):
                    act.wait_ge(S("o_turned"), at(ph, "o_turned") + t + 1)
                    nc.scalar.activation(o_hi[:, :, t * P:(t + 1) * P],
                                         ps[:, t % 4, :].rearrange("p (a b) -> p a b", a=KB), ACT.Copy
                                         ).then_inc(S("o_hi"), 1)

            def project(ph):
                act.wait_ge(S("merged"), at(ph, "merged"))
                load_residual(ph)
                with act.Fori(0, KD // 2) as i:
                    for s in range(2):
                        unit_done(ph.unit + 2 * i + s, s)
                        for c, (a, b) in enumerate(((0, LAT), (LAT, TOK))[:1 + (ph.tiles > LT)]):
                            last = nc.scalar.activation(
                                acc[:, bass.ds(2 * i + s, 1), a:b].rearrange("p a b -> p (a b)"), span(2 * s, b - a, a),
                                ACT.Copy, scale=mods_v[:, ph.layer, 2, bass.ds(2 * i + s, 1), c])
                        last.then_inc(S("projected"), 1)

            def residual(ph):
                last = ph.layer == DEPTH - 1 and ph.part == 1
                normalise(ph, 0, xr, xr)
                for t in range(ph.tiles):
                    act.wait_ge(S("shifted"), at(ph, "shifted") + t + 1)
                    dst = out[t, :, :] if last else scratch[2 * ph.layer + ph.part + 1, t, :, :]
                    act.dma_start(dst, xr[:, t, :]).then_inc(S("stored"), 16)
                if not last:
                    normalise(ph, 1, xn, xr)
                act.wait_ge(S("stored"), at(ph, "stored") + 16 * ph.tiles)

            def gate_up(ph):
                with act.Fori(0, PARTS[ph.part][1] // 2) as i:
                    for c in range(2):
                        unit_done(ph.unit + 4 * i + 2 * c, 0)
                        act.wait_ge(S("hidden"), at(ph, "hidden") + 2 * i + c - 1)
                        nc.scalar.activation(silu_g[:, c, 0:ph.width], span(4 * c, ph.width), ACT.Silu
                                             ).then_inc(S("silu"), 1)
                        unit_done(ph.unit + 4 * i + 2 * c + 1, 1)

            def down(ph):
                if ph.part == len(PARTS) - 1:
                    load_residual(ph)
                end = ph.unit + KD == n_units
                with act.Fori(0, KD // 2 - end) as i:
                    for s in range(2):
                        unit_done(ph.unit + 2 * i + s, s)

            for ph in phases:
                {"first_norm": first_norm, "modulate": modulate, "fourier_in": fourier_in, "tokens_a": tokens,
                 "tokens_b": tokens, "fourier": fourier, "merge": merge, "attention": attention, "project": project,
                 "residual": residual, "gate_up": gate_up, "down": down}[ph.kind](ph)

        @block.vector
        def _(dve):
            prime(dve, ("branch_read", "merged", "hidden", "summed", "piece_lo", "o_norm", "added", "pt_dve", "inverse"))
            nc.vector.memset(eps_c[:, :], EPS)
            dve.wait_ge(S("consts"), 16 * 5)
            dve.wait_ge(S("ada_used"), DEPTH * ADA_UNITS)
            nc.vector.tensor_tensor(mods[:, :, :], ps[:, 7, 0:2 * DEPTH * ADA_UNITS].rearrange("p (a c) -> p a c", c=2),
                                    ada_bias[:, :].unsqueeze(2).broadcast_to([P, DEPTH * ADA_UNITS, 2]), ALU.add
                                    ).then_inc(S("mods_ready"), 1)
            dve.wait_ge(S("mods_ready"), 1)
            for s, n in ((1, 2), (4, 3)):
                nc.vector.tensor_scalar(mods_v[:, :, s, :, :], mods_v[:, :, s, :, :], 1.0, None, ALU.add
                                        ).then_inc(S("mods_ready"), 1)

            def chain(name, start):
                count = [start]

                def step(instruction):
                    count[0] += 1
                    instruction.then_inc(S(name), 1)
                    dve.wait_ge(S(name), count[0])
                return step

            def inverse_root(step, n, ph, k):
                dve.wait_ge(S("std_ready"), at(ph, "std_ready") + k + 1)
                step(nc.vector.reciprocal(inv_s[:, 0:n], std_s[:, 0:n]))
                step(nc.vector.tensor_tensor(tmp_s[:, 0:n], inv_s[:, 0:n], inv_s[:, 0:n], ALU.mult))
                step(nc.vector.tensor_tensor(tmp_s[:, 0:n], tmp_s[:, 0:n], var_s[:, 0:n], ALU.mult))
                step(nc.vector.tensor_scalar(tmp_s[:, 0:n], tmp_s[:, 0:n], -0.5, 1.5, ALU.mult, ALU.add))
                step(nc.vector.tensor_tensor(inv_s[:, 0:n], inv_s[:, 0:n], tmp_s[:, 0:n], ALU.mult))

            def statistics(ph, k, before):
                n = ph.tiles
                step = chain("norm_step", at(ph, "norm_step") + k * (3 * n + 8))
                for t in range(n):
                    before(t)
                    for half in range(2):
                        step(nc.vector.bn_stats(stats[:, t, half, :], xr[:, t, half * 512:(half + 1) * 512]))
                    step(nc.vector.bn_aggr(mean_var[:, t, :], stats[:, t, :, :].rearrange("p a b -> p (a b)")))
                nc.vector.tensor_scalar(var_s[:, 0:n], mean_var[:, 0:n, 1], EPS, None, ALU.add
                                        ).then_inc(S("var_ready"), 1)
                inverse_root(step, n, ph, k)
                step(nc.vector.tensor_scalar(tmp_s[:, 0:n], mean_var[:, 0:n, 0], -1.0, None, ALU.mult))
                step(nc.vector.tensor_tensor(shift_s[:, 0:n], tmp_s[:, 0:n], inv_s[:, 0:n], ALU.mult))
                step(nc.vector.tensor_copy(tmp_s[:, 0:n], inv_s[:, 0:n]))

            def first_norm(ph):
                dve.wait_ge(S("loaded"), 16 * ALLT)
                statistics(ph, 0, lambda t: None)

            def modulate(ph):
                m = 3 * ph.part
                for k in range(KD):
                    slot = 2 * (k % 4)
                    dve.wait_ge(S("h_hi"), at(ph, "h_hi") + k + 1)
                    for c, (a, b) in enumerate(((0, LAT), (LAT, TOK))[:1 + (ph.tiles > LT)]):
                        last = nc.vector.tensor_scalar(h_tmp[:, k % 2, a:b], span(slot, b - a, a),
                                                       mods_v[:, ph.layer, m + 1, k, c:c + 1],
                                                       mods_v[:, ph.layer, m, k, c:c + 1], ALU.mult, ALU.add)
                    last.then_inc(S("h_val"), 1)
                    dve.wait_ge(S("h_val"), at(ph, "h_val") + k + 1)
                    nc.vector.tensor_tensor(h_lo[:, k, 0:ph.width], h_tmp[:, k % 2, 0:ph.width],
                                            h_hi[:, k, 0:ph.width].bitcast(F32), ALU.subtract).then_inc(S("h_lo"), 1)

            def tokens_a(ph):
                step = chain("rope_step", at(ph, "rope_step"))
                heads_of = [NH_A if t < ph.tiles else KV_A for t in range(ALLT)]
                sums = var_s[:, :].rearrange("p (t h) -> p t h", t=ALLT)
                invs = inv_s[:, :].rearrange("p (t h) -> p t h", t=ALLT)
                step(nc.vector.memset(var_s[:, :], 1.0))
                for n, (g, scale) in enumerate(((0, QSCALE), (1, QSCALE), (2, 1.0), (3, 1.0))):
                    last = nc.vector.scalar_tensor_tensor(
                        rope_g[:, n, :, :], rope[:, n % 2, :, :], scale,
                        gain[:, ph.layer, g, :].unsqueeze(1).broadcast_to([P, ALLT, HD]), ALU.mult, ALU.mult)
                step(last)
                dve.wait_ge(S("evacuated"), at(ph, "evacuated") + ph.tiles + ALLT)

                def view(a, t):
                    n = heads_of[t]
                    return a[:, (NH_A - n) * HD:].rearrange("p (h d) -> p h d", d=HD)

                for t in range(ALLT):
                    n = heads_of[t]
                    x = view(tok_a[:, t, :], t)
                    sq = view(rope_t[t % 2][:, :], t)
                    step(nc.vector.tensor_tensor(sq, x, x, ALU.mult))
                    step(nc.vector.tensor_reduce(sums[:, t, NH_A - n:], sq, axis=AX.X, op=ALU.add))
                step(nc.vector.tensor_scalar(var_s[:, :], var_s[:, :], 1.0 / HD, EPS, ALU.mult, ALU.add))
                nc.vector.tensor_copy(tmp_s[:, :], var_s[:, :]).then_inc(S("var_ready"), 1)
                inverse_root(step, ALLT * NH_A, ph, 0)
                for t in range(ALLT):
                    n = heads_of[t]
                    x = view(tok_a[:, t, :], t)
                    kept, turned = view(rope_t[0][:, :], t), view(rope_t[1][:, :], t)
                    step(nc.vector.tensor_tensor(x, x, invs[:, t, NH_A - n:].unsqueeze(2).broadcast_to([P, n, HD]),
                                                 ALU.mult))
                    parts = ((0, n - KV_A, 0), (n - KV_A, n, 2)) if n > KV_A else ((0, n, 2),)
                    for a, b, g in parts:
                        nc.vector.tensor_tensor(kept[:, a:b, :], x[:, a:b, :],
                                                rope_g[:, g, t, :].unsqueeze(1).broadcast_to([P, b - a, HD]), ALU.mult)
                    for a, b, g in parts:
                        for quarter in range(2):
                            def of(v, q):
                                return v.rearrange("p h (a q d) -> p h a q d", a=2, q=2)[:, :, :, q, :]
                            sin = rope_g[:, g + 1, t, :].rearrange("p (a q d) -> p a q d", a=2, q=2)[:, :, quarter, :]
                            last = nc.vector.tensor_tensor(of(turned[:, a:b, :], quarter), of(x[:, a:b, :], 1 - quarter),
                                                           sin.unsqueeze(1).broadcast_to([P, b - a, 2, HD // 4]), ALU.mult)
                    step(last)
                    step(nc.vector.tensor_tensor(x, kept, turned, ALU.add))

            def fourier(ph):
                for g in range(KB):
                    dve.wait_ge(S("o_hi"), at(ph, "o_hi") + g + 1)
                    nc.vector.tensor_tensor(o_lo[:, g, 0:ph.width], span(2 * g, ph.width),
                                            o_hi[:, g, 0:ph.width].bitcast(F32), ALU.subtract).then_inc(S("o_lo"), 1)

            def merge(ph):
                w = ph.width
                with dve.Fori(0, 2) as i:
                    for half in range(2):
                        for j in range(2):
                            c = 2 * half + j
                            chunk = acc[:, bass.ds(4 * i + c, 1), 0:w].rearrange("p a b -> p (a b)")
                            dve.wait_ge(S("unit_done"), ph.unit + 6 * i + 3 * half + 3)
                            dve.wait_ge(S("gated"), at(ph, "gated") + 4 * i + c + 1)
                            if ph.part == 2:
                                nc.vector.tensor_tensor(chunk, gate[:, c, 0:w], span(4 + 2 * j, w), ALU.mult
                                                        ).then_inc(S("merged"), 1)
                            else:
                                nc.vector.tensor_tensor(gate[:, c, 0:w], gate[:, c, 0:w], span(4 + 2 * j, w), ALU.mult
                                                        ).then_inc(S("branch_read"), 1)
                                dve.wait_ge(S("branch_read"), at(ph, "branch_read") + 4 * i + c + 1)
                                nc.vector.tensor_tensor(chunk, chunk, gate[:, c, 0:w], ALU.add
                                                        ).then_inc(S("merged"), 1)
                            if ph.part == 1:
                                y = at(ph, "y_split") + 8 * i + 2 * c
                                hi = y_hi[:, bass.ds(4 * i + c, 1), 0:w].rearrange("p a b -> p (a b)")
                                lo = y_lo[:, bass.ds(4 * i + c, 1), 0:w].rearrange("p a b -> p (a b)")
                                dve.wait_ge(S("merged"), at(ph, "merged") + 4 * i + c + 1)
                                nc.vector.tensor_scalar(hi, chunk, 1.0, None, ALU.mult).then_inc(S("y_split"), 1)
                                dve.wait_ge(S("y_split"), y + 1)
                                nc.vector.tensor_tensor(lo, chunk, hi.bitcast(F32), ALU.subtract
                                                        ).then_inc(S("y_split"), 1)

            def attention(ph):
                t_n, rounds, branch = ph.tiles, ROUNDS[ph.tiles], ph.part

                def piece(h, s, r):
                    what, a, b = PIECES[r]
                    dve.wait_ge(S("piece_hi"), at(ph, "piece_hi") + rounds * h + r + 1)
                    if what == "q":
                        rows, dst, hi = slice(HD, P), q_st[s], q_st[s]
                    else:
                        rows, dst, hi = slice(0, P), k_ll[s], k_hh[s]
                    nc.vector.tensor_tensor(dst[rows, a:b], ps[rows, 7, 0:b - a], hi[rows, a:b].bitcast(F32),
                                            ALU.subtract).then_inc(S("piece_lo"), 1)

                def maximum(n, h, s, t):
                    keys = P * len(key_tiles(branch, t))
                    dve.wait_ge(S("scored"), at(ph, "scored") + n + 1)
                    dve.wait_ge(S("probs"), at(ph, "probs") + n - 1)
                    if branch == 1 and t < LT:
                        if t == 0:
                            dve.wait_ge(bias_ready[h[1]], 16 * (HEADS // 2) * ph.layer + 16 * h[0] + 16)
                        nc.vector.tensor_reduce(max_c[:, s:s + 1], span(2 * s, CTX), axis=AX.X, op=ALU.max
                                                ).then_inc(S("max_part"), 1)
                        lat = span(2 * s, keys - CTX, CTX)
                        nc.vector.tensor_tensor_reduce(out=lat, in0=lat,
                                                       in1=bias_sb[h[1]][:, BIAS_AT[t]:BIAS_AT[t] + BIAS_KEYS[t]],
                                                       scale=1.0, scalar=3 * MASKED, op0=ALU.add, op1=ALU.max,
                                                       accum_out=max_a[:, s:s + 1]).then_inc(S("max_bias"), 1)
                        dve.wait_ge(S("max_part"), at(ph, "max_part") + n + 1)
                        dve.wait_ge(S("max_bias"), bias_count(ph, n, h, t))
                        nc.vector.tensor_scalar(neg_max[:, s:s + 1], max_a[:, s:s + 1], max_c[:, s:s + 1], -1.0,
                                                ALU.max, ALU.mult).then_inc(S("max_ready"), 1)
                    else:
                        nc.vector.tensor_reduce(max_c[:, s:s + 1], span(2 * s, keys), axis=AX.X, op=ALU.max
                                                ).then_inc(S("max_part"), 1)
                        dve.wait_ge(S("max_part"), at(ph, "max_part") + n + 1)
                        nc.vector.tensor_scalar(neg_max[:, s:s + 1], max_c[:, s:s + 1], -1.0, None, ALU.mult
                                                ).then_inc(S("max_ready"), 1)

                def bias_count(ph, n, h, t):
                    return 4 * HEADS * ph.layer + 4 * (2 * h[0] + h[1]) + t + 1

                def copy_turned(n, t):
                    keys = P * len(key_tiles(branch, t))
                    if keys > 512:
                        dve.wait_ge(S("turned_p"), at(ph, "turned_p") + n + 1)
                        nc.vector.tensor_copy(pt_sb[:, 512:keys], ps[:, 5, 0:keys - 512]).then_inc(S("pt_dve"), 1)

                def normalise(n, h, s, t):
                    dve.wait_ge(S("probs"), at(ph, "probs") + n + 1)
                    nc.vector.reciprocal(row_inv[:, s:s + 1], row_sum[:, s:s + 1]).then_inc(S("inverse"), 1)
                    dve.wait_ge(S("inverse"), at(ph, "inverse") + n + 1)
                    dve.wait_ge(S("attended"), at(ph, "attended") + n + 1)
                    nc.vector.tensor_scalar(o_tok[:, t, bass.ds((2 * h[0] + h[1]) * HD, HD)], ps[:, 6, 0:HD],
                                            row_inv[:, s:s + 1], None, ALU.mult).then_inc(S("o_norm"), 1)

                for r in range(rounds):
                    piece(0, 0, r)
                maximum(0, (0, 0), 0, 0)
                maximum(1, (0, 0), 1, 1)

                def pair(i, last):
                    for m in range(2 * t_n):
                        n = 2 * t_n * i + m
                        for s, h, r in pieces_at(t_n, m, last):
                            piece(2 * i + h, s, r)
                        copy_turned(n, m % t_n)
                        if m + 2 < 2 * t_n:
                            maximum(n + 2, (i, (m + 2) // t_n), m % 2, (m + 2) % t_n)
                        elif not last:
                            maximum(n + 2, (i + 1, 0), m % 2, m + 2 - 2 * t_n)
                        normalise(n, (i, m // t_n), m % 2, m % t_n)

                with dve.Fori(0, HEADS // 2 - 1) as i:
                    pair(i, False)
                pair(HEADS // 2 - 1, True)
                for t in range(t_n):
                    dve.wait_ge(S("o_hi"), at(ph, "o_hi") + t + 1)
                    nc.vector.tensor_tensor(o_lo[:, :, t * P:(t + 1) * P],
                                            ps[:, t % 4, :].rearrange("p (a b) -> p a b", a=KB),
                                            o_hi[:, :, t * P:(t + 1) * P].bitcast(F32), ALU.subtract
                                            ).then_inc(S("o_lo"), 1)

            def residual(ph):
                def add(t):
                    dve.wait_ge(S("turned"), at(ph, "turned") + t + 1)
                    nc.vector.scalar_tensor_tensor(xr[:, t, :], xr[:, t, :], ALPHA, span(2 * (t % 4), D), ALU.mult,
                                                   ALU.add).then_inc(S("added"), 1)
                    dve.wait_ge(S("added"), at(ph, "added") + t + 1)

                dve.wait_ge(S("loaded"), at(ph, "loaded"))
                statistics(ph, 0, add)

                def affine(t):
                    dve.wait_ge(S("normed"), at(ph, "normed") + t + 1)
                    nc.vector.tensor_tensor(xr[:, t, :], xr[:, t, :], ln_rows[:, 0, :], ALU.mult).then_inc(S("scaled"), 1)
                    dve.wait_ge(S("scaled"), at(ph, "scaled") + t + 1)
                    nc.vector.tensor_tensor(xr[:, t, :], xr[:, t, :], ln_rows[:, 1, :], ALU.add).then_inc(S("shifted"), 1)
                    dve.wait_ge(S("shifted"), at(ph, "shifted") + t + 1)

                if ph.layer == DEPTH - 1 and ph.part == 1:
                    for t in range(ph.tiles):
                        affine(t)
                else:
                    dve.wait_ge(S("normed"), at(ph, "normed") + ph.tiles)
                    statistics(ph, 1, affine)

            def gate_up(ph):
                w = ph.width
                with dve.Fori(0, PARTS[ph.part][1] // 2) as i:
                    for c in range(2):
                        n = 2 * i + c
                        hi = hid_hi[:, bass.ds(n, 1), 0:w].rearrange("p a b -> p (a b)")
                        lo = hid_lo[:, bass.ds(n, 1), 0:w].rearrange("p a b -> p (a b)")
                        dve.wait_ge(S("unit_done"), ph.unit + 4 * i + 2 * c + 2)
                        dve.wait_ge(S("silu"), at(ph, "silu") + n + 1)
                        nc.vector.tensor_tensor(hid[:, c, 0:w], silu_g[:, c, 0:w], span(4 * c + 2, w), ALU.mult
                                                ).then_inc(S("hidden"), 1)
                        dve.wait_ge(S("hidden"), at(ph, "hidden") + n + 1)
                        nc.vector.tensor_scalar(hi, hid[:, c, 0:w], 1.0, None, ALU.mult).then_inc(S("hidden_hi"), 1)
                        dve.wait_ge(S("hidden_hi"), at(ph, "hidden_hi") + n + 1)
                        nc.vector.tensor_tensor(lo, hid[:, c, 0:w], hi.bitcast(F32), ALU.subtract
                                                ).then_inc(S("hidden_lo"), 1)

            def down(ph):
                with dve.Fori(0, KD // 2) as i:
                    for s in range(2):
                        n = 2 * i + s
                        dve.wait_ge(S("unit_done"), ph.unit + n + 1)
                        for c, (a, b) in enumerate(((0, LAT), (LAT, TOK))[:1 + (ph.tiles > LT)]):
                            dst = acc[:, bass.ds(n, 1), a:b].rearrange("p a b -> p (a b)")
                            g2 = mods_v[:, ph.layer, 5, bass.ds(n, 1), c]
                            if ph.part == 0:
                                last = nc.vector.tensor_scalar(dst, span(2 * s, b - a, a), g2, None, ALU.mult)
                            else:
                                last = nc.vector.scalar_tensor_tensor(dst, span(2 * s, b - a, a), g2, dst, ALU.mult,
                                                                      ALU.add)
                        last.then_inc(S("summed"), 1)

            for ph in phases:
                work = {"first_norm": first_norm, "modulate": modulate, "tokens_a": tokens_a, "fourier": fourier,
                        "merge": merge, "attention": attention, "residual": residual, "gate_up": gate_up,
                        "down": down}.get(ph.kind)
                if work:
                    work(ph)

        @block.tensor
        def _(pe):
            prime(pe, ("piece", "attended", "scored", "turned_p"))

            pe.wait_ge(S("cond_ready"), 1)
            with pe.Fori(0, DEPTH * ADA_UNITS // ADA_SLOTS) as i:
                for s in range(ADA_SLOTS):
                    pe.wait_ge(ada_ready[s], 16 * i + 16)
                    for k in range(KD):
                        last = nc.tensor.matmul(ps[:, 7, bass.ds(2 * ADA_SLOTS * i + 2 * s, 2)],
                                                ada_raw[:, s, k * P:(k + 1) * P], cond_act[:, k, :],
                                                start=(k == 0), stop=(k == KD - 1))
                    last.then_inc(S("ada_used"), 1)

            def columns(ph, u, s, bank, x_hi, x_lo, k_tiles, first=0):
                pe.wait_ge(S("lo_made"), u + 1)
                wide = ph.width > LAT
                for k in range(k_tiles):
                    for name in TERMS:
                        w, x = term(name, s, x_hi, x_lo)
                        tile = w[:, s, (first + k) * P:(first + k + 1) * P]
                        start = k == 0 and name == TERMS[0]
                        stop = k == k_tiles - 1 and name == TERMS[-1]
                        last = nc.tensor.matmul(bank(0), tile, x[:, k, 0:LAT], start=start, stop=stop)
                        if wide:
                            last = nc.tensor.matmul(bank(1), tile, x[:, k, LAT:TOK], start=start, stop=stop)
                return last

            def fixed(b):
                return lambda half: ps[:, b, :] if half == 0 else ps[:, b + 1, 0:CTX]

            def modulate(ph):
                pe.wait_ge(S("consts"), 16 * 5)
                pe.wait_ge(S("mods_ready"), 1)
                pe.wait_ge(S("normed"), at(ph, "normed"))
                if ph.unit:
                    pe.wait_ge(S("added"), at(ph, "added"))
                for k in range(KD):
                    if k >= 4:
                        pe.wait_ge(S("h_val"), at(ph, "h_val") + k - 3)
                    for t in range(ph.tiles):
                        last = nc.tensor.transpose(span(2 * (k % 4), P, t * P), xn[:, t, k * P:(k + 1) * P], ident[:, :])
                    last.then_inc(S("turned"), 1)

            def fourier_in(ph):
                pe.wait_ge(S("h_lo"), at(ph, "h_lo"))
                with pe.Fori(0, KB // 2) as i:
                    for s in range(2):
                        def bank(half):
                            b = ps[:, bass.ds(4 * i + 2 * s + half, 1), :].rearrange("p a b -> p (a b)")
                            return b if half == 0 else b[:, 0:CTX]
                        columns(ph, ph.unit + 2 * i + s, s, bank, h_hi, h_lo, KD).then_inc(S("unit_done"), 1)

            def tokens(ph):
                if ph.kind == "tokens_a":
                    groups = ((4, ph.tiles, 512), (2, ALLT, 256))
                else:
                    groups = ((4, ph.tiles, 512), (4, ALLT, 512), (4, ALLT, 512))
                    pe.wait_ge(S("merged"), at(ph, "merged"))
                    pe.wait_ge(S("gated"), at(ph, "gated"))
                if ph.kind == "tokens_a":
                    pe.wait_ge(S("evacuated"), at(ph, "evacuated"))
                u, bank = ph.unit, 0
                for units, tiles, cols in groups:
                    per = UNIT * P // cols
                    for j in range(units):
                        s = j % 2
                        pe.wait_ge(S("lo_made"), u + j + 1)
                        for kk in range(per):
                            k = j * per + kk
                            for t in range(tiles):
                                if k == 0 and bank + t >= 8:
                                    pe.wait_ge(S("evacuated"), at(ph, "evacuated") + bank + t - 7)
                                for name in TERMS:
                                    w, x = {"lo_hi": (w_lo, h_hi), "hi_lo": (w_hi, h_lo), "hi_hi": (w_hi, h_hi)}[name]
                                    last = nc.tensor.matmul(ps[:, (bank + t) % 8, 0:cols], x[:, k, t * P:(t + 1) * P],
                                                            w[:, s, kk * cols:(kk + 1) * cols],
                                                            start=k == 0 and name == TERMS[0],
                                                            stop=k == KD - 1 and name == TERMS[-1])
                        last.then_inc(S("unit_done"), 1)
                    u += units
                    bank += tiles

            def fourier(ph):
                pe.wait_ge(S("evacuated"), at(ph, "evacuated"))
                for n in range(2 * ph.tiles):
                    t, g = n // 2, n % 2
                    if n >= 8:
                        pe.wait_ge(S("evacuated"), at(ph, "evacuated") + n - 7)
                    for j in range(2):
                        last = nc.tensor.matmul(ps[:, n % 8, 256 * j:256 * j + 256],
                                                u_cols[:, 2 * g + j, t * P:(t + 1) * P], dft_c[:, :],
                                                start=True, stop=True)
                    last.then_inc(S("z_made"), 1)
                pe.wait_ge(S("evacuated"), at(ph, "evacuated") + 2 * ph.tiles)
                pe.wait_ge(S("dft_loaded"), 32 * (ph.layer + 1))
                for g in range(KB):
                    for t in range(LT):
                        for part in range(2):
                            last = nc.tensor.matmul(ps[:, 2 * g, :], z_sb[:, t, g, part * P:(part + 1) * P],
                                                    dft_l[:, t, part, :], start=t + part == 0,
                                                    stop=t + part == LT)
                    for t in range(ph.tiles - LT):
                        for part in range(2):
                            last = nc.tensor.matmul(ps[:, 2 * g + 1, 0:CTX],
                                                    z_sb[:, LT + t, g, part * P:(part + 1) * P],
                                                    dft_x[:, t, part, :], start=t + part == 0, stop=t + part == CT)
                    last.then_inc(S("mixed"), 1)

            def merge(ph):
                pe.wait_ge(S("o_lo"), at(ph, "o_lo"))
                read = "merged" if ph.part == 2 else "branch_read"
                with pe.Fori(0, 2) as i:
                    for half in range(2):
                        for j in range(3):
                            n = 3 * half + j
                            u = ph.unit + 6 * i + n
                            if j < 2:
                                pe.wait_ge(S("gated"), at(ph, "gated") + 4 * i + 2 * half + j - 1)
                                columns(ph, u, n % 2, fixed(2 * j), h_hi, h_lo, KD).then_inc(S("unit_done"), 1)
                            else:
                                for c in range(2):
                                    pe.wait_ge(S(read), at(ph, read) + 4 * i + 2 * half + c - 1)
                                    last = columns(ph, u, n % 2, fixed(4 + 2 * c), o_hi, o_lo, KB, first=KB * c)
                                last.then_inc(S("unit_done"), 1)

            def attention(ph):
                t_n, rounds, branch = ph.tiles, ROUNDS[ph.tiles], ph.part
                v = v_a if branch == 0 else v_b

                def piece(h, s, r):
                    what, a, b = PIECES[r]
                    if r == 0:
                        pe.wait_ge(S("staged"), at(ph, "staged") + 2 * h + 2)
                    pe.wait_ge(S("piece_lo"), at(ph, "piece_lo") + rounds * h + r)
                    src = stage_q[s] if what == "q" else stage_k[s]
                    for t in range(a // P, b // P):
                        last = nc.tensor.transpose(ps[:, 7, t * P - a:(t + 1) * P - a],
                                                   src[:, t, :, :].rearrange("p a b -> p (a b)"), ident[:, :])
                    last.then_inc(S("piece"), 1)

                def score(n, h, hs, s, t):
                    if t == 0:
                        pe.wait_ge(S("piece_lo"), at(ph, "piece_lo") + rounds * h + rounds)
                    pe.wait_ge(S("probs"), at(ph, "probs") + n - 1)
                    runs = key_runs(branch, t)
                    for part, kk in enumerate((k_hh[hs], k_ll[hs])):
                        for a, b, at_col in runs:
                            if part == 0 and at_col == 0:
                                first = True
                            last = nc.tensor.matmul(span(2 * s, b - a, at_col) if at_col < 512 else
                                                    ps[:, 2 * s + 1, at_col - 512:at_col - 512 + b - a],
                                                    q_st[hs][:, t * P:(t + 1) * P], kk[:, a:b],
                                                    start=part == 0 and at_col in (0, 512), stop=part == 1,
                                                    skip_group_check=True)
                    last.then_inc(S("scored"), 1)

                def turn(n, h, s, t):
                    pe.wait_ge(S("probs"), at(ph, "probs") + n + 1)
                    pe.wait_ge(S("pt_act"), at(ph, "pt_act") + n)
                    pe.wait_ge(S("pt_dve"), at(ph, "pt_dve") + wide_tiles(branch, t_n) * h + wide_tiles(branch, t))
                    for kk in range(len(key_tiles(branch, t))):
                        last = nc.tensor.transpose(ps[:, 4 + kk // 4, (kk % 4) * P:(kk % 4 + 1) * P],
                                                   p_sb[s][:, kk * P:(kk + 1) * P], ident[:, :])
                    last.then_inc(S("turned_p"), 1)

                def attend(n, h, t):
                    pe.wait_ge(S("pt_act"), at(ph, "pt_act") + n + 1)
                    pe.wait_ge(S("pt_dve"), at(ph, "pt_dve") + wide_tiles(branch, t_n) * h + wide_tiles(branch, t + 1))
                    pe.wait_ge(S("o_norm"), at(ph, "o_norm") + n)
                    col = (h // 4) * HD if branch == 0 else h * HD
                    tiles = key_tiles(branch, t)
                    for kk, kt in enumerate(tiles):
                        last = nc.tensor.matmul(ps[:, 6, 0:HD], pt_sb[:, kk * P:(kk + 1) * P],
                                                v[:, kt, bass.ds(col, HD)], start=kk == 0, stop=kk == len(tiles) - 1)
                    last.then_inc(S("attended"), 1)

                for r in range(rounds):
                    piece(0, 0, r)
                score(0, 0, 0, 0, 0)
                score(1, 0, 0, 1, 1)

                def pair(i, last):
                    for m in range(2 * t_n):
                        n = 2 * t_n * i + m
                        for s, h, r in pieces_at(t_n, m, last):
                            piece(2 * i + h, s, r)
                        turn(n, 2 * i + m // t_n, m % 2, m % t_n)
                        if m + 2 < 2 * t_n:
                            hs = (m + 2) // t_n
                            score(n + 2, 2 * i + hs, hs, m % 2, (m + 2) % t_n)
                        elif not last:
                            score(n + 2, 2 * i + 2, 0, m % 2, m + 2 - 2 * t_n)
                        attend(n, 2 * i + m // t_n, m % t_n)

                with pe.Fori(0, HEADS // 2 - 1) as i:
                    pair(i, False)
                pair(HEADS // 2 - 1, True)
                pe.wait_ge(S("o_norm"), at(ph, "o_norm") + HEADS * t_n)
                for t in range(t_n):
                    if t >= 4:
                        pe.wait_ge(S("o_lo"), at(ph, "o_lo") + t - 3)
                    for c in range(KB):
                        last = nc.tensor.transpose(ps[:, t % 4, c * P:(c + 1) * P], o_tok[:, t, c * P:(c + 1) * P],
                                                   ident[:, :])
                    last.then_inc(S("o_turned"), 1)

            def project(ph):
                pe.wait_ge(S("y_split"), at(ph, "y_split"))
                pe.wait_ge(S("gated"), at(ph, "gated"))
                with pe.Fori(0, KD // 2) as i:
                    for s in range(2):
                        pe.wait_ge(S("projected"), at(ph, "projected") + 2 * i + s - 1)
                        columns(ph, ph.unit + 2 * i + s, s, fixed(2 * s), y_hi, y_lo, KD).then_inc(S("unit_done"), 1)

            def residual(ph):
                pe.wait_ge(S("projected"), at(ph, "projected"))
                if ph.part == 1:
                    pe.wait_ge(S("summed"), at(ph, "summed"))
                for t in range(ph.tiles):
                    if t >= 4:
                        pe.wait_ge(S("added"), at(ph, "added") + t - 3)
                    for j in range(KD):
                        last = nc.tensor.transpose(span(2 * (t % 4), P, j * P) if j < 4 else
                                                   ps[:, 2 * (t % 4) + 1, (j - 4) * P:(j - 3) * P],
                                                   acc[:, j, t * P:(t + 1) * P], ident[:, :])
                    last.then_inc(S("turned"), 1)

            def gate_up(ph):
                pe.wait_ge(S("h_lo"), at(ph, "h_lo"))
                pe.wait_ge(S("summed"), at(ph, "summed"))
                with pe.Fori(0, PARTS[ph.part][1] // 2) as i:
                    for c in range(2):
                        u = ph.unit + 4 * i + 2 * c
                        pe.wait_ge(S("silu"), at(ph, "silu") + 2 * i + c - 1)
                        columns(ph, u, 0, fixed(4 * c), h_hi, h_lo, KD).then_inc(S("unit_done"), 1)
                        pe.wait_ge(S("hidden"), at(ph, "hidden") + 2 * i + c - 1)
                        columns(ph, u + 1, 1, fixed(4 * c + 2), h_hi, h_lo, KD).then_inc(S("unit_done"), 1)

            def down(ph):
                chunks = PARTS[ph.part][1]
                pe.wait_ge(S("hidden_lo"), at(ph, "hidden_lo"))
                with pe.Fori(0, KD // 2) as i:
                    for s in range(2):
                        pe.wait_ge(S("summed"), at(ph, "summed") + 2 * i + s - 1)
                        columns(ph, ph.unit + 2 * i + s, s, fixed(2 * s), hid_hi, hid_lo, chunks
                                ).then_inc(S("unit_done"), 1)

            for ph in phases:
                work = {"modulate": modulate, "fourier_in": fourier_in, "tokens_a": tokens, "tokens_b": tokens,
                        "fourier": fourier, "merge": merge, "attention": attention, "project": project,
                        "residual": residual, "gate_up": gate_up, "down": down}.get(ph.kind)
                if work:
                    work(ph)


PIECES = (("q", 0, LAT), ("k", 0, LAT), ("k", LAT, TOK), ("q", LAT, TOK))


def pieces_at(t_n, m, last):
    if t_n == ALLT:
        first = {0: (0,), 1: (1,), 2: (2,), 3: (3,)}
        second = {6: (0,), 7: (1,), 8: (2,), 9: (3,)}
    else:
        first = {0: (0, 1), 1: (2,)}
        second = {3: (0,), 4: (1,), 5: (2,)}
    got = [(1, 1, r) for r in first.get(m, ())]
    if not last:
        got += [(0, 2, r) for r in second.get(m, ())]
    return got


def key_tiles(branch, t):
    ctx = [LT + c for c in range(CT)]
    if t >= LT:
        return ctx
    if branch == 0:
        return ctx + list(range(LT))
    return ctx + [FIRST_BLOCK[t] + b for b in range(BIAS_KEYS[t] // P)]


def wide_tiles(branch, n):
    return sum(P * len(key_tiles(branch, t)) > 512 for t in range(n))


def key_runs(branch, t):
    runs = [(LAT, TOK, 0)]
    lat = key_tiles(branch, t)[CT:]
    if lat:
        a = lat[0] * P
        runs.append((a, a + 256, 256))
        if len(lat) > 2:
            runs.append((a + 256, a + len(lat) * P, 512))
    return runs


def block_order(a):
    return a.reshape(ROWS, GRID_W // WIN, WIN, *a.shape[1:]).swapaxes(0, 1).reshape(a.shape)


def feature_units(w):
    k, n = w.shape
    return w.reshape(k // P, P, n // P, P).transpose(2, 1, 0, 3).reshape(n // P, P, k)


def token_units(w, cols):
    per = UNIT * P // cols
    return w.reshape(KD // per, per, P, cols).transpose(0, 2, 1, 3).reshape(KD // per, P, per * cols)


def lay_stream(w_in, w_branch, w_out, w_gu, w_down):
    units = []
    for l in range(DEPTH):
        w = w_in[l]
        qa, ka, va, qb, kb, vb, uc, gz = np.split(w, np.cumsum((512, 128, 128, 512, 512, 512, 512)), axis=1)

        def merge(b):
            gates = feature_units(gz[:, b * D:(b + 1) * D])
            wb = w_branch[l, b].reshape(KB, P, KD // 2, 2, P).transpose(2, 1, 3, 0, 4).reshape(KD // 2, P, UNIT * P)
            for j in range(KD // 2):
                units.extend((gates[2 * j][None], gates[2 * j + 1][None], wb[j][None]))

        units.append(feature_units(uc))
        units.append(token_units(qa, 512))
        units.append(token_units(np.concatenate([ka, va], 1), 256))
        merge(2)
        merge(0)
        for m in (qb, kb, vb):
            units.append(token_units(m, 512))
        merge(1)
        units.append(feature_units(w_out[l]))
        gate, up = feature_units(w_gu[l][:, :D_FF]), feature_units(w_gu[l][:, D_FF:])
        for first, count in PARTS:
            for c in range(first, first + count):
                units.extend((gate[c][None], up[c][None]))
            rows = w_down[l][first * P:(first + count) * P]
            part = np.zeros((KD, P, UNIT * P), w_down.dtype)
            part[:, :, :count * P] = feature_units(rows)
            units.append(part)
    return np.concatenate(units, 0)


def lay_bias(rpb):
    out = np.full((DEPTH, HEADS, P, BIAS_W), MASKED, rpb.dtype)
    row, col = np.divmod(np.arange(P), WIN)
    for block in range(GRID_W // WIN):
        if block == 2:
            continue
        q_col = block * WIN + col
        start = np.clip(q_col - WIN // 2, 0, GRID_W - WIN)
        for b in range(BIAS_KEYS[block] // P):
            k_col = (FIRST_BLOCK[block] + b) * WIN + col
            dr = row[None, :] - row[:, None] + ROWS - 1
            dc = k_col[None, :] - q_col[:, None] + WIN - 1
            seen = (k_col[None, :] >= start[:, None]) & (k_col[None, :] < start[:, None] + WIN)
            at = BIAS_AT[block] + b * P
            got = rpb[:, :, dr, np.clip(dc, 0, 2 * WIN - 2)]
            out[:, :, :, at:at + P] = np.where(seen, got, out[:, :, :, at:at + P])
    return out


def shape_tables():
    ident = np.eye(P, dtype=np.float32)
    quarter = HD // 4
    freqs = (10000.0 ** (-np.arange(quarter, dtype=np.float32) / np.float32(quarter))).astype(np.float32)
    pos = block_order(np.arange(LAT))
    rope = np.zeros((2, TOK, HD), np.float32)
    rope[0] = 1.0
    for half, where in enumerate((pos // GRID_W, pos % GRID_W)):
        ang = (where.astype(np.float32)[:, None] * freqs).astype(np.float32)
        for q in range(2):
            sl = slice(half * 2 * quarter + q * quarter, half * 2 * quarter + (q + 1) * quarter)
            rope[0, :LAT, sl] = np.cos(ang)
            rope[1, :LAT, sl] = (-1.0, 1.0)[q] * np.sin(ang)
    rope = rope.reshape(2, ALLT, P, HD).transpose(2, 0, 1, 3)

    def angles(n, i, j):
        return 2.0 * np.pi * ((i[:, None] * j[None, :]) % n) / n

    ch = angles(P, np.arange(P), np.arange(P))
    dft_ch = np.concatenate([np.cos(ch), np.sin(ch)], 1)
    lat = angles(LAT, pos, pos)
    dft_lat = np.stack([np.cos(lat), -np.sin(lat)], 1) / np.sqrt(LAT * P)
    ctx = angles(CTX, np.arange(CTX), np.arange(CTX))
    dft_ctx = np.stack([np.cos(ctx), -np.sin(ctx)], 1) / np.sqrt(CTX * P)
    dft_lat = dft_lat.reshape(LT, P, 2, LAT).transpose(1, 0, 2, 3)
    dft_ctx = dft_ctx.reshape(CT, P, 2, CTX).transpose(1, 0, 2, 3)
    return [np.ascontiguousarray(a, np.float32) for a in (ident, rope, dft_ch, dft_lat, dft_ctx)]


def lay_out(x, c, ctx, c_ctx, w_ada, b_ada, w_in, q_norm, k_norm, rpb, w_branch, w_out, ln1_g, ln1_b, w_gu, w_down,
            ln2_g, ln2_b):
    swap = np.arange(HD).reshape(2, 2, HD // 4)[:, ::-1].reshape(HD)
    ident, rope, dft_ch, dft_lat, dft_ctx = shape_tables()
    cond = np.stack([c[0].reshape(KD, P).T, c_ctx.reshape(KD, P).T], 2)
    return {
        "x_in": block_order(x[0]),
        "ctx_in": ctx[0],
        "cond": cond,
        "w_ada": np.concatenate([feature_units(w_ada[l]) for l in range(DEPTH)], 0),
        "b_ada": b_ada.reshape(DEPTH * ADA_UNITS, P).T,
        "stream": lay_stream(w_in, w_branch, w_out, w_gu, w_down),
        "qk_gain": np.stack([q_norm, q_norm[:, swap], k_norm, k_norm[:, swap]], 1).reshape(-1),
        "norm_rows": np.stack([np.stack([ln1_g, ln1_b], 1), np.stack([ln2_g, ln2_b], 1)], 1),
        "bias": lay_bias(rpb),
        "ident_in": ident, "rope_in": rope, "dft_ch": dft_ch, "dft_lat": dft_lat, "dft_ctx": dft_ctx,
    }


def program(nc, arrays):
    args = [nc.dram_tensor(f"in_{n}", a.shape, mybir.dt.from_np(a.dtype), kind="ExternalInput").ap()
            for n, a in arrays.items()]
    scratch = nc.dram_tensor("scratch", (2 * DEPTH, ALLT, P, D), F32, kind="Internal").ap()
    out = nc.dram_tensor("out_x", (LT, P, D), F32, kind="ExternalOutput").ap()
    build(nc, *args, scratch, out)


def kernel(**inputs):
    import concourse.bacc as bacc
    from concourse.bass_utils import run_bass_kernel_spmd

    arrays = {n: np.ascontiguousarray(a) for n, a in
              lay_out(**{n: np.asarray(a) for n, a in inputs.items()}).items()}
    nc = bacc.Bacc("TRN2", target_bir_lowering=False, num_devices=1)
    program(nc, arrays)
    r = run_bass_kernel_spmd(nc, [{f"in_{n}": a for n, a in arrays.items()}], core_ids=[0])
    got = r.results[0]["out_x"].reshape(GRID_W // WIN, ROWS, WIN, D)
    return np.ascontiguousarray(got.swapaxes(0, 1).reshape(1, LAT, D))
```

```python
import concourse.bass as bass
from concourse import mybir
import numpy as np

F32 = mybir.dt.float32
F32R = mybir.dt.float32r
ALU = mybir.AluOpType
ACT = mybir.ActivationFunctionType
AX = mybir.AxisListType

DEPTH = 2
D = 1024
LAT, CTX = 512, 256
P = 128
KD = D // P
LT, CT = LAT // P, CTX // P
ALLT = LT + CT
TOK = LAT + CTX
HD = 64
HEADS = 8
KV_A = 2
GRID_W, ROWS, WIN = 64, 8, 16
BRANCH = 512
KB = BRANCH // P
D_FF = 2816
FF = D_FF // P
UNIT = 8
PARTS = ((0, 8), (8, 8), (16, 6))
ALPHA = (2.0 * DEPTH) ** 0.25
EPS = 1e-6
QSCALE = HD ** -0.5
MASKED = -1e30
BIAS_AT = (0, 256, 256, 640)
BIAS_KEYS = (256, 384, 384, 256)
FIRST_BLOCK = (0, 0, 1, 2)
BIAS_W = 896
ADA_UNITS = 6 * D // P
ADA_SLOTS = 3
ROUNDS = {ALLT: 4, LT: 3}
PRIME = 8
ADA_WINDOWS = {("fourier_in", 0): (18, 42), ("tokens_b", 0): (42, 48)}
ADA_BESIDE = {("gate_up", 0): 48, ("down", 0): 60, ("gate_up", 1): 72, ("down", 1): 84}
ADA_PER_PAIR = 6
ROTATE_STEPS = 5 + 3 * ALLT
ADA_FIRST = 18
NORM_ORDER = (("add", 0), ("square", 0), ("add", 1), ("square", 1), ("var", 0), ("std", 0), ("add", 2), ("square", 2),
              ("root", 0), ("affine", 0), ("var", 1), ("std", 1), ("square2", 0), ("root", 1), ("affine", 1),
              ("var2", 0), ("std2", 0), ("var", 2), ("std", 2), ("square2", 1), ("root2", 0), ("apply", 0),
              ("root", 2), ("affine", 2), ("var2", 1), ("std2", 1), ("square2", 2), ("root2", 1), ("apply", 1),
              ("var2", 2), ("std2", 2), ("root2", 2), ("apply", 2))


class Phase:

    def __init__(self, kind, layer, tiles, unit, part=None):
        self.kind, self.layer, self.tiles, self.unit, self.part = kind, layer, tiles, unit, part
        self.width = tiles * P
        self.pairs = 0
        self.at = {}


def plan():
    phases, unit = [], 0

    def add(kind, layer, tiles, units=0, part=None):
        nonlocal unit
        phases.append(Phase(kind, layer, tiles, unit, part))
        unit += units

    add("first_norm", 0, ALLT)
    for layer in range(DEPTH):
        t = ALLT if layer < DEPTH - 1 else LT
        add("modulate", layer, ALLT, part=0)
        add("fourier_in", layer, t, 4)
        add("tokens_a", layer, t, 6)
        add("fourier", layer, t)
        add("merge", layer, t, 12, part=2)
        add("attention", layer, t, part=0)
        add("merge", layer, t, 12, part=0)
        add("tokens_b", layer, t, 12)
        add("attention", layer, t, part=1)
        add("merge", layer, t, 12, part=1)
        add("project", layer, t, 8)
        add("residual", layer, t, part=0)
        add("modulate", layer, t, part=1)
        for part, (_, chunks) in enumerate(PARTS):
            add("gate_up", layer, t, 2 * chunks, part=part)
            phases[-1].pairs = chunks
            add("down", layer, t, 8, part=part)
            phases[-1].pairs = 4
        add("residual", layer, t, part=1)
    counts = {}
    for ph in phases:
        ph.at = dict(counts)
        for name, n in increments(ph).items():
            counts[name] = counts.get(name, 0) + n
    return phases, unit


def ada_beside(ph):
    return ADA_BESIDE.get((ph.kind, ph.part)) if ph.layer == 0 and ph.kind in ("gate_up", "down") else None


def increments(ph):
    t, k = ph.tiles, ph.kind
    if k in ("first_norm", "residual"):
        first = k == "first_norm"
        last = ph.layer == DEPTH - 1 and ph.part == 1
        norms = 1 if first or last else 2
        groups = norms * t // 2
        got = {"mean_ready": norms * t, "squared": norms * t, "var_ready": groups, "std_ready": groups,
               "root_ready": groups, "normed": 0 if last else t}
        got["norm_step"] = groups // norms * ((not first) * 4 + (not last) * 5)
        if first:
            return {**got, "loaded": 16 * t, "summed_x": t}
        return {**got, "turned": t, "added": t, "scaled": t, "shifted": t, "stored": 16 * t, "rows_loaded": 32}
    if k == "modulate":
        return {"turned": KD, "h_val": KD, "h_hi": KD, "h_lo": KD // 2, "h_lo_pool": KD // 2}
    if k == "fourier_in":
        return {"evacuated": 4}
    if k == "tokens_a":
        return {"evacuated": t + ALLT, "rope_step": 8 + 5 * ALLT, "var_ready": 1}
    if k == "tokens_b":
        return {"evacuated": t + 2 * ALLT - ALLT // 2, "values_out": ALLT // 2}
    if k == "fourier":
        return {"z_made": 2 * t, "evacuated": 2 * t, "mixed": KB, "o_hi": KB, "o_lo": KB, "std_ready": 1}
    if k == "merge":
        return {"gated": KD, "branch_read": KD * (ph.part != 2), "merged": KD, "y_split": 2 * KD * (ph.part == 1)}
    if k == "attention":
        n, r = HEADS * t, HEADS * ROUNDS[t]
        return {"staged": 2 * HEADS, "piece": r, "piece_hi": r, "piece_lo": r, "scored": n, "max_part": n,
                "max_ready": n, "probs": n, "turned_p": n, "pt_act": n, "pt_dve": HEADS * wide_tiles(ph.part, t), "attended": n,
                "inverse": n, "o_norm": n, "o_turned": t, "o_hi": t, "o_lo": t}
    if k == "project":
        return {"projected": KD, "loaded": 16 * t}
    if k == "gate_up":
        n = PARTS[ph.part][1]
        return {"silu": n, "hidden": n, "hidden_hi": n, "hidden_lo": n}
    if k == "down":
        return {"summed": KD, "loaded": 16 * t * (ph.part == len(PARTS) - 1)}
    raise ValueError(k)


def build(nc, x_in, ctx_in, cond, cond_cols, w_first, w_ada, b_ada, stream, qk_gain, norm_rows, bias, ident_in, rope_in, dft_ch, dft_lat,
          dft_ctx, scratch, cond_scratch, out):
    phases, n_units = plan()

    base = (nc.sbuf_base + 63) // 64 * 64
    end = nc.sbuf_top
    cursor = [base]

    def sb(name, shape, dtype=F32, at=None):
        size = (2 if dtype == mybir.dt.bfloat16 else 4) * int(np.prod(shape[1:]))
        if at is None:
            at = cursor[0]
            cursor[0] += (size + 63) // 64 * 64
        assert at + size <= end, (name, at + size - end)
        return nc.alloc_sbuf_tensor_at(name, shape, dtype, offset=at)

    K = 1024
    raw = sb("raw", [P, 2, UNIT * P])
    w_hi = sb("w_hi", [P, 2, UNIT * P], F32R)
    w_lo = sb("w_lo", [P, 2, UNIT * P], F32R)
    h_hi = sb("h_hi", [P, KD, TOK], F32R)
    h_lo = sb("h_lo", [P, KD, TOK], F32R)
    acc = sb("acc", [P, KD, TOK])
    ident = sb("ident", [P, P])
    rope = sb("rope", [P, 2, ALLT, HD])
    rope_g = sb("rope_g", [P, 4, ALLT, HD])
    gain = sb("gain", [P, DEPTH, 4, HD])
    mods = sb("mods", [P, DEPTH * ADA_UNITS, 2])
    mods_v = mods[:, :, :].rearrange("p (l s k) c -> p l s k c", l=DEPTH, s=6)
    ada_bias = sb("ada_bias", [P, DEPTH * ADA_UNITS])
    sum_s = sb("sum_s", [P, 2, ALLT])
    neg_mean = sb("neg_mean", [P, 2, ALLT])
    square_s = sb("square_s", [P, 2, ALLT])
    NH_A = HEADS + KV_A
    var_s = sb("var_s", [P, ALLT * NH_A])
    std_s = sb("std_s", [P, ALLT * NH_A])
    inv_s = sb("inv_s", [P, ALLT * NH_A])
    tmp_s = sb("tmp_s", [P, ALLT * NH_A])
    shift_s = sb("shift_s", [P, ALLT])
    max_c = sb("max_c", [P, 2])
    max_a = sb("max_a", [P, 2])
    neg_max = sb("neg_max", [P, 2])
    row_sum = sb("row_sum", [P, 4])
    row_inv = sb("row_inv", [P, 4])
    dft_c = sb("dft_c", [P, 2 * P])
    R = cursor[0]

    o_hi = sb("o_hi", [P, KB, TOK], F32R, at=R)
    o_lo = sb("o_lo", [P, KB, TOK], F32R, at=R + 12 * K)
    u_cols = sb("u_cols", [P, KB, TOK], at=R)
    q_st = [sb(f"q_st{s}", [P, TOK], F32R, at=R + 3 * K * s) for s in range(2)]
    k_hh = [sb(f"k_hh{s}", [P, TOK], F32R, at=R + 6 * K + 3 * K * s) for s in range(2)]
    k_ll = [sb(f"k_ll{s}", [P, TOK], F32R, at=R + 12 * K + 3 * K * s) for s in range(2)]
    stage_q = [[sb(f"stage_q{b}{s}", [P, ALLT, 2, HD], at=R + (54, 18)[b] * K + 3 * K * s) for s in range(2)]
               for b in range(2)]
    stage_k = [[sb(f"stage_k{b}{s}", [P, ALLT, 2, HD], at=R + (88, 82)[b] * K + 3 * K * s) for s in range(2)]
               for b in range(2)]
    tok_a = sb("tok_a", [P, ALLT, NH_A * HD], at=R + 24 * K)
    v_a = sb("v_a", [P, ALLT, KV_A * HD], at=R + 39 * K)
    z_sb = sb("z_sb", [P, ALLT, KB, 2 * P], at=R + 42 * K)
    dft_l = sb("dft_l", [P, LT, 2, LAT], at=R + 66 * K)
    dft_x = sb("dft_x", [P, CT, 2, CTX], at=R + 82 * K)
    rope_t = [sb(f"rope_t{s}", [P, NH_A * HD], at=R + 86 * K + 2560 * s) for s in range(2)]
    tok_b = sb("tok_b", [P, ALLT, 2, BRANCH], at=R + 24 * K)
    v_b = sb("v_b", [P, ALLT, BRANCH], at=R + 48 * K)
    o_tok = sb("o_tok", [P, ALLT, BRANCH], at=R + 60 * K)
    keys_n = (TOK, CTX + max(BIAS_KEYS))
    p_sb = [[sb(f"p_sb{b}{s}", [P, keys_n[b]], at=R + (42, 72)[b] * K + 4 * keys_n[b] * s) for s in range(2)]
            for b in range(2)]
    pt_sb = [[sb(f"pt_sb{b}{s}", [P, keys_n[b]], at=R + (48, 77)[b] * K + 4 * keys_n[b] * s) for s in range(2)]
             for b in range(2)]
    bias_sb = [sb(f"bias_sb{s}", [P, BIAS_W], at=R + 88 * K + 3584 * s) for s in range(2)]
    gate = sb("gate", [P, 4, TOK], at=R + 72 * K)
    y_hi = sb("y_hi", [P, KD, TOK], F32R, at=R + 24 * K)
    y_lo = sb("y_lo", [P, KD, TOK], F32R, at=R + 48 * K)
    ln_rows = sb("ln_rows", [P, 2, D], at=R + 60 * K)
    unused = sb("unused", [P, D], at=R + 68 * K)
    xn = sb("xn", [P, ALLT, D], at=R + 24 * K)
    h_tmp = sb("h_tmp", [P, 4, TOK], at=R + 48 * K)
    xr = sb("xr", [P, ALLT, D], at=R + 72 * K)
    hid_hi = sb("hid_hi", [P, 8, TOK], F32R, at=R + 8 * K)
    hid_lo = sb("hid_lo", [P, 8, TOK], F32R, at=R + 32 * K)
    silu_g = sb("silu_g", [P, 2, TOK], at=R + 56 * K)
    hid = sb("hid", [P, 2, TOK], at=R + 62 * K)
    ada_at = {"fourier_in": 42, "tokens_b": 60, "gate_up": 68}
    ada_raw = {k: sb(f"ada_raw_{k}", [P, ADA_SLOTS, D], at=R + a * K) for k, a in ada_at.items()}
    ada_cond = {k: sb(f"ada_cond_{k}", [P, 2, D], at=R + (a + 12) * K) for k, a in ada_at.items()}
    ada_unused = {k: sb(f"ada_unused_{k}", [P, D], mybir.dt.bfloat16, at=R + (a + 20) * K) for k, a in ada_at.items()}

    first_raw = sb("first_raw", [P, 2, ADA_FIRST * P], at=R)
    first_rows = sb("first_rows", [2, ADA_FIRST * P], at=R + 48 * K)
    cond_act = sb("cond_act", [P, KD, 2], at=R + 58 * K)
    cond_rows = sb("cond_rows", [2, D], at=R + 60 * K)

    ps = nc.alloc_psum_tensor("ps", [P, 8, 512], F32)

    def span(bank, width, start=0):
        n = (start + width + 511) // 512
        return ps[:, bank:bank + n, :].rearrange("p a b -> p (a b)")[:, start:start + width]

    sems = {}

    def S(name):
        if name not in sems:
            sems[name] = nc.alloc_semaphore(name)
        return sems[name]

    raw_ready = [nc.alloc_semaphore(f"raw_ready{s}") for s in range(2)]
    ada_ready = [nc.alloc_semaphore(f"ada_ready{s}") for s in range(ADA_SLOTS)]
    first_ready = [nc.alloc_semaphore(f"first_ready{s}") for s in range(2)]
    bias_ready = [nc.alloc_semaphore(f"bias_ready{s}") for s in range(2)]

    def after(ph):
        return phases[phases.index(ph) + 1]

    PRIMED = ("gated", "branch_read", "merged", "projected", "silu", "hidden", "summed", "probs", "piece", "piece_lo",
              "o_norm", "attended", "scored", "turned_p", "added", "evacuated", "pt_act", "pt_dve", "inverse", "ada_used")

    def at(ph, name):
        return ph.at.get(name, 0) + (PRIME if name in PRIMED else 0)

    def prime(eng, names):
        for name in names:
            eng.sem_inc(S(name), PRIME)

    TERMS = ("lo_hi", "hi_lo", "hi_hi")

    def term(name, slot, x_hi, x_lo):
        return {"lo_hi": (w_lo, x_hi), "hi_lo": (w_hi, x_lo), "hi_hi": (w_hi, x_hi)}[name]

    block = nc.Block()
    with block:

        @block.sync
        def _(sp):
            def load_pair(i):
                for s in range(2):
                    sp.wait_ge(S("lo_made"), 2 * i + s - 1)
                    sp.dma_start(raw[:, s, :], stream[bass.ds(2 * i + s, 1), :, :]
                                 .rearrange("a p c -> p (a c)")).then_inc(raw_ready[s], 16)

            def load_ada(kind, first, count):
                for n in range(count):
                    sp.wait_ge(S("ada_used"), PRIME - ADA_FIRST + first + n - ADA_SLOTS + 1)
                    sp.dma_start(ada_raw[kind][:, n % ADA_SLOTS, :], w_ada[bass.ds(first + n, 1), :, :]
                                 .rearrange("a p c -> p (a c)")).then_inc(ada_ready[n % ADA_SLOTS], 16)

            def load_beside(ph, first, done):
                each = ph.pairs // 4
                with sp.Fori(0, 4) as i:
                    load_ada("gate_up", first + ADA_SLOTS * i, ADA_SLOTS)
                    for n in range(each):
                        load_pair(done // 2 + each * i + n)

            sp.dma_start(cond_act[:, :, :], cond_cols[:, :, :]).then_inc(S("cond_loaded"), 16)
            for k in range(KD):
                if k >= 2:
                    sp.wait_ge(S("first_used"), k - 1)
                sp.dma_start(first_raw[:, k % 2, :], w_first[k, :, :]).then_inc(first_ready[k % 2], 16)
            for s in range(2):
                sp.dma_start(raw[:, s, :], stream[s, :, :]).then_inc(raw_ready[s], 16)
            done = 2
            for ph in phases:
                beside = ada_beside(ph)
                if beside and beside != ADA_UNITS:
                    load_beside(ph, beside, done)
                    done += 2 * ph.pairs
                    continue
                if (ph.kind, ph.layer) not in ADA_WINDOWS and not beside:
                    continue
                with sp.Fori(done // 2, ph.unit // 2 + 2) as i:
                    load_pair(i)
                done = ph.unit + 4
                if ph.kind == "fourier_in":
                    sp.wait_ge(S("h_lo"), at(ph, "h_lo"))
                    sp.wait_ge(S("h_lo_pool"), at(ph, "h_lo_pool"))
                elif ph.kind == "tokens_b":
                    sp.wait_ge(S("merged"), at(ph, "merged"))
                else:
                    sp.wait_ge(S("normed"), at(ph, "normed"))
                    sp.wait_ge(S("stored"), at(ph, "stored"))
                sp.wait_ge(S("cond_stored"), 16)
                sp.dma_start(ada_cond[ph.kind][:, :, :].rearrange("p a b -> p (a b)"),
                             cond_scratch.rearrange("a b -> (a b)").partition_broadcast(P)
                             ).then_inc(S("cond_loaded"), 16)
                if beside:
                    load_beside(ph, beside, done)
                    done += 2 * ph.pairs
                    continue
                first, end = ADA_WINDOWS[ph.kind, ph.layer]
                pairs = (end - first) // ADA_PER_PAIR
                with sp.Fori(0, pairs) as i:
                    load_ada(ph.kind, first + ADA_PER_PAIR * i, ADA_PER_PAIR // 2)
                    load_pair(i + done // 2)
                    load_ada(ph.kind, first + ADA_PER_PAIR * i + ADA_PER_PAIR // 2, ADA_PER_PAIR // 2)
                done += 2 * pairs
            with sp.Fori(done // 2, n_units // 2) as i:
                load_pair(i)

        @block.gpsimd
        def _(pool):
            def lo_parts(first, end):
                with pool.Fori(first // 2, end // 2) as i:
                    for s in range(2):
                        pool.wait_ge(S("hi_made"), 2 * i + s + 1)
                        nc.gpsimd.tensor_tensor(w_lo[:, s, :], raw[:, s, :], w_hi[:, s, :].bitcast(F32),
                                                ALU.subtract).then_inc(S("lo_made"), 1)

            def odd_rows(ph):
                for k in range(1, KD, 2):
                    pool.wait_ge(S("h_hi"), at(ph, "h_hi") + k + 1)
                    nc.gpsimd.tensor_tensor(h_lo[:, k, 0:ph.width], h_tmp[:, k % 4, 0:ph.width],
                                            h_hi[:, k, 0:ph.width].bitcast(F32), ALU.subtract
                                            ).then_inc(S("h_lo_pool"), 1)

            def stage_starts(ph):
                if ph.part == 0:
                    pool.wait_ge(S("rope_step"), at(ph, "rope_step"))
                else:
                    pool.wait_ge(S("evacuated"), at(ph, "evacuated") - ALLT // 2)

            def stage(ph, i, slots=(0, 1)):
                rounds = ROUNDS[ph.tiles]
                for s in slots:
                    h = 2 * i + s
                    pool.wait_ge(S("piece"), at(ph, "piece") + rounds * (2 * i + s - 1))
                    if ph.part == 0:
                        q_src = tok_a[:, 0:ph.tiles, bass.ds(h * HD, HD)]
                        k_src = tok_a[:, :, bass.ds(HEADS * HD + (i // 2) * HD, HD)]
                    else:
                        q_src = tok_b[:, 0:ph.tiles, 0, bass.ds(h * HD, HD)]
                        k_src = tok_b[:, :, 1, bass.ds(h * HD, HD)]
                    nc.gpsimd.tensor_copy(stage_q[ph.part][s][:, 0:ph.tiles, :, :],
                                          q_src.unsqueeze(2).broadcast_to([P, ph.tiles, 2, HD])
                                          ).then_inc(S("staged"), 1)
                    nc.gpsimd.tensor_copy(stage_k[ph.part][s][:, :, :, :],
                                          k_src.unsqueeze(2).broadcast_to([P, ALLT, 2, HD])
                                          ).then_inc(S("staged"), 1)

            done = 0
            for ph in phases:
                if ph.kind not in ("attention", "modulate"):
                    continue
                if ph.kind == "attention":
                    ahead = ph.unit - 2 * ph.part
                    lo_parts(done, ahead)
                    stage_starts(ph)
                    stage(ph, 0, (0,))
                    if ahead < ph.unit:
                        lo_parts(ahead, ph.unit)
                    stage(ph, 0, (1,))
                    lo_parts(ph.unit, ph.unit + 2)
                    with pool.Fori(1, HEADS // 2) as i:
                        stage(ph, i)
                    done = ph.unit + 2
                    continue
                if ph.unit + 2 > done:
                    lo_parts(done, ph.unit + 2)
                    done = ph.unit + 2
                odd_rows(ph)
            lo_parts(done, n_units)

        @block.scalar
        def _(act):
            prime(act, ("gated", "projected", "silu", "probs", "evacuated", "pt_act"))
            consts = [(ident[:, :], ident_in[:, :]), (rope[:, :, :, :], rope_in[:, :, :, :]),
                      (ada_bias[:, :], b_ada[:, :]), (dft_c[:, :], dft_ch[:, :])]
            act.dma_start(cond_rows[:, :], cond[:, :]).then_inc(S("cond_loaded"), 16)
            act.wait_ge(S("cond_loaded"), 32)
            nc.scalar.activation(cond_act[:, :, :], cond_act[:, :, :], ACT.Silu).then_inc(S("cond_ready"), 1)
            nc.scalar.activation(cond_rows[:, :], cond_rows[:, :], ACT.Silu).then_inc(S("cond_ready"), 1)
            act.wait_ge(S("cond_ready"), 2)
            act.dma_start(cond_scratch[:, :], cond_rows[:, :]).then_inc(S("cond_stored"), 16)

            def split(u, s):
                act.wait_ge(raw_ready[s], 8 * (u - s) + 16)
                nc.scalar.activation(w_hi[:, s, :], raw[:, s, :], ACT.Copy).then_inc(S("hi_made"), 1)

            def unit_done(u, s, ahead=True):
                act.wait_ge(S("unit_done"), u + 1)
                if ahead:
                    split(u + 2, s)

            def norm_steps(ph, first=False, last=False):
                seen = dict.fromkeys(("square", "std"), 0)
                for name, g in NORM_ORDER:
                    if not in_norms(name, g, ph, first, last):
                        continue
                    tiles = (2 * g, 2 * g + 1)
                    second = int(name.endswith("2"))
                    if name.startswith("square"):
                        for t in tiles:
                            if seen["square"]:
                                act.wait_ge(S("squared"), at(ph, "squared") + seen["square"])
                            seen["square"] += 1
                            act.wait_ge(S("mean_ready"), at(ph, "mean_ready") + seen["square"])
                            nc.scalar.activation(unused[:, :], xr[:, t, :], ACT.Square, bias=neg_mean[:, second, t:t + 1],
                                                 accum_out=square_s[:, second, t:t + 1]).then_inc(S("squared"), 1)
                    elif name.startswith("std"):
                        seen["std"] += 1
                        act.wait_ge(S("var_ready"), at(ph, "var_ready") + seen["std"])
                        a = ALLT * second + 2 * g
                        nc.scalar.activation(std_s[:, a:a + 2], var_s[:, a:a + 2], ACT.Sqrt).then_inc(S("std_ready"), 1)
                    elif name == "apply":
                        act.wait_ge(S("root_ready"), at(ph, "root_ready") + steps_before(("root2", g), ph, first, last))
                        for t in tiles:
                            nc.scalar.activation(xn[:, t, :], xr[:, t, :], ACT.Identity,
                                                 scale=inv_s[:, ALLT + t:ALLT + t + 1],
                                                 bias=shift_s[:, t:t + 1]).then_inc(S("normed"), 1)
                    if not first and name == ("affine" if last else "square2"):
                        store(ph, tiles, last)

            def store(ph, tiles, last):
                for t in tiles:
                    act.wait_ge(S("shifted"), at(ph, "shifted") + t + 1)
                    dst = out[t, :, :] if last else scratch[2 * ph.layer + ph.part + 1, t, :, :]
                    act.dma_start(dst, xr[:, t, :]).then_inc(S("stored"), 16)

            def rows_of_input(t):
                return x_in[t * P:(t + 1) * P, :] if t < LT else ctx_in[(t - LT) * P:(t - LT + 1) * P, :]

            def load_residual(ph):
                which = 0 if ph.kind == "project" else 1
                for t in range(ph.tiles):
                    src = rows_of_input(t) if ph.layer + which == 0 else scratch[ph.layer * 2 + which, t, :, :]
                    act.dma_start(xr[:, t, :], src).then_inc(S("loaded"), 16)

            def first_norm(ph):
                for t in range(ALLT):
                    act.dma_start(xr[:, t, :], rows_of_input(t)).then_inc(S("loaded"), 16)
                for dst, src in consts:
                    act.dma_start(dst, src).then_inc(S("consts"), 16)
                act.dma_start(gain[:, :, :, :].rearrange("p a b c -> p (a b c)"),
                              qk_gain.partition_broadcast(P)).then_inc(S("consts"), 16)
                norm_steps(ph, first=True)
                for s in range(2):
                    split(s, s)
                for b in range(-(-ADA_FIRST // 4)):
                    w = min(4, ADA_FIRST - 4 * b) * P
                    act.wait_ge(S("first_used"), KD)
                    nc.scalar.activation(first_rows[:, 512 * b:512 * b + w], ps[0:2, b, 0:w], ACT.Copy
                                         ).then_inc(S("rows_out"), 1)

            def modulate(ph):
                act.wait_ge(S("mods_ready"), MODS_READY[ph.layer, ph.part])
                if ph.unit:
                    act.wait_ge(S("unit_done"), ph.unit)
                m = 3 * ph.part
                for k in range(KD):
                    slot = 2 * (k % 4)
                    act.wait_ge(S("turned"), at(ph, "turned") + k + 1)
                    if k >= 4:
                        act.wait_ge(S("h_lo"), at(ph, "h_lo") + (k - 4) // 2 + 1)
                        if k % 2:
                            act.wait_ge(S("h_lo_pool"), at(ph, "h_lo_pool") + (k - 4) // 2 + 1)
                    for c, (a, b) in enumerate(((0, LAT), (LAT, TOK))[:1 + (ph.tiles > LT)]):
                        last = nc.scalar.activation(h_tmp[:, k % 4, a:b], span(slot, b - a, a), ACT.Identity,
                                                    scale=mods_v[:, ph.layer, m + 1, k, c:c + 1],
                                                    bias=mods_v[:, ph.layer, m, k, c:c + 1])
                    last.then_inc(S("h_val"), 1)
            def fourier_in(ph):
                with act.Fori(0, KB // 2) as i:
                    for s in range(2):
                        unit_done(ph.unit + 2 * i + s, s)
                        src = ps[:, bass.ds(4 * i + 2 * s, 2), :].rearrange("p a b -> p (a b)")[:, 0:ph.width]
                        nc.scalar.activation(u_cols[:, bass.ds(2 * i + s, 1), 0:ph.width].rearrange("p a b -> p (a b)"),
                                             src, ACT.Copy).then_inc(S("evacuated"), 1)

            def groups(ph):
                if ph.kind == "tokens_a":
                    return ((4, ph.tiles, 512, lambda t: ((tok_a[:, t, 0:512], 0, 512),), 1.0),
                            (2, ALLT, 256, lambda t: ((tok_a[:, t, 512:640], 0, 128), (v_a[:, t, :], 128, 256)), 1.0))
                return ((4, ph.tiles, 512, lambda t: ((tok_b[:, t, 0, :], 0, 512),), QSCALE),
                        (4, ALLT, 512, lambda t: ((tok_b[:, t, 1, :], 0, 512),), 1.0),
                        (4, ALLT, 512, lambda t: ((v_b[:, t, :], 0, 512),), 1.0))

            def piece(ph, h, s, r, bank=7):
                what, a, b = PIECES[r]
                act.wait_ge(S("piece"), at(ph, "piece") + ROUNDS[ph.tiles] * h + r + 1)
                dst = q_st[s] if what == "q" else k_hh[s]
                nc.scalar.activation(dst[:, a:b], ps[:, bank, 0:b - a], ACT.Copy).then_inc(S("piece_hi"), 1)

            def load_bias(ph, h, s):
                act.dma_start(bias_sb[s][:, :], bias[ph.layer, bass.ds(h, 1), :, :]
                              .rearrange("a p c -> p (a c)")).then_inc(bias_ready[s], 16)

            def tokens(ph):
                if ph.kind == "tokens_b":
                    for s in range(2):
                        load_bias(ph, s, s)
                if ph.kind == "tokens_a":
                    act.dma_start(dft_l[:, :, :, :], dft_lat[:, :, :, :]).then_inc(S("dft_loaded"), 16)
                    act.dma_start(dft_x[:, :, :, :], dft_ctx[:, :, :, :]).then_inc(S("dft_loaded"), 16)
                banks, u, n = token_banks(ph), ph.unit, 0
                for units, tiles, cols, dests, scale in groups(ph):
                    values = ph.kind == "tokens_b" and u == ph.unit + 8
                    for j in range(units):
                        unit_done(u + j, j % 2)
                        if values:
                            for r in early_pieces(ph, j + 1):
                                piece(after(ph), 0, 0, r, START_BANKS[1][r])
                    u += units
                    for t in range(0, tiles, 1 + values):
                        for dst, a, b in dests(t):
                            last = nc.scalar.activation(dst, ps[:, banks[n], a:b], ACT.Copy, scale=scale)
                        last.then_inc(S("evacuated"), 1)
                        n += 1 + values

            def fourier(ph):
                for n in range(2 * ph.tiles):
                    g, t = divmod(n, ph.tiles)
                    if n == 0 and ph.layer == 0:
                        act.wait_ge(S("ada_used"), PRIME - ADA_FIRST + ADA_WINDOWS["fourier_in", 0][1])
                    act.wait_ge(S("z_made"), at(ph, "z_made") + n + 1)
                    nc.scalar.activation(z_sb[:, t, 2 * g:2 * g + 2, :].rearrange("p a b -> p (a b)"),
                                         ps[:, z_bank(ph, n), :], ACT.Copy).then_inc(S("evacuated"), 1)
                act.wait_ge(S("var_ready"), at(ph, "var_ready"))
                nc.scalar.activation(std_s[:, :], var_s[:, :], ACT.Sqrt).then_inc(S("std_ready"), 1)
                for g in range(KB):
                    act.wait_ge(S("mixed"), at(ph, "mixed") + g + 1)
                    nc.scalar.activation(o_hi[:, g, 0:ph.width], span(2 * g, ph.width), ACT.Copy).then_inc(S("o_hi"), 1)

            def merge(ph):
                with act.Fori(0, 2) as i:
                    for half in range(2):
                        for j in range(3):
                            n = 3 * half + j
                            unit_done(ph.unit + 6 * i + n, n % 2)
                            if j < 2:
                                c = 2 * half + j
                                act.wait_ge(S("merged"), at(ph, "merged") + 4 * i + c - 3)
                                nc.scalar.activation(gate[:, c, 0:ph.width], span(2 * j, ph.width), ACT.Sigmoid
                                                     ).then_inc(S("gated"), 1)

            def attention(ph):
                t_n, rounds, branch = ph.tiles, ROUNDS[ph.tiles], ph.part

                def probs(i, m):
                    n, s, t = 2 * t_n * i + m, m % 2, m % t_n
                    keys = P * len(key_tiles(branch, t))
                    act.wait_ge(S("max_ready"), at(ph, "max_ready") + n + 1)
                    act.wait_ge(S("inverse"), at(ph, "inverse") + n - 1)
                    act.wait_ge(S("turned_p"), at(ph, "turned_p") + n - 1)
                    nc.scalar.activation(p_sb[branch][s][:, 0:keys], span(2 * s, keys), ACT.Exp,
                                         bias=neg_max[:, s:s + 1], accum_out=row_sum[:, s:s + 1]
                                         ).then_inc(S("probs"), 1)

                def copy_turned(i, m):
                    keys = min(512, P * len(key_tiles(branch, m % t_n)))
                    act.wait_ge(S("turned_p"), at(ph, "turned_p") + 2 * t_n * i + m + 1)
                    nc.scalar.activation(pt_sb[branch][m % 2][:, 0:keys], span(4, keys), ACT.Copy
                                         ).then_inc(S("pt_act"), 1)

                if branch == 0:
                    for r in range(rounds):
                        piece(ph, 0, 0, r, START_BANKS[0][r])
                probs(0, 0)
                probs(0, 1)
                for r in range(2):
                    piece(ph, 1, 1, r)
                copy_turned(0, 0)

                def pair(i, last):
                    for m in range(1, 2 * t_n + 1 - last):
                        if m + 1 < 2 * t_n or not last:
                            probs(i, m + 1)
                        for h, r in pieces_at(t_n, m, last):
                            piece(ph, 2 * i + h, h % 2, r)
                        copy_turned(i, m)
                        for h in range(2):
                            if branch == 1 and m + 1 == (h + 1) * t_n - 1 and not last:
                                load_bias(ph, 2 * i + 2 + h, h)

                with act.Fori(0, HEADS // 2 - 1) as i:
                    pair(i, False)
                pair(HEADS // 2 - 1, True)
                for t in range(t_n):
                    act.wait_ge(S("o_turned"), at(ph, "o_turned") + t + 1)
                    nc.scalar.activation(o_hi[:, :, t * P:(t + 1) * P],
                                         ps[:, TURN_BANKS[t_n][t], :].rearrange("p (a b) -> p a b", a=KB), ACT.Copy
                                         ).then_inc(S("o_hi"), 1)

            def project(ph):
                act.wait_ge(S("merged"), at(ph, "merged"))
                act.wait_ge(S("mods_ready"), MODS_READY[ph.layer, 1])

                def chunks(i):
                    for s in range(2):
                        unit_done(ph.unit + 2 * i + s, s)
                        for c, (a, b) in enumerate(((0, LAT), (LAT, TOK))[:1 + (ph.tiles > LT)]):
                            last = nc.scalar.activation(
                                acc[:, bass.ds(2 * i + s, 1), a:b].rearrange("p a b -> p (a b)"), span(2 * s, b - a, a),
                                ACT.Copy, scale=mods_v[:, ph.layer, 2, bass.ds(2 * i + s, 1), c])
                        last.then_inc(S("projected"), 1)

                with act.Fori(0, KD // 4) as i:
                    chunks(i)
                load_residual(ph)
                with act.Fori(KD // 4, KD // 2) as i:
                    chunks(i)

            def residual(ph):
                last = ph.layer == DEPTH - 1 and ph.part == 1
                act.wait_ge(S("unit_done"), ph.unit)
                for n in range(2):
                    act.dma_start(ln_rows[:, n, :], norm_rows[ph.layer, ph.part, n, :].partition_broadcast(P)
                                  ).then_inc(S("rows_loaded"), 16)
                norm_steps(ph, last=last)
                act.wait_ge(S("stored"), at(ph, "stored") + 16 * ph.tiles)

            def gate_up(ph):
                with act.Fori(0, PARTS[ph.part][1] // 2) as i:
                    for c in range(2):
                        unit_done(ph.unit + 4 * i + 2 * c, 0)
                        act.wait_ge(S("hidden"), at(ph, "hidden") + 2 * i + c - 1)
                        nc.scalar.activation(silu_g[:, c, 0:ph.width], span(4 * c, ph.width), ACT.Silu
                                             ).then_inc(S("silu"), 1)
                        unit_done(ph.unit + 4 * i + 2 * c + 1, 1)

            def down(ph):
                if ph.part == len(PARTS) - 1:
                    load_residual(ph)
                end = ph.unit + KD == n_units
                with act.Fori(0, KD // 2 - end) as i:
                    for s in range(2):
                        unit_done(ph.unit + 2 * i + s, s)

            for ph in phases:
                {"first_norm": first_norm, "modulate": modulate, "fourier_in": fourier_in, "tokens_a": tokens,
                 "tokens_b": tokens, "fourier": fourier, "merge": merge, "attention": attention, "project": project,
                 "residual": residual, "gate_up": gate_up, "down": down}[ph.kind](ph)

        @block.vector
        def _(dve):
            prime(dve, ("branch_read", "merged", "hidden", "summed", "piece_lo", "o_norm", "added", "pt_dve", "inverse",
                        "ada_used"))
            def ada_three(kind, n):
                for s in range(ADA_SLOTS):
                    dve.wait_ge(ada_ready[s], 16 * (n - ADA_FIRST // ADA_SLOTS) + 16)
                    u = ADA_SLOTS * n + s
                    for c, done in enumerate(("ada_half", "ada_used")):
                        if c == 0:
                            dve.wait_ge(S("ada_used"), PRIME + u - ADA_FIRST)
                        else:
                            dve.wait_ge(S("ada_half"), u + 1 - ADA_FIRST)
                        nc.vector.scalar_tensor_tensor(
                            ada_unused[kind][:, :], ada_raw[kind][:, s, :], 1.0, ada_cond[kind][:, c, :],
                            ALU.mult, ALU.mult, accum_out=mods[:, bass.ds(u, 1), c]).then_inc(S(done), 1)

            def ada_biased(first, end, products):
                nc.vector.tensor_tensor(mods[:, first:end, :], products,
                                        ada_bias[:, first:end].unsqueeze(2).broadcast_to([P, end - first, 2]), ALU.add
                                        ).then_inc(S("mods_ready"), 1)

            def ada_window(kind, layer):
                first, end = ADA_WINDOWS[kind, layer]
                n = list(ADA_WINDOWS).index((kind, layer)) + 1
                dve.wait_ge(S("cond_loaded"), 32 + 16 * n)
                with dve.Fori(first // ADA_SLOTS, end // ADA_SLOTS) as i:
                    ada_three(kind, i)
                dve.wait_ge(S("ada_used"), PRIME - ADA_FIRST + end)
                ada_biased(first, end, mods[:, first:end, :])
                dve.wait_ge(S("mods_ready"), n + 1)

            def chain(name, start):
                count = [start]

                def step(instruction):
                    count[0] += 1
                    instruction.then_inc(S(name), 1)
                    dve.wait_ge(S(name), count[0])
                return step

            def inverse_root(step, n, ph):
                dve.wait_ge(S("std_ready"), at(ph, "std_ready") + 1)
                step(nc.vector.reciprocal(inv_s[:, 0:n], std_s[:, 0:n]))
                step(nc.vector.tensor_tensor(tmp_s[:, 0:n], inv_s[:, 0:n], inv_s[:, 0:n], ALU.mult))
                step(nc.vector.tensor_tensor(tmp_s[:, 0:n], tmp_s[:, 0:n], var_s[:, 0:n], ALU.mult))
                step(nc.vector.tensor_scalar(tmp_s[:, 0:n], tmp_s[:, 0:n], -0.5, 1.5, ALU.mult, ALU.add))
                step(nc.vector.tensor_tensor(inv_s[:, 0:n], inv_s[:, 0:n], tmp_s[:, 0:n], ALU.mult))

            def norms(ph, first=False, last=False):
                step = chain("norm_step", at(ph, "norm_step"))
                seen = dict.fromkeys(("std", "root"), 0)

                def mean(second, t):
                    nc.vector.tensor_scalar(neg_mean[:, second, t:t + 1], sum_s[:, second, t:t + 1], -1.0 / D, None,
                                            ALU.mult).then_inc(S("mean_ready"), 1)

                for name, g in NORM_ORDER:
                    if not in_norms(name, g, ph, first, last):
                        continue
                    tiles = (2 * g, 2 * g + 1)
                    second = int(name.endswith("2"))
                    a = ALLT * second + 2 * g
                    if name == "add":
                        for t in tiles:
                            dve.wait_ge(S("turned"), at(ph, "turned") + t + 1)
                            nc.vector.scalar_tensor_tensor(xr[:, t, :], xr[:, t, :], ALPHA,
                                                           span(2 * ((t + 2) % 4), D),
                                                           ALU.mult, ALU.add, accum_out=sum_s[:, 0, t:t + 1]
                                                           ).then_inc(S("added"), 1)
                        for t in tiles:
                            dve.wait_ge(S("added"), at(ph, "added") + t + 1)
                            mean(0, t)
                    elif name.startswith("var"):
                        squares = 2 * steps_before(("square2" if second else "square", g), ph, first, last)
                        dve.wait_ge(S("squared"), at(ph, "squared") + squares)
                        nc.vector.tensor_scalar(var_s[:, a:a + 2], square_s[:, second, 2 * g:2 * g + 2], 1.0 / D, EPS,
                                                ALU.mult, ALU.add).then_inc(S("var_ready"), 1)
                    elif name.startswith("root"):
                        seen["std"] += 1
                        seen["root"] += 1
                        dve.wait_ge(S("std_ready"), at(ph, "std_ready") + seen["std"])
                        inv, tmp = inv_s[:, a:a + 2], tmp_s[:, a:a + 2]
                        step(nc.vector.reciprocal(inv, std_s[:, a:a + 2]))
                        step(nc.vector.tensor_tensor(tmp, inv, inv, ALU.mult))
                        step(nc.vector.tensor_tensor(tmp, tmp, var_s[:, a:a + 2], ALU.mult))
                        step(nc.vector.tensor_scalar(tmp, tmp, -0.5, 1.5, ALU.mult, ALU.add))
                        last_step = nc.vector.tensor_tensor(inv, inv, tmp, ALU.mult)
                        if second:
                            step(last_step)
                            last_step = nc.vector.tensor_tensor(shift_s[:, 2 * g:2 * g + 2],
                                                                neg_mean[:, 1, 2 * g:2 * g + 2], inv, ALU.mult)
                        last_step.then_inc(S("root_ready"), 1)
                    elif name == "affine" and first:
                        for t in tiles:
                            nc.vector.tensor_reduce(sum_s[:, 1, t:t + 1], xr[:, t, :], axis=AX.X, op=ALU.add
                                                    ).then_inc(S("summed_x"), 1)
                        for t in tiles:
                            dve.wait_ge(S("summed_x"), at(ph, "summed_x") + t + 1)
                            mean(1, t)
                    elif name == "affine":
                        if g == 0:
                            dve.wait_ge(S("rows_loaded"), at(ph, "rows_loaded") + 32)
                        dve.wait_ge(S("root_ready"), at(ph, "root_ready") + seen["root"])
                        for t in tiles:
                            nc.vector.scalar_tensor_tensor(xr[:, t, :], xr[:, t, :], neg_mean[:, 0, t:t + 1],
                                                           ln_rows[:, 0, :], ALU.add, ALU.mult
                                                           ).then_inc(S("scaled"), 1)
                        for t in tiles:
                            dve.wait_ge(S("scaled"), at(ph, "scaled") + t + 1)
                            nc.vector.scalar_tensor_tensor(xr[:, t, :], xr[:, t, :], inv_s[:, t:t + 1],
                                                           ln_rows[:, 1, :], ALU.mult, ALU.add,
                                                           accum_out=sum_s[:, 1, t:t + 1]).then_inc(S("shifted"), 1)
                        if not last:
                            for t in tiles:
                                dve.wait_ge(S("shifted"), at(ph, "shifted") + t + 1)
                                mean(1, t)

            def first_norm(ph):
                dve.wait_ge(S("loaded"), 16 * ALLT)
                norms(ph, first=True)
                dve.wait_ge(S("consts"), 16 * 5)
                bias_v = ada_bias[:, :].rearrange("p (l s k) -> p l s k", l=DEPTH, s=6)
                for s in (1, 4):
                    nc.vector.tensor_scalar(bias_v[:, :, s, :], bias_v[:, :, s, :], 1.0, None, ALU.add
                                            ).then_inc(S("bias_raised"), 1)
                dve.wait_ge(S("bias_raised"), 2)
                dve.wait_ge(S("columns"), 1)
                ada_biased(0, ADA_FIRST, ps[:, 7, 0:2 * ADA_FIRST].rearrange("p (a c) -> p a c", c=2))
                dve.wait_ge(S("mods_ready"), 1)

            def modulate(ph):
                w = ph.width
                for k in range(KD):
                    dve.wait_ge(S("h_val"), at(ph, "h_val") + k + 1)
                    nc.vector.tensor_copy(h_hi[:, k, 0:w], h_tmp[:, k % 4, 0:w]).then_inc(S("h_hi"), 1)
                    if k % 2 == 0:
                        dve.wait_ge(S("h_hi"), at(ph, "h_hi") + k + 1)
                        nc.vector.tensor_tensor(h_lo[:, k, 0:w], h_tmp[:, k % 4, 0:w], h_hi[:, k, 0:w].bitcast(F32),
                                                ALU.subtract).then_inc(S("h_lo"), 1)

            def heads_view(ph, a, t):
                n = NH_A if t < ph.tiles else KV_A
                return a[:, (NH_A - n) * HD:].rearrange("p (h d) -> p h d", d=HD), n

            def tokens_a(ph):
                step = chain("rope_step", at(ph, "rope_step"))
                sums = var_s[:, :].rearrange("p (t h) -> p t h", t=ALLT)
                step(nc.vector.memset(var_s[:, :], 1.0))
                for n, (g, scale) in enumerate(((0, QSCALE), (1, QSCALE), (2, 1.0), (3, 1.0))):
                    last = nc.vector.scalar_tensor_tensor(
                        rope_g[:, n, :, :], rope[:, n % 2, :, :], scale,
                        gain[:, ph.layer, g, :].unsqueeze(1).broadcast_to([P, ALLT, HD]), ALU.mult, ALU.mult)
                step(last)
                dve.wait_ge(S("evacuated"), at(ph, "evacuated") + ph.tiles + ALLT)

                for t in range(ALLT):
                    x, n = heads_view(ph, tok_a[:, t, :], t)
                    sq, _ = heads_view(ph, rope_t[t % 2][:, :], t)
                    step(nc.vector.tensor_tensor(sq, x, x, ALU.mult))
                    step(nc.vector.tensor_reduce(sums[:, t, NH_A - n:], sq, axis=AX.X, op=ALU.add))
                step(nc.vector.tensor_scalar(var_s[:, :], var_s[:, :], 1.0 / HD, EPS, ALU.mult, ALU.add))
                nc.vector.tensor_copy(tmp_s[:, :], var_s[:, :]).then_inc(S("var_ready"), 1)

            def rotate(ph):
                step = chain("rope_step", at(ph, "rope_step") - ROTATE_STEPS)
                invs = inv_s[:, :].rearrange("p (t h) -> p t h", t=ALLT)
                inverse_root(step, ALLT * NH_A, ph)
                for t in range(ALLT):
                    x, n = heads_view(ph, tok_a[:, t, :], t)
                    kept, turned = heads_view(ph, rope_t[0][:, :], t)[0], heads_view(ph, rope_t[1][:, :], t)[0]
                    step(nc.vector.tensor_tensor(x, x, invs[:, t, NH_A - n:].unsqueeze(2).broadcast_to([P, n, HD]),
                                                 ALU.mult))
                    parts = ((0, n - KV_A, 0), (n - KV_A, n, 2)) if n > KV_A else ((0, n, 2),)
                    for a, b, g in parts:
                        nc.vector.tensor_tensor(kept[:, a:b, :], x[:, a:b, :],
                                                rope_g[:, g, t, :].unsqueeze(1).broadcast_to([P, b - a, HD]), ALU.mult)
                    for a, b, g in parts:
                        for quarter in range(2):
                            def of(v, q):
                                return v.rearrange("p h (a q d) -> p h a q d", a=2, q=2)[:, :, :, q, :]
                            sin = rope_g[:, g + 1, t, :].rearrange("p (a q d) -> p a q d", a=2, q=2)[:, :, quarter, :]
                            last = nc.vector.tensor_tensor(of(turned[:, a:b, :], quarter), of(x[:, a:b, :], 1 - quarter),
                                                           sin.unsqueeze(1).broadcast_to([P, b - a, 2, HD // 4]), ALU.mult)
                    step(last)
                    step(nc.vector.tensor_tensor(x, kept, turned, ALU.add))

            def fourier(ph):
                for g in range(KB):
                    dve.wait_ge(S("o_hi"), at(ph, "o_hi") + g + 1)
                    nc.vector.tensor_tensor(o_lo[:, g, 0:ph.width], span(2 * g, ph.width),
                                            o_hi[:, g, 0:ph.width].bitcast(F32), ALU.subtract).then_inc(S("o_lo"), 1)
                rotate(ph)

            def merge(ph):
                w = ph.width
                with dve.Fori(0, 2) as i:
                    for half in range(2):
                        for j in range(2):
                            c = 2 * half + j
                            chunk = acc[:, bass.ds(4 * i + c, 1), 0:w].rearrange("p a b -> p (a b)")
                            dve.wait_ge(S("unit_done"), ph.unit + 6 * i + 3 * half + 3)
                            dve.wait_ge(S("gated"), at(ph, "gated") + 4 * i + c + 1)
                            if ph.part == 2:
                                nc.vector.tensor_tensor(chunk, gate[:, c, 0:w], span(4 + 2 * j, w), ALU.mult
                                                        ).then_inc(S("merged"), 1)
                            else:
                                nc.vector.tensor_tensor(gate[:, c, 0:w], gate[:, c, 0:w], span(4 + 2 * j, w), ALU.mult
                                                        ).then_inc(S("branch_read"), 1)
                                dve.wait_ge(S("branch_read"), at(ph, "branch_read") + 4 * i + c + 1)
                                nc.vector.tensor_tensor(chunk, chunk, gate[:, c, 0:w], ALU.add
                                                        ).then_inc(S("merged"), 1)
                            if ph.part == 1:
                                y = at(ph, "y_split") + 8 * i + 2 * c
                                hi = y_hi[:, bass.ds(4 * i + c, 1), 0:w].rearrange("p a b -> p (a b)")
                                lo = y_lo[:, bass.ds(4 * i + c, 1), 0:w].rearrange("p a b -> p (a b)")
                                dve.wait_ge(S("merged"), at(ph, "merged") + 4 * i + c + 1)
                                nc.vector.tensor_scalar(hi, chunk, 1.0, None, ALU.mult).then_inc(S("y_split"), 1)
                                dve.wait_ge(S("y_split"), y + 1)
                                nc.vector.tensor_tensor(lo, chunk, hi.bitcast(F32), ALU.subtract
                                                        ).then_inc(S("y_split"), 1)

            def piece(ph, h, s, r, bank=7):
                what, a, b = PIECES[r]
                dve.wait_ge(S("piece_hi"), at(ph, "piece_hi") + ROUNDS[ph.tiles] * h + r + 1)
                if what == "q":
                    rows, dst, hi = slice(HD, P), q_st[s], q_st[s]
                else:
                    rows, dst, hi = slice(0, P), k_ll[s], k_hh[s]
                nc.vector.tensor_tensor(dst[rows, a:b], ps[rows, bank, 0:b - a], hi[rows, a:b].bitcast(F32),
                                        ALU.subtract).then_inc(S("piece_lo"), 1)

            def tokens_b(ph):
                for r in range(ROUNDS[ph.tiles]):
                    piece(after(ph), 0, 0, r, START_BANKS[1][r])
                dve.wait_ge(S("unit_done"), ph.unit + 12)
                for t in range(1, ALLT, 2):
                    nc.vector.tensor_copy(v_b[:, t, :], ps[:, VALUE_BANKS[ph.tiles][t], :]
                                          ).then_inc(S("values_out"), 1)

            def attention(ph):
                t_n, rounds, branch = ph.tiles, ROUNDS[ph.tiles], ph.part

                def maximum(i, m):
                    n, s, t, h = 2 * t_n * i + m, m % 2, m % t_n, m // t_n
                    keys = P * len(key_tiles(branch, t))
                    dve.wait_ge(S("scored"), at(ph, "scored") + n + 1)
                    dve.wait_ge(S("probs"), at(ph, "probs") + n - 1)
                    if branch == 1 and t < LT:
                        if t == 0:
                            dve.wait_ge(bias_ready[h % 2], 16 * (HEADS // 2) * ph.layer + 16 * (i + h // 2) + 16)
                        nc.vector.tensor_reduce(max_c[:, s:s + 1], span(2 * s, CTX), axis=AX.X, op=ALU.max
                                                ).then_inc(S("max_part"), 1)
                        lat = span(2 * s, keys - CTX, CTX)
                        nc.vector.tensor_tensor_reduce(out=lat, in0=lat,
                                                       in1=bias_sb[h % 2][:, BIAS_AT[t]:BIAS_AT[t] + BIAS_KEYS[t]],
                                                       scale=1.0, scalar=3 * MASKED, op0=ALU.add, op1=ALU.max,
                                                       accum_out=max_a[:, s:s + 1]).then_inc(S("max_bias"), 1)
                        dve.wait_ge(S("max_part"), at(ph, "max_part") + n + 1)
                        dve.wait_ge(S("max_bias"), LT * (HEADS * ph.layer + 2 * i + h) + t + 1)
                        nc.vector.tensor_scalar(neg_max[:, s:s + 1], max_a[:, s:s + 1], max_c[:, s:s + 1], -1.0,
                                                ALU.max, ALU.mult).then_inc(S("max_ready"), 1)
                    else:
                        nc.vector.tensor_reduce(max_c[:, s:s + 1], span(2 * s, keys), axis=AX.X, op=ALU.max
                                                ).then_inc(S("max_part"), 1)
                        dve.wait_ge(S("max_part"), at(ph, "max_part") + n + 1)
                        nc.vector.tensor_scalar(neg_max[:, s:s + 1], max_c[:, s:s + 1], -1.0, None, ALU.mult
                                                ).then_inc(S("max_ready"), 1)

                def copy_turned(i, m):
                    keys = P * len(key_tiles(branch, m % t_n))
                    if keys > 512:
                        dve.wait_ge(S("turned_p"), at(ph, "turned_p") + 2 * t_n * i + m + 1)
                        nc.vector.tensor_scalar(pt_sb[branch][m % 2][:, 512:keys], ps[:, 5, 0:keys - 512], 1.0, None,
                                                ALU.mult).then_inc(S("pt_dve"), 1)

                def invert(i, m):
                    dve.wait_ge(S("probs"), at(ph, "probs") + 2 * t_n * i + m + 1)
                    nc.vector.reciprocal(row_inv[:, m % 4:m % 4 + 1], row_sum[:, m % 2:m % 2 + 1]
                                         ).then_inc(S("inverse"), 1)

                def normalise(i, m):
                    n, t, h = 2 * t_n * i + m, m % t_n, m // t_n
                    dve.wait_ge(S("inverse"), at(ph, "inverse") + n + 1)
                    dve.wait_ge(S("attended"), at(ph, "attended") + n + 1)
                    col = HD * (i // 2) if branch == 0 else HD * h
                    nc.vector.tensor_scalar(o_tok[:, t, bass.ds((2 * i + h) * HD, HD)], ps[:, 6, bass.ds(col, HD)],
                                            row_inv[:, m % 4:m % 4 + 1], None, ALU.mult).then_inc(S("o_norm"), 1)

                if branch == 0:
                    for r in range(rounds):
                        piece(ph, 0, 0, r, START_BANKS[0][r])
                maximum(0, 0)
                maximum(0, 1)
                for r in range(2):
                    piece(ph, 1, 1, r)
                copy_turned(0, 0)
                invert(0, 0)
                maximum(0, 2)

                def pair(i, last):
                    for m in range(1, 2 * t_n + 1 - last):
                        for h, r in pieces_at(t_n, m, last):
                            piece(ph, 2 * i + h, h % 2, r)
                        copy_turned(i, m)
                        invert(i, m)
                        if m + 2 < 2 * t_n or not last:
                            maximum(i, m + 2)
                        normalise(i, m - 1)
                    if last:
                        normalise(i, 2 * t_n - 1)

                with dve.Fori(0, HEADS // 2 - 1) as i:
                    pair(i, False)
                pair(HEADS // 2 - 1, True)
                for t in range(t_n):
                    dve.wait_ge(S("o_hi"), at(ph, "o_hi") + t + 1)
                    nc.vector.tensor_tensor(o_lo[:, :, t * P:(t + 1) * P],
                                            ps[:, TURN_BANKS[t_n][t], :].rearrange("p (a b) -> p a b", a=KB),
                                            o_hi[:, :, t * P:(t + 1) * P].bitcast(F32), ALU.subtract
                                            ).then_inc(S("o_lo"), 1)

            def residual(ph):
                dve.wait_ge(S("loaded"), at(ph, "loaded"))
                norms(ph, last=ph.layer == DEPTH - 1 and ph.part == 1)

            def gate_up(ph):
                w = ph.width
                beside = ada_beside(ph)
                if beside == ADA_UNITS:
                    dve.wait_ge(S("cond_loaded"), 32 + 16 * (len(ADA_WINDOWS) + 1))
                with dve.Fori(0, PARTS[ph.part][1] // 2) as i:
                    for c in range(2):
                        if c and beside:
                            ada_three("gate_up", beside // ADA_SLOTS + i)
                        n = 2 * i + c
                        hi = hid_hi[:, bass.ds(n, 1), 0:w].rearrange("p a b -> p (a b)")
                        lo = hid_lo[:, bass.ds(n, 1), 0:w].rearrange("p a b -> p (a b)")
                        dve.wait_ge(S("unit_done"), ph.unit + 4 * i + 2 * c + 2)
                        dve.wait_ge(S("silu"), at(ph, "silu") + n + 1)
                        nc.vector.tensor_tensor(hid[:, c, 0:w], silu_g[:, c, 0:w], span(4 * c + 2, w), ALU.mult
                                                ).then_inc(S("hidden"), 1)
                        dve.wait_ge(S("hidden"), at(ph, "hidden") + n + 1)
                        nc.vector.tensor_scalar(hi, hid[:, c, 0:w], 1.0, None, ALU.mult).then_inc(S("hidden_hi"), 1)
                        dve.wait_ge(S("hidden_hi"), at(ph, "hidden_hi") + n + 1)
                        nc.vector.tensor_tensor(lo, hid[:, c, 0:w], hi.bitcast(F32), ALU.subtract
                                                ).then_inc(S("hidden_lo"), 1)

            def down(ph):
                beside = ada_beside(ph)
                with dve.Fori(0, KD // 2) as i:
                    for s in range(2):
                        if s and beside:
                            ada_three("gate_up", beside // ADA_SLOTS + i)
                        n = 2 * i + s
                        dve.wait_ge(S("unit_done"), ph.unit + n + 1)
                        for c, (a, b) in enumerate(((0, LAT), (LAT, TOK))[:1 + (ph.tiles > LT)]):
                            dst = acc[:, bass.ds(n, 1), a:b].rearrange("p a b -> p (a b)")
                            g2 = mods_v[:, ph.layer, 5, bass.ds(n, 1), c]
                            if ph.part == 0:
                                last = nc.vector.tensor_scalar(dst, span(2 * s, b - a, a), g2, None, ALU.mult)
                            else:
                                last = nc.vector.scalar_tensor_tensor(dst, span(2 * s, b - a, a), g2, dst, ALU.mult,
                                                                      ALU.add)
                        last.then_inc(S("summed"), 1)
                if beside and (ph.kind, ph.part) == list(ADA_BESIDE)[-1]:
                    end = DEPTH * ADA_UNITS
                    dve.wait_ge(S("ada_used"), PRIME + end - ADA_FIRST)
                    ada_biased(ADA_UNITS, end, mods[:, ADA_UNITS:end, :])
                    dve.wait_ge(S("mods_ready"), MODS_READY[1, 0])

            for ph in phases:
                if (ph.kind, ph.layer) in ADA_WINDOWS:
                    ada_window(ph.kind, ph.layer)
                work = {"first_norm": first_norm, "modulate": modulate, "tokens_a": tokens_a, "tokens_b": tokens_b,
                        "fourier": fourier, "merge": merge, "attention": attention, "residual": residual, "gate_up": gate_up,
                        "down": down}.get(ph.kind)
                if work:
                    work(ph)

        @block.tensor
        def _(pe):
            prime(pe, ("piece", "attended", "scored", "turned_p"))

            def first_norm(ph):
                pe.wait_ge(S("cond_ready"), 1)
                for k in range(KD):
                    pe.wait_ge(first_ready[k % 2], 16 * (k // 2) + 16)
                    for b in range(-(-ADA_FIRST // 4)):
                        w = min(4, ADA_FIRST - 4 * b) * P
                        last = nc.tensor.matmul(ps[0:2, b, 0:w], cond_act[:, k, :],
                                                first_raw[:, k % 2, 512 * b:512 * b + w],
                                                start=k == 0, stop=k == KD - 1)
                    last.then_inc(S("first_used"), 1)
                pe.wait_ge(S("consts"), 16 * 5)
                for j in range(ADA_FIRST):
                    pe.wait_ge(S("rows_out"), j // 4 + 1)
                    last = nc.tensor.transpose(ps[:, 7, 2 * j:2 * j + 2], first_rows[:, j * P:(j + 1) * P],
                                               ident[0:2, 0:2])
                last.then_inc(S("columns"), 1)

            def columns(ph, u, s, bank, x_hi, x_lo, k_tiles, first=0, ready=lambda k: None):
                pe.wait_ge(S("lo_made"), u + 1)
                wide = ph.width > LAT
                for k in range(k_tiles):
                    ready(k)
                    for name in TERMS:
                        w, x = term(name, s, x_hi, x_lo)
                        tile = w[:, s, (first + k) * P:(first + k + 1) * P]
                        start = k == 0 and name == TERMS[0]
                        stop = k == k_tiles - 1 and name == TERMS[-1]
                        last = nc.tensor.matmul(bank(0), tile, x[:, k, 0:LAT], start=start, stop=stop)
                        if wide:
                            last = nc.tensor.matmul(bank(1), tile, x[:, k, LAT:TOK], start=start, stop=stop)
                return last

            def fixed(b):
                return lambda half: ps[:, b, :] if half == 0 else ps[:, b + 1, 0:CTX]

            def modulate(ph):
                pe.wait_ge(S("consts"), 16 * 5)
                if ph.unit:
                    pe.wait_ge(S("added"), at(ph, "added"))
                else:
                    pe.wait_ge(S("mods_ready"), 1)
                for t in range(ph.tiles):
                    pe.wait_ge(S("normed"), at(ph, "normed") - ph.tiles + t + 1)
                    for k in range(4):
                        last = nc.tensor.transpose(span(2 * k, P, t * P), xn[:, t, k * P:(k + 1) * P], ident[:, :])
                        if t == ph.tiles - 1:
                            last.then_inc(S("turned"), 1)
                for k in range(4, KD):
                    pe.wait_ge(S("h_val"), at(ph, "h_val") + k - 3)
                    for t in range(ph.tiles):
                        last = nc.tensor.transpose(span(2 * (k % 4), P, t * P), xn[:, t, k * P:(k + 1) * P], ident[:, :])
                    last.then_inc(S("turned"), 1)

            def h_ready(ph):
                def ready(k):
                    name = ("h_lo", "h_lo_pool")[k % 2]
                    pe.wait_ge(S(name), at(ph, name) - KD // 2 + k // 2 + 1)
                return ready

            def fourier_in(ph):
                pe.wait_ge(S("h_val"), at(ph, "h_val") - 3)
                with pe.Fori(0, KB // 2) as i:
                    for s in range(2):
                        def bank(half):
                            b = ps[:, bass.ds(4 * i + 2 * s + half, 1), :].rearrange("p a b -> p (a b)")
                            return b if half == 0 else b[:, 0:CTX]
                        columns(ph, ph.unit + 2 * i + s, s, bank, h_hi, h_lo, KD, ready=h_ready(ph)
                                ).then_inc(S("unit_done"), 1)

            def piece(ph, h, s, r, bank=7):
                what, a, b = PIECES[r]
                rounds = ROUNDS[ph.tiles]
                if r == 0:
                    pe.wait_ge(S("staged"), at(ph, "staged") + 2 * h + 2)
                if bank == 7:
                    pe.wait_ge(S("piece_lo"), at(ph, "piece_lo") + rounds * h + r)
                elif ph.part == 1 and r >= 2:
                    pe.wait_ge(S("piece_lo"), at(ph, "piece_lo") + r - 1)
                src = stage_q[ph.part][s] if what == "q" else stage_k[ph.part][s]
                for t in range(a // P, b // P):
                    last = nc.tensor.transpose(ps[:, bank, t * P - a:(t + 1) * P - a],
                                               src[:, t, :, :].rearrange("p a b -> p (a b)"), ident[:, :])
                last.then_inc(S("piece"), 1)

            def tokens(ph):
                if ph.kind == "tokens_a":
                    groups = ((4, ph.tiles, 512), (2, ALLT, 256))
                else:
                    groups = ((4, ph.tiles, 512), (4, ALLT, 512), (4, ALLT, 512))
                    pe.wait_ge(S("gated"), at(ph, "gated"))
                banks, u, first = token_banks(ph), ph.unit, 0
                for units, tiles, cols in groups:
                    per = UNIT * P // cols
                    for j in range(units):
                        s = j % 2
                        if ph.kind == "tokens_b" and u == ph.unit + 8:
                            for r in early_pieces(ph, j):
                                piece(after(ph), 0, 0, r, START_BANKS[1][r])
                        pe.wait_ge(S("lo_made"), u + j + 1)
                        for kk in range(per):
                            k = j * per + kk
                            for t in range(tiles):
                                n = first + t
                                if k == 0 and banks[n] in banks[:n]:
                                    held = max(m for m in range(n) if banks[m] == banks[n])
                                    pe.wait_ge(S("evacuated"), at(ph, "evacuated") + held + 1)
                                elif k == 0 and ph.kind == "tokens_a":
                                    pe.wait_ge(S("evacuated"), at(ph, "evacuated") - KB + banks[n] // 2 + 1)
                                elif k == 0 and banks[n] >= 4:
                                    pe.wait_ge(S("merged"), at(ph, "merged") - 1 + (banks[n] - 4) // 2)
                                for name in TERMS:
                                    w, x = {"lo_hi": (w_lo, h_hi), "hi_lo": (w_hi, h_lo), "hi_hi": (w_hi, h_hi)}[name]
                                    last = nc.tensor.matmul(ps[:, banks[n], 0:cols], x[:, k, t * P:(t + 1) * P],
                                                            w[:, s, kk * cols:(kk + 1) * cols],
                                                            start=k == 0 and name == TERMS[0],
                                                            stop=k == KD - 1 and name == TERMS[-1])
                        last.then_inc(S("unit_done"), 1)
                    u += units
                    first += tiles

            def fourier(ph):
                for n in range(2 * ph.tiles):
                    g, t = divmod(n, ph.tiles)
                    pe.wait_ge(S("evacuated"), at(ph, "evacuated") + n - 7)
                    for j in range(2):
                        last = nc.tensor.matmul(ps[:, z_bank(ph, n), 256 * j:256 * j + 256],
                                                u_cols[:, 2 * g + j, t * P:(t + 1) * P], dft_c[:, :],
                                                start=True, stop=True)
                    last.then_inc(S("z_made"), 1)
                pe.wait_ge(S("dft_loaded"), 32 * (ph.layer + 1))
                for g in range(KB):
                    held = [n for n in range(2 * ph.tiles) if z_bank(ph, n) in (2 * g, 2 * g + 1)]
                    pe.wait_ge(S("evacuated"), at(ph, "evacuated") + max(max(held) + 1, (g // 2 + 1) * ph.tiles))
                    for t in range(LT):
                        for part in range(2):
                            last = nc.tensor.matmul(ps[:, 2 * g, :], z_sb[:, t, g, part * P:(part + 1) * P],
                                                    dft_l[:, t, part, :], start=t + part == 0,
                                                    stop=t + part == LT)
                    for t in range(ph.tiles - LT):
                        for part in range(2):
                            last = nc.tensor.matmul(ps[:, 2 * g + 1, 0:CTX],
                                                    z_sb[:, LT + t, g, part * P:(part + 1) * P],
                                                    dft_x[:, t, part, :], start=t + part == 0, stop=t + part == CT)
                    last.then_inc(S("mixed"), 1)

            def merge(ph):
                read = "merged" if ph.part == 2 else "branch_read"
                with pe.Fori(0, 2) as i:
                    for half in range(2):
                        for j in range(3):
                            n = 3 * half + j
                            u = ph.unit + 6 * i + n
                            if j < 2:
                                if ph.part == 2:
                                    pe.wait_ge(S("o_lo"), at(ph, "o_lo") - KB + 1 + j)
                                elif j:
                                    pe.wait_ge(S("o_lo"), at(ph, "o_lo") - 1)
                                pe.wait_ge(S("gated"), at(ph, "gated") + 4 * i + 2 * half + j - 1)
                                columns(ph, u, n % 2, fixed(2 * j), h_hi, h_lo, KD).then_inc(S("unit_done"), 1)
                            else:
                                pe.wait_ge(S("o_lo"), at(ph, "o_lo"))
                                for c in range(2):
                                    pe.wait_ge(S(read), at(ph, read) + 4 * i + 2 * half + c - 1)
                                    last = columns(ph, u, n % 2, fixed(4 + 2 * c), o_hi, o_lo, KB, first=KB * c)
                                last.then_inc(S("unit_done"), 1)

            def attention(ph):
                t_n, rounds, branch = ph.tiles, ROUNDS[ph.tiles], ph.part

                def score(i, m):
                    n, s, t, h = 2 * t_n * i + m, m % 2, m % t_n, m // t_n
                    if t == 0:
                        pe.wait_ge(S("piece_lo"), at(ph, "piece_lo") + rounds * (2 * i + h + 1))
                    pe.wait_ge(S("probs"), at(ph, "probs") + n - 1)
                    for part, kk in enumerate((k_hh[h % 2], k_ll[h % 2])):
                        for a, b, at_col in key_runs(branch, t):
                            last = nc.tensor.matmul(span(2 * s, b - a, at_col) if at_col < 512 else
                                                    ps[:, 2 * s + 1, at_col - 512:at_col - 512 + b - a],
                                                    q_st[h % 2][:, t * P:(t + 1) * P], kk[:, a:b],
                                                    start=part == 0 and at_col in (0, 512), stop=part == 1,
                                                    skip_group_check=True)
                    last.then_inc(S("scored"), 1)

                def turn(i, m):
                    n, t, h = 2 * t_n * i + m, m % t_n, m // t_n
                    pe.wait_ge(S("probs"), at(ph, "probs") + n + 1)
                    pe.wait_ge(S("pt_act"), at(ph, "pt_act") + n)
                    pe.wait_ge(S("pt_dve"), at(ph, "pt_dve") + wide_tiles(branch, t_n) * (2 * i + h)
                               + wide_tiles(branch, t))
                    for kk in range(len(key_tiles(branch, t))):
                        last = nc.tensor.transpose(ps[:, 4 + kk // 4, (kk % 4) * P:(kk % 4 + 1) * P],
                                                   p_sb[branch][m % 2][:, kk * P:(kk + 1) * P], ident[:, :])
                    last.then_inc(S("turned_p"), 1)

                def attend(i, m):
                    n, t, h = 2 * t_n * i + m, m % t_n, m // t_n
                    pe.wait_ge(S("pt_act"), at(ph, "pt_act") + n + 1)
                    pe.wait_ge(S("pt_dve"), at(ph, "pt_dve") + wide_tiles(branch, t_n) * (2 * i + h)
                               + wide_tiles(branch, t + 1))
                    pe.wait_ge(S("o_norm"), at(ph, "o_norm") + n)
                    tiles = key_tiles(branch, t)
                    for kk, kt in enumerate(tiles):
                        values = v_a[:, kt, :] if branch == 0 else v_b[:, kt, bass.ds(2 * HD * i, 2 * HD)]
                        last = nc.tensor.matmul(ps[:, 6, 0:2 * HD], pt_sb[branch][m % 2][:, kk * P:(kk + 1) * P],
                                                values, start=kk == 0, stop=kk == len(tiles) - 1)
                    last.then_inc(S("attended"), 1)

                def values_out(banks):
                    for t in (VALUE_BANKS[t_n].index(b) for b in banks if b in VALUE_BANKS[t_n]):
                        name = ("evacuated", "values_out")[t % 2]
                        pe.wait_ge(S(name), at(ph, name) - ALLT // 2 + t // 2 + 1)

                if branch == 0:
                    pe.wait_ge(S("gated"), at(ph, "gated"))
                    for r in range(rounds):
                        piece(ph, 0, 0, r, START_BANKS[0][r])
                else:
                    values_out((0, 1))
                score(0, 0)
                if branch == 1:
                    values_out((2, 3))
                score(0, 1)
                if branch == 0:
                    pe.wait_ge(S("merged"), at(ph, "merged"))
                else:
                    values_out((4, 5, 6, 7))
                for r in range(2):
                    piece(ph, 1, 1, r)
                turn(0, 0)
                score(0, 2)

                def pair(i, last):
                    for m in range(1, 2 * t_n + 1 - last):
                        for h, r in pieces_at(t_n, m, last):
                            piece(ph, 2 * i + h, h % 2, r)
                        turn(i, m)
                        if m + 2 < 2 * t_n or not last:
                            score(i, m + 2)
                        attend(i, m - 1)
                    if last:
                        attend(i, 2 * t_n - 1)

                with pe.Fori(0, HEADS // 2 - 1) as i:
                    pair(i, False)
                pair(HEADS // 2 - 1, True)
                for t in range(t_n):
                    pe.wait_ge(S("o_norm"), at(ph, "o_norm") + (HEADS - 1) * t_n + t + 1)
                    for c in range(KB):
                        last = nc.tensor.transpose(ps[:, TURN_BANKS[t_n][t], c * P:(c + 1) * P], o_tok[:, t, c * P:(c + 1) * P],
                                                   ident[:, :])
                    last.then_inc(S("o_turned"), 1)

            def project(ph):
                def ready(k):
                    pe.wait_ge(S("y_split"), at(ph, "y_split") - 2 * KD + 2 * k + 2)
                pe.wait_ge(S("gated"), at(ph, "gated"))
                with pe.Fori(0, KD // 2) as i:
                    for s in range(2):
                        pe.wait_ge(S("projected"), at(ph, "projected") + 2 * i + s - 1)
                        columns(ph, ph.unit + 2 * i + s, s, fixed(2 * s), y_hi, y_lo, KD, ready=ready
                                ).then_inc(S("unit_done"), 1)

            def residual(ph):
                chunks = ("projected", "summed")[ph.part]
                for t in range(ph.tiles):
                    if t >= 4:
                        pe.wait_ge(S("added"), at(ph, "added") + t - 3)
                    bank = 2 * ((t + 2) % 4)
                    for j in range(KD):
                        if t == 0:
                            pe.wait_ge(S(chunks), at(ph, chunks) - KD + j + 1)
                        last = nc.tensor.transpose(span(bank, P, j * P) if j < 4 else
                                                   ps[:, bank + 1, (j - 4) * P:(j - 3) * P],
                                                   acc[:, j, t * P:(t + 1) * P], ident[:, :])
                    last.then_inc(S("turned"), 1)

            def gate_up(ph):
                pe.wait_ge(S("h_val"), at(ph, "h_val") - 3)
                pe.wait_ge(S("summed"), at(ph, "summed") - 1)
                with pe.Fori(0, PARTS[ph.part][1] // 2) as i:
                    for c in range(2):
                        u = ph.unit + 4 * i + 2 * c
                        pe.wait_ge(S("silu"), at(ph, "silu") + 2 * i + c - 1)
                        columns(ph, u, 0, fixed(4 * c), h_hi, h_lo, KD, ready=h_ready(ph)).then_inc(S("unit_done"), 1)
                        pe.wait_ge(S("summed"), at(ph, "summed"))
                        pe.wait_ge(S("hidden"), at(ph, "hidden") + 2 * i + c - 1)
                        columns(ph, u + 1, 1, fixed(4 * c + 2), h_hi, h_lo, KD).then_inc(S("unit_done"), 1)

            def down(ph):
                chunks = PARTS[ph.part][1]

                def ready(k):
                    pe.wait_ge(S("hidden_lo"), at(ph, "hidden_lo") - chunks + k + 1)

                with pe.Fori(0, KD // 2) as i:
                    for s in range(2):
                        pe.wait_ge(S("summed"), at(ph, "summed") + 2 * i + s - 1)
                        columns(ph, ph.unit + 2 * i + s, s, fixed(2 * s), hid_hi, hid_lo, chunks,
                                ready=ready).then_inc(S("unit_done"), 1)

            for ph in phases:
                work = {"first_norm": first_norm, "modulate": modulate, "fourier_in": fourier_in, "tokens_a": tokens, "tokens_b": tokens,
                        "fourier": fourier, "merge": merge, "attention": attention, "project": project,
                        "residual": residual, "gate_up": gate_up, "down": down}.get(ph.kind)
                if work:
                    work(ph)


MODS_READY = {(0, 0): 1, (0, 1): 2, (1, 0): 4, (1, 1): 4}


def in_norms(name, g, ph, first, last):
    if g >= ph.tiles // 2:
        return False
    of_second = name in ("square2", "var2", "std2", "root2", "apply")
    return name == "affine" or (of_second and not last) or (not of_second and not first)


def steps_before(step, ph, first, last):
    kind = step[0].rstrip("2")
    steps = [s for s in NORM_ORDER if s[0].rstrip("2") == kind and in_norms(*s, ph, first, last)]
    return steps.index(step) + 1


START_BANKS = ((0, 1, 2, 3), (5, 6, 5, 6))
TURN_BANKS = {ALLT: (4, 5, 7, 3, 2, 6), LT: (4, 5, 7, 6)}


def token_banks(ph):
    if ph.kind == "tokens_a":
        return [n % 8 for n in range(ph.tiles + ALLT)]
    keys = [(ph.tiles + n) % 8 for n in range(ALLT)]
    return list(range(ph.tiles)) + keys + list(VALUE_BANKS[ph.tiles])


VALUE_BANKS = {ALLT: (4, 0, 1, 2, 3, 7), LT: (2, 3, 0, 1, 4, 7)}


def early_pieces(ph, unit):
    return {2: (0, 1), 3: tuple(range(2, ROUNDS[ph.tiles]))}.get(unit, ())


def z_bank(ph, n):
    return (n + ph.tiles + ALLT) % 8


PIECES = (("q", 0, LAT), ("k", 0, LAT), ("k", LAT, TOK), ("q", LAT, TOK))


def pieces_at(t_n, m, last):
    if t_n == ALLT:
        steps = {1: ((1, 2),), 2: ((1, 3),), 5: ((2, 0),), 6: ((2, 1),), 7: ((2, 2),), 8: ((2, 3),), 11: ((3, 0),),
                 12: ((3, 1),)}
    else:
        steps = {1: ((1, 2),), 3: ((2, 0),), 4: ((2, 1),), 5: ((2, 2),), 7: ((3, 0),), 8: ((3, 1),)}
    return [(h, r) for h, r in steps.get(m, ()) if h == 1 or not last]


def key_tiles(branch, t):
    ctx = [LT + c for c in range(CT)]
    if t >= LT:
        return ctx
    if branch == 0:
        return ctx + list(range(LT))
    return ctx + [FIRST_BLOCK[t] + b for b in range(BIAS_KEYS[t] // P)]


def wide_tiles(branch, n):
    return sum(P * len(key_tiles(branch, t)) > 512 for t in range(n))


def key_runs(branch, t):
    runs = [(LAT, TOK, 0)]
    lat = key_tiles(branch, t)[CT:]
    if lat:
        a = lat[0] * P
        runs.append((a, a + 256, 256))
        if len(lat) > 2:
            runs.append((a + 256, a + len(lat) * P, 512))
    return runs


def block_order(a):
    return a.reshape(ROWS, GRID_W // WIN, WIN, *a.shape[1:]).swapaxes(0, 1).reshape(a.shape)


def feature_units(w):
    k, n = w.shape
    return w.reshape(k // P, P, n // P, P).transpose(2, 1, 0, 3).reshape(n // P, P, k)


def token_units(w, cols):
    per = UNIT * P // cols
    return w.reshape(KD // per, per, P, cols).transpose(0, 2, 1, 3).reshape(KD // per, P, per * cols)


def lay_stream(w_in, w_branch, w_out, w_gu, w_down):
    units = []
    for l in range(DEPTH):
        w = w_in[l]
        qa, ka, va, qb, kb, vb, uc, gz = np.split(w, np.cumsum((512, 128, 128, 512, 512, 512, 512)), axis=1)

        def merge(b):
            gates = feature_units(gz[:, b * D:(b + 1) * D])
            wb = w_branch[l, b].reshape(KB, P, KD // 2, 2, P).transpose(2, 1, 3, 0, 4).reshape(KD // 2, P, UNIT * P)
            for j in range(KD // 2):
                units.extend((gates[2 * j][None], gates[2 * j + 1][None], wb[j][None]))

        units.append(feature_units(uc))
        units.append(token_units(qa, 512))
        units.append(token_units(np.concatenate([ka, va], 1), 256))
        merge(2)
        merge(0)
        for m in (qb, kb, vb):
            units.append(token_units(m, 512))
        merge(1)
        units.append(feature_units(w_out[l]))
        gate, up = feature_units(w_gu[l][:, :D_FF]), feature_units(w_gu[l][:, D_FF:])
        for first, count in PARTS:
            for c in range(first, first + count):
                units.extend((gate[c][None], up[c][None]))
            rows = w_down[l][first * P:(first + count) * P]
            part = np.zeros((KD, P, UNIT * P), w_down.dtype)
            part[:, :, :count * P] = feature_units(rows)
            units.append(part)
    return np.concatenate(units, 0)


def lay_bias(rpb):
    out = np.full((DEPTH, HEADS, P, BIAS_W), MASKED, rpb.dtype)
    row, col = np.divmod(np.arange(P), WIN)
    for block in range(GRID_W // WIN):
        if block == 2:
            continue
        q_col = block * WIN + col
        start = np.clip(q_col - WIN // 2, 0, GRID_W - WIN)
        for b in range(BIAS_KEYS[block] // P):
            k_col = (FIRST_BLOCK[block] + b) * WIN + col
            dr = row[None, :] - row[:, None] + ROWS - 1
            dc = k_col[None, :] - q_col[:, None] + WIN - 1
            seen = (k_col[None, :] >= start[:, None]) & (k_col[None, :] < start[:, None] + WIN)
            at = BIAS_AT[block] + b * P
            got = rpb[:, :, dr, np.clip(dc, 0, 2 * WIN - 2)]
            out[:, :, :, at:at + P] = np.where(seen, got, out[:, :, :, at:at + P])
    return out


def shape_tables():
    ident = np.eye(P, dtype=np.float32)
    quarter = HD // 4
    freqs = (10000.0 ** (-np.arange(quarter, dtype=np.float32) / np.float32(quarter))).astype(np.float32)
    pos = block_order(np.arange(LAT))
    rope = np.zeros((2, TOK, HD), np.float32)
    rope[0] = 1.0
    for half, where in enumerate((pos // GRID_W, pos % GRID_W)):
        ang = (where.astype(np.float32)[:, None] * freqs).astype(np.float32)
        for q in range(2):
            sl = slice(half * 2 * quarter + q * quarter, half * 2 * quarter + (q + 1) * quarter)
            rope[0, :LAT, sl] = np.cos(ang)
            rope[1, :LAT, sl] = (-1.0, 1.0)[q] * np.sin(ang)
    rope = rope.reshape(2, ALLT, P, HD).transpose(2, 0, 1, 3)

    def angles(n, i, j):
        return 2.0 * np.pi * ((i[:, None] * j[None, :]) % n) / n

    ch = angles(P, np.arange(P), np.arange(P))
    dft_ch = np.concatenate([np.cos(ch), np.sin(ch)], 1)
    lat = angles(LAT, pos, pos)
    dft_lat = np.stack([np.cos(lat), -np.sin(lat)], 1) / np.sqrt(LAT * P)
    ctx = angles(CTX, np.arange(CTX), np.arange(CTX))
    dft_ctx = np.stack([np.cos(ctx), -np.sin(ctx)], 1) / np.sqrt(CTX * P)
    dft_lat = dft_lat.reshape(LT, P, 2, LAT).transpose(1, 0, 2, 3)
    dft_ctx = dft_ctx.reshape(CT, P, 2, CTX).transpose(1, 0, 2, 3)
    return [np.ascontiguousarray(a, np.float32) for a in (ident, rope, dft_ch, dft_lat, dft_ctx)]


def lay_out(x, c, ctx, c_ctx, w_ada, b_ada, w_in, q_norm, k_norm, rpb, w_branch, w_out, ln1_g, ln1_b, w_gu, w_down,
            ln2_g, ln2_b):
    swap = np.arange(HD).reshape(2, 2, HD // 4)[:, ::-1].reshape(HD)
    ident, rope, dft_ch, dft_lat, dft_ctx = shape_tables()
    return {
        "x_in": block_order(x[0]),
        "ctx_in": ctx[0],
        "cond": np.stack([c[0], c_ctx], 0),
        "cond_cols": np.stack([c[0].reshape(KD, P).T, c_ctx.reshape(KD, P).T], 2),
        "w_first": w_ada[0][:, :ADA_FIRST * P].reshape(KD, P, ADA_FIRST * P),
        "w_ada": w_ada.swapaxes(1, 2).reshape(DEPTH * ADA_UNITS, P, D),
        "b_ada": b_ada.reshape(DEPTH * ADA_UNITS, P).T,
        "stream": lay_stream(w_in, w_branch, w_out, w_gu, w_down),
        "qk_gain": np.stack([q_norm, q_norm[:, swap], k_norm, k_norm[:, swap]], 1).reshape(-1),
        "norm_rows": np.stack([np.stack([ln1_g, ln1_b], 1), np.stack([ln2_g, ln2_b], 1)], 1),
        "bias": lay_bias(rpb),
        "ident_in": ident, "rope_in": rope, "dft_ch": dft_ch, "dft_lat": dft_lat, "dft_ctx": dft_ctx,
    }


def program(nc, arrays):
    args = [nc.dram_tensor(f"in_{n}", a.shape, mybir.dt.from_np(a.dtype), kind="ExternalInput").ap()
            for n, a in arrays.items()]
    scratch = nc.dram_tensor("scratch", (2 * DEPTH, ALLT, P, D), F32, kind="Internal").ap()
    out = nc.dram_tensor("out_x", (LT, P, D), F32, kind="ExternalOutput").ap()
    cond_scratch = nc.dram_tensor("cond_scratch", (2, D), F32, kind="Internal").ap()
    build(nc, *args, scratch, cond_scratch, out)


def kernel(**inputs):
    import concourse.bacc as bacc
    from concourse.bass_utils import run_bass_kernel_spmd

    arrays = {n: np.ascontiguousarray(a) for n, a in
              lay_out(**{n: np.asarray(a) for n, a in inputs.items()}).items()}
    nc = bacc.Bacc("TRN2", target_bir_lowering=False, num_devices=1)
    program(nc, arrays)
    r = run_bass_kernel_spmd(nc, [{f"in_{n}": a for n, a in arrays.items()}], core_ids=[0])
    got = r.results[0]["out_x"].reshape(GRID_W // WIN, ROWS, WIN, D)
    return np.ascontiguousarray(got.swapaxes(0, 1).reshape(1, LAT, D))
```

```python
import concourse.bass as bass
from concourse import mybir
import numpy as np

F32 = mybir.dt.float32
F32R = mybir.dt.float32r
ALU = mybir.AluOpType
ACT = mybir.ActivationFunctionType
AX = mybir.AxisListType

DEPTH = 2
D = 1024
LAT, CTX = 512, 256
P = 128
KD = D // P
LT, CT = LAT // P, CTX // P
ALLT = LT + CT
TOK = LAT + CTX
HD = 64
HEADS = 8
KV_A = 2
GRID_W, ROWS, WIN = 64, 8, 16
BRANCH = 512
KB = BRANCH // P
D_FF = 2816
FF = D_FF // P
UNIT = 8
PARTS = ((0, 8), (8, 8), (16, 6))
ALPHA = (2.0 * DEPTH) ** 0.25
EPS = 1e-6
QSCALE = HD ** -0.5
MASKED = -1e30
BIAS_AT = (0, 256, 640, 1024)
BIAS_KEYS = (256, 384, 384, 256)
FIRST_BLOCK = (0, 0, 1, 2)
BIAS_W = 1280
FREQ_L, FREQ_X = LAT // 2 + 2 * ROWS, CTX // 2 + 1
ADA_UNITS = 6 * D // P
ADA_SLOTS = 3
ROUNDS = {ALLT: 4, LT: 3}
PRIME = 8
ADA_WINDOWS = {("fourier_in", 0): (18, 42), ("tokens_b", 0): (42, 48)}
ADA_BESIDE = {("gate_up", 0): 48, ("down", 0): 60, ("gate_up", 1): 72, ("down", 1): 84}
ADA_PER_PAIR = 6
ROTATE_STEPS = 4 + 3 * ALLT
ADA_FIRST = 18
NORM_ORDER = (("add", 0), ("square", 0), ("add", 1), ("var", 0), ("std", 0), ("square", 1), ("add", 2), ("square", 2),
              ("root", 0), ("var", 1), ("std", 1), ("affine", 0), ("square2", 0), ("root", 1), ("var", 2), ("std", 2),
              ("affine", 1), ("var2", 0), ("std2", 0), ("square2", 1), ("root", 2), ("affine", 2), ("root2", 0),
              ("apply", 0), ("var2", 1), ("std2", 1), ("square2", 2), ("root2", 1), ("apply", 1), ("var2", 2),
              ("std2", 2), ("root2", 2), ("apply", 2))


class Phase:

    def __init__(self, kind, layer, tiles, unit, part=None):
        self.kind, self.layer, self.tiles, self.unit, self.part = kind, layer, tiles, unit, part
        self.width = tiles * P
        self.pairs = 0
        self.at = {}


def plan():
    phases, unit = [], 0

    def add(kind, layer, tiles, units=0, part=None):
        nonlocal unit
        phases.append(Phase(kind, layer, tiles, unit, part))
        unit += units

    add("first_norm", 0, ALLT)
    for layer in range(DEPTH):
        t = ALLT if layer < DEPTH - 1 else LT
        add("modulate", layer, ALLT, part=0)
        add("fourier_in", layer, t, 4)
        add("tokens_a", layer, t, 6)
        add("fourier", layer, t)
        add("merge", layer, t, 12, part=2)
        add("attention", layer, t, part=0)
        add("merge", layer, t, 12, part=0)
        add("tokens_b", layer, t, 12)
        add("attention", layer, t, part=1)
        add("merge", layer, t, 12, part=1)
        add("project", layer, t, 8)
        add("residual", layer, t, part=0)
        add("modulate", layer, t, part=1)
        for part, (_, chunks) in enumerate(PARTS):
            add("gate_up", layer, t, 2 * chunks, part=part)
            phases[-1].pairs = chunks
            add("down", layer, t, 8, part=part)
            phases[-1].pairs = 4
        add("residual", layer, t, part=1)
    counts = {}
    for ph in phases:
        ph.at = dict(counts)
        for name, n in increments(ph).items():
            counts[name] = counts.get(name, 0) + n
    return phases, unit


def ada_beside(ph):
    return ADA_BESIDE.get((ph.kind, ph.part)) if ph.layer == 0 and ph.kind in ("gate_up", "down") else None


def increments(ph):
    t, k = ph.tiles, ph.kind
    if k in ("first_norm", "residual"):
        first = k == "first_norm"
        last = ph.layer == DEPTH - 1 and ph.part == 1
        norms = 1 if first or last else 2
        groups = norms * t // 2
        got = {"mean_ready": norms * t, "squared": norms * t, "var_ready": groups, "std_ready": groups,
               "root_ready": groups, "normed": 0 if last else t // 2, "normed_odd": 0 if last else t // 2}
        got["norm_step"] = groups // norms * ((not first) * 3 + (not last) * 4)
        if first:
            return {**got, "loaded": 16 * t, "summed_x": t}
        return {**got, "turned": t, "added": t, "scaled": t // 2, "centred": t // 2,
                "scaled_odd": t // 2, "shifted": t, "stored": 16 * t, "rows_loaded": 32}
    if k == "modulate":
        return {"turned": KD, "h_val": KD, "h_hi": KD, "h_lo": KD // 2, "h_lo_pool": KD // 2}
    if k == "fourier_in":
        return {"evacuated": 4}
    if k == "tokens_a":
        return {"evacuated": t + ALLT, "rope_step": 7 + 5 * ALLT, "var_ready": 1}
    if k == "tokens_b":
        return {"evacuated": t + 2 * ALLT - ALLT // 2, "values_out": ALLT // 2}
    if k == "fourier":
        return {"z_made": 2 * t, "evacuated": 2 * t, "mixed": KB, "odd_out": KB, "halves_made": KB,
                "mix_made": KB, "o_hi": KB, "o_lo": KB, "std_ready": 1}
    if k == "merge":
        return {"gated": KD, "branch_read": KD * (ph.part != 2), "merged": KD, "y_split": 2 * KD * (ph.part == 1)}
    if k == "attention":
        n, r = HEADS * t, pieces_before(ph, HEADS)
        return {"staged": staged_before(ph, HEADS), "piece": r, "piece_hi": r, "piece_lo": r, "scored": n,
                "max_part": n, "max_ready": n, "probs": n, "turned_p": n, "pt_act": n, "pt_dve": HEADS * wide_tiles(ph.part, t, t),
                "attended": n,
                "inverse": n, "o_norm": n, "o_turned": t, "o_hi": t, "o_lo": t}
    if k == "project":
        return {"projected": KD, "loaded": 16 * t}
    if k == "gate_up":
        n = PARTS[ph.part][1]
        return {"silu": n, "hidden": n, "hidden_hi": n, "hidden_lo": n}
    if k == "down":
        return {"summed": KD, "loaded": 16 * t * (ph.part == len(PARTS) - 1)}
    raise ValueError(k)


def build(nc, x_in, ctx_in, cond, cond_cols, w_first, w_ada, b_ada, stream, qk_gain, norm_rows, bias, ident_in,
          rope_in, dft_ch, dft_lat, dft_ctx, scratch, cond_scratch, out):
    phases, n_units = plan()

    base = (nc.sbuf_base + 63) // 64 * 64
    end = nc.sbuf_top
    cursor = [base]

    def sb(name, shape, dtype=F32, at=None):
        size = (2 if dtype == mybir.dt.bfloat16 else 4) * int(np.prod(shape[1:]))
        if at is None:
            at = cursor[0]
            cursor[0] += (size + 63) // 64 * 64
        assert at + size <= end, (name, at + size - end)
        return nc.alloc_sbuf_tensor_at(name, shape, dtype, offset=at)

    K = 1024
    raw = sb("raw", [P, 2, UNIT * P])
    w_hi = sb("w_hi", [P, 2, UNIT * P], F32R)
    w_lo = sb("w_lo", [P, 2, UNIT * P], F32R)
    h_hi = sb("h_hi", [P, KD, TOK], F32R)
    h_lo = sb("h_lo", [P, KD, TOK], F32R)
    acc = sb("acc", [P, KD, TOK])
    ident = sb("ident", [P, P])
    rope = sb("rope", [P, 2, ALLT, HD])
    gain = sb("gain", [P, DEPTH, 4, HD])
    mods = sb("mods", [P, DEPTH * ADA_UNITS, 2])
    mods_v = mods[:, :, :].rearrange("p (l s k) c -> p l s k c", l=DEPTH, s=6)
    ada_bias = sb("ada_bias", [P, DEPTH * ADA_UNITS])
    sum_s = sb("sum_s", [P, 2, ALLT])
    neg_mean = sb("neg_mean", [P, 2, ALLT])
    square_s = sb("square_s", [P, 2, ALLT])
    NH_A = HEADS + KV_A
    var_s = sb("var_s", [P, ALLT * NH_A])
    std_s = sb("std_s", [P, ALLT * NH_A])
    inv_s = sb("inv_s", [P, ALLT * NH_A])
    tmp_s = sb("tmp_s", [P, ALLT * NH_A])
    shift_s = sb("shift_s", [P, ALLT])
    max_c = sb("max_c", [P, 2])
    max_a = sb("max_a", [P, 2])
    neg_max = sb("neg_max", [P, 2])
    row_sum = sb("row_sum", [P, 4])
    row_inv = sb("row_inv", [P, 4])
    dft_c = sb("dft_c", [P, 2 * P])
    warm = sb("warm", [P, 1])
    R = cursor[0]

    o_hi = sb("o_hi", [P, KB, TOK], F32R, at=R)
    o_lo = sb("o_lo", [P, KB, TOK], F32R, at=R + 12 * K)
    u_cols = sb("u_cols", [P, KB, TOK], at=R)
    q_st = [sb(f"q_st{s}", [P, TOK], F32R, at=R + 3 * K * s) for s in range(2)]
    k_hh = sb("k_hh", [P, 2, TOK], F32R, at=R + 6 * K)
    k_ll = sb("k_ll", [P, 2, TOK], F32R, at=R + 12 * K)
    stage_q = [[sb(f"stage_q{b}{s}", [P, ALLT, 2, HD], at=R + (54, 18)[b] * K + 3 * K * s) for s in range(2)]
               for b in range(2)]
    stage_k = [[sb(f"stage_k{b}{s}", [P, ALLT, 2, HD], at=R + (88, 82)[b] * K + 3 * K * s) for s in range(2)]
               for b in range(2)]
    tok_a = sb("tok_a", [P, ALLT, NH_A * HD], at=R + 24 * K)
    v_a = sb("v_a", [P, ALLT, KV_A * HD], at=R + 39 * K)
    z_sb = sb("z_sb", [P, ALLT, KB, 2 * P], at=R + 42 * K)
    dft_l = sb("dft_l", [P, LT, 2, FREQ_L], at=R + 66 * K)
    dft_x = sb("dft_x", [P, CT, 2, FREQ_X], at=R + 75 * K)
    rope_g = sb("rope_g", [P, 4, ALLT, HD], at=R + 91 * K)
    mix = sb("mix", [P, 2, TOK], at=R + 78 * K)
    odd = sb("odd", [P, 2, FREQ_L + FREQ_X], at=R + 98 * K)
    rope_t = [sb(f"rope_t{s}", [P, NH_A * HD], at=R + 86 * K + 2560 * s) for s in range(2)]
    tok_b = sb("tok_b", [P, ALLT, 2, BRANCH], at=R + 24 * K)
    v_b = sb("v_b", [P, ALLT, BRANCH], at=R + 48 * K)
    o_tok = sb("o_tok", [P, ALLT, BRANCH], at=R + 60 * K)
    keys_n = (TOK, CTX + max(BIAS_KEYS))
    p_sb = [[sb(f"p_sb{b}{s}", [P, keys_n[b]], at=R + (42, 72)[b] * K + 4 * keys_n[b] * s) for s in range(2)]
            for b in range(2)]
    pt_sb = [[sb(f"pt_sb{b}{s}", [P, keys_n[b]], at=R + (48, 77)[b] * K + 4 * keys_n[b] * s) for s in range(2)]
             for b in range(2)]
    bias_sb = [sb(f"bias_sb{s}", [P, BIAS_W], at=R + 88 * K + 4 * BIAS_W * s) for s in range(2)]
    gate = sb("gate", [P, 4, TOK], at=R + 72 * K)
    y_hi = sb("y_hi", [P, KD, TOK], F32R, at=R + 24 * K)
    y_lo = sb("y_lo", [P, KD, TOK], F32R, at=R + 48 * K)
    ln_rows = sb("ln_rows", [P, 2, D], at=R + 60 * K)
    unused = sb("unused", [P, D], at=R + 68 * K)
    xn = sb("xn", [P, ALLT, D], at=R + 24 * K)
    h_tmp = sb("h_tmp", [P, 4, TOK], at=R + 48 * K)
    xr = sb("xr", [P, ALLT, D], at=R + 72 * K)
    hid_hi = sb("hid_hi", [P, 8, TOK], F32R, at=R + 8 * K)
    hid_lo = sb("hid_lo", [P, 8, TOK], F32R, at=R + 32 * K)
    silu_g = sb("silu_g", [P, 2, TOK], at=R + 56 * K)
    hid = sb("hid", [P, 2, TOK], at=R + 62 * K)
    ada_at = {"fourier_in": 42, "tokens_b": 60, "gate_up": 68}
    ada_raw = {k: sb(f"ada_raw_{k}", [P, ADA_SLOTS, D], at=R + a * K) for k, a in ada_at.items()}
    ada_cond = {k: sb(f"ada_cond_{k}", [P, 2, D], at=R + (a + 12) * K) for k, a in ada_at.items()}
    ada_unused = {k: sb(f"ada_unused_{k}", [P, D], mybir.dt.bfloat16, at=R + (a + 20) * K) for k, a in ada_at.items()}

    first_raw = sb("first_raw", [P, 2, ADA_FIRST * P], at=R)
    first_rows = sb("first_rows", [2, ADA_FIRST * P], at=R + 48 * K)
    cond_act = sb("cond_act", [P, KD, 2], at=R + 58 * K)
    cond_rows = sb("cond_rows", [2, D], at=R + 60 * K)

    ps = nc.alloc_psum_tensor("ps", [P, 8, 512], F32)

    def span(bank, width, start=0):
        n = (start + width + 511) // 512
        return ps[:, bank:bank + n, :].rearrange("p a b -> p (a b)")[:, start:start + width]

    sems = {}

    def S(name):
        if name not in sems:
            sems[name] = nc.alloc_semaphore(name)
        return sems[name]

    raw_ready = [nc.alloc_semaphore(f"raw_ready{s}") for s in range(2)]
    ada_ready = [nc.alloc_semaphore(f"ada_ready{s}") for s in range(ADA_SLOTS)]
    first_ready = [nc.alloc_semaphore(f"first_ready{s}") for s in range(2)]
    bias_ready = [nc.alloc_semaphore(f"bias_ready{s}") for s in range(2)]

    def after(ph):
        return phases[phases.index(ph) + 1]

    PRIMED = ("gated", "branch_read", "merged", "projected", "silu", "hidden", "summed", "probs", "piece", "piece_lo",
              "o_norm", "attended", "scored", "turned_p", "added", "evacuated", "pt_act", "pt_dve", "inverse", "ada_used")

    def at(ph, name):
        return ph.at.get(name, 0) + (PRIME if name in PRIMED else 0)

    def prime(eng, names):
        for name in names:
            eng.sem_inc(S(name), PRIME)

    TERMS = ("lo_hi", "hi_lo", "hi_hi")

    def term(name, slot, x_hi, x_lo):
        return {"lo_hi": (w_lo, x_hi), "hi_lo": (w_hi, x_lo), "hi_hi": (w_hi, x_hi)}[name]

    block = nc.Block()
    with block:

        @block.sync
        def _(sp):
            def load_pair(i):
                for s in range(2):
                    sp.wait_ge(S("lo_made"), 2 * i + s - 1)
                    sp.dma_start(raw[:, s, :], stream[bass.ds(2 * i + s, 1), :, :]
                                 .rearrange("a p c -> p (a c)")).then_inc(raw_ready[s], 16)

            def load_ada(kind, first, count):
                for n in range(count):
                    sp.wait_ge(S("ada_used"), PRIME - ADA_FIRST + first + n - ADA_SLOTS + 1)
                    sp.dma_start(ada_raw[kind][:, n % ADA_SLOTS, :], w_ada[bass.ds(first + n, 1), :, :]
                                 .rearrange("a p c -> p (a c)")).then_inc(ada_ready[n % ADA_SLOTS], 16)

            def load_beside(ph, first, done):
                each = ph.pairs // 4
                with sp.Fori(0, 4) as i:
                    load_ada("gate_up", first + ADA_SLOTS * i, ADA_SLOTS)
                    for n in range(each):
                        load_pair(done // 2 + each * i + n)

            sp.dma_start(cond_act[:, :, :], cond_cols[:, :, :]).then_inc(S("cond_loaded"), 16)
            for k in range(KD):
                if k >= 2:
                    sp.wait_ge(S("first_used"), k - 1)
                sp.dma_start(first_raw[:, k % 2, :], w_first[k, :, :]).then_inc(first_ready[k % 2], 16)
            for s in range(2):
                sp.dma_start(raw[:, s, :], stream[s, :, :]).then_inc(raw_ready[s], 16)
            done = 2
            for ph in phases:
                beside = ada_beside(ph)
                if beside and beside != ADA_UNITS:
                    load_beside(ph, beside, done)
                    done += 2 * ph.pairs
                    continue
                if (ph.kind, ph.layer) not in ADA_WINDOWS and not beside:
                    continue
                with sp.Fori(done // 2, ph.unit // 2 + 2) as i:
                    load_pair(i)
                done = ph.unit + 4
                if ph.kind == "fourier_in":
                    sp.wait_ge(S("h_lo"), at(ph, "h_lo"))
                    sp.wait_ge(S("h_lo_pool"), at(ph, "h_lo_pool"))
                elif ph.kind == "tokens_b":
                    sp.wait_ge(S("merged"), at(ph, "merged"))
                else:
                    sp.wait_ge(S("turned"), at(ph, "turned"))
                    sp.wait_ge(S("stored"), at(ph, "stored"))
                sp.wait_ge(S("cond_stored"), 16)
                sp.dma_start(ada_cond[ph.kind][:, :, :].rearrange("p a b -> p (a b)"),
                             cond_scratch.rearrange("a b -> (a b)").partition_broadcast(P)
                             ).then_inc(S("cond_loaded"), 16)
                if beside:
                    load_beside(ph, beside, done)
                    done += 2 * ph.pairs
                    continue
                first, end = ADA_WINDOWS[ph.kind, ph.layer]
                pairs = (end - first) // ADA_PER_PAIR
                with sp.Fori(0, pairs) as i:
                    load_ada(ph.kind, first + ADA_PER_PAIR * i, ADA_PER_PAIR // 2)
                    load_pair(i + done // 2)
                    load_ada(ph.kind, first + ADA_PER_PAIR * i + ADA_PER_PAIR // 2, ADA_PER_PAIR // 2)
                done += 2 * pairs
            with sp.Fori(done // 2, n_units // 2) as i:
                load_pair(i)

        @block.gpsimd
        def _(pool):
            def lo_parts(first, end):
                with pool.Fori(first // 2, end // 2) as i:
                    for s in range(2):
                        pool.wait_ge(S("hi_made"), 2 * i + s + 1)
                        nc.gpsimd.tensor_tensor(w_lo[:, s, :], raw[:, s, :], w_hi[:, s, :].bitcast(F32),
                                                ALU.subtract).then_inc(S("lo_made"), 1)

            def centre(ph):
                pool.wait_ge(S("rows_loaded"), at(ph, "rows_loaded") + 32)
                for t in range(1, ph.tiles, 2):
                    pool.wait_ge(S("mean_ready"), at(ph, "mean_ready") + t + 1)
                    nc.gpsimd.tensor_tensor(xn[:, t, :], xr[:, t, :], neg_mean[:, 0, t:t + 1].broadcast_to([P, D]),
                                            ALU.add).then_inc(S("centred"), 1)
                    pool.wait_ge(S("centred"), at(ph, "centred") + t // 2 + 1)
                    nc.gpsimd.tensor_tensor(xn[:, t, :], xn[:, t, :], ln_rows[:, 0, :], ALU.mult
                                            ).then_inc(S("scaled_odd"), 1)

            def odd_rows(ph):
                for k in range(1, KD, 2):
                    pool.wait_ge(S("h_hi"), at(ph, "h_hi") + k + 1)
                    nc.gpsimd.tensor_tensor(h_lo[:, k, 0:ph.width], h_tmp[:, k % 4, 0:ph.width],
                                            h_hi[:, k, 0:ph.width].bitcast(F32), ALU.subtract
                                            ).then_inc(S("h_lo_pool"), 1)

            def stage_starts(ph):
                if ph.part == 0:
                    pool.wait_ge(S("rope_step"), at(ph, "rope_step"))
                else:
                    pool.wait_ge(S("evacuated"), at(ph, "evacuated") - ALLT // 2)

            def stage_keys(ph, s, src):
                nc.gpsimd.tensor_copy(stage_k[ph.part][s][:, :, :, :],
                                      src.unsqueeze(2).broadcast_to([P, ALLT, 2, HD])).then_inc(S("staged"), 1)

            def stage(ph, i, slots=(0, 1)):
                for s in slots:
                    h = 2 * i + s
                    q_slot = stage_q[ph.part][s][:, 0:ph.tiles, :, :]
                    if ph.part == 0:
                        if not (isinstance(h, int) and h < 2):
                            pool.wait_ge(S("piece"), at(ph, "piece") + pieces_before(ph, h - 1))
                        q_src = tok_a[:, 0:ph.tiles, bass.ds(h * HD, HD)]
                    else:
                        pool.wait_ge(S("piece"), at(ph, "piece") + ROUNDS[ph.tiles] * (h - 1))
                        q_src = tok_b[:, 0:ph.tiles, 0, bass.ds(h * HD, HD)]
                        stage_keys(ph, s, tok_b[:, :, 1, bass.ds(h * HD, HD)])
                    nc.gpsimd.tensor_copy(q_slot, q_src.unsqueeze(2).broadcast_to([P, ph.tiles, 2, HD])
                                          ).then_inc(S("staged"), 1)
                    if ph.part == 0 and isinstance(h, int) and h < 2:
                        stage_keys(ph, s, tok_a[:, :, (HEADS + s) * HD:(HEADS + s + 1) * HD])

            done = 0
            for ph in phases:
                if ph.kind not in ("attention", "modulate", "residual", "fourier"):
                    continue
                if ph.kind == "attention":
                    ahead = ph.unit - 2 * ph.part
                    lo_parts(done, ahead)
                    stage_starts(ph)
                    stage(ph, 0, (0,))
                    if ahead < ph.unit:
                        lo_parts(ahead, ph.unit)
                    stage(ph, 0, (1,))
                    lo_parts(ph.unit, ph.unit + 2)
                    with pool.Fori(1, HEADS // 2) as i:
                        stage(ph, i)
                    done = ph.unit + 2
                    continue
                end = min(ph.unit + 2, n_units)
                if end > done:
                    lo_parts(done, end)
                    done = end
                if ph.kind == "residual":
                    centre(ph)
                elif ph.kind == "fourier":
                    for g in range(KB):
                        pool.wait_ge(S("o_hi"), at(ph, "o_hi") + g + 1)
                        nc.gpsimd.tensor_tensor(o_lo[:, g, 0:ph.width], mix[:, g % 2, 0:ph.width],
                                                o_hi[:, g, 0:ph.width].bitcast(F32), ALU.subtract
                                                ).then_inc(S("o_lo"), 1)
                else:
                    odd_rows(ph)
        @block.scalar
        def _(act):
            prime(act, ("gated", "projected", "silu", "probs", "evacuated", "pt_act"))
            consts = [(ident[:, :], ident_in[:, :]), (rope[:, :, :, :], rope_in[:, :, :, :]),
                      (ada_bias[:, :], b_ada[:, :]), (dft_c[:, :], dft_ch[:, :])]
            act.dma_start(cond_rows[:, :], cond[:, :]).then_inc(S("cond_loaded"), 16)
            act.wait_ge(S("cond_loaded"), 32)
            nc.scalar.activation(cond_act[:, :, :], cond_act[:, :, :], ACT.Silu).then_inc(S("cond_ready"), 1)
            nc.scalar.activation(cond_rows[:, :], cond_rows[:, :], ACT.Silu).then_inc(S("cond_ready"), 1)
            act.wait_ge(S("cond_ready"), 2)
            act.dma_start(cond_scratch[:, :], cond_rows[:, :]).then_inc(S("cond_stored"), 16)

            def split(u, s):
                act.wait_ge(raw_ready[s], 8 * (u - s) + 16)
                nc.scalar.activation(w_hi[:, s, :], raw[:, s, :], ACT.Copy).then_inc(S("hi_made"), 1)

            warmed = [0]

            def unit_done(u, s, use=None):
                act.wait_ge(S("unit_done"), u + 1)
                if use:
                    use()
                split(u + 2, s)

            def load_table(function):
                act.wait_ge(S("consts"), 16 * 5)
                if warmed[0]:
                    act.wait_ge(S("warmed"), warmed[0])
                nc.scalar.activation(warm[:, :], ident[:, 0:1], function).then_inc(S("warmed"), 1)
                warmed[0] += 1

            def norm_steps(ph, first=False, last=False):
                seen = dict.fromkeys(("square", "std"), 0)
                for name, g in NORM_ORDER:
                    if not in_norms(name, g, ph, first, last):
                        continue
                    tiles = (2 * g, 2 * g + 1)
                    second = int(name.endswith("2"))
                    if name.startswith("square"):
                        for t in tiles:
                            if seen["square"]:
                                act.wait_ge(S("squared"), at(ph, "squared") + seen["square"])
                            seen["square"] += 1
                            act.wait_ge(S("mean_ready"), at(ph, "mean_ready") + seen["square"])
                            nc.scalar.activation(unused[:, :], xr[:, t, :], ACT.Square, bias=neg_mean[:, second, t:t + 1],
                                                 accum_out=square_s[:, second, t:t + 1]).then_inc(S("squared"), 1)
                    elif name.startswith("std"):
                        seen["std"] += 1
                        act.wait_ge(S("var_ready"), at(ph, "var_ready") + seen["std"])
                        a = ALLT * second + 2 * g
                        nc.scalar.activation(std_s[:, a:a + 2], var_s[:, a:a + 2], ACT.Sqrt).then_inc(S("std_ready"), 1)
                    elif name == "apply":
                        act.wait_ge(S("root_ready"), at(ph, "root_ready") + steps_before(("root2", g), ph, first, last))
                        t = tiles[0]
                        nc.scalar.activation(xn[:, t, :], xr[:, t, :], ACT.Identity,
                                             scale=inv_s[:, ALLT + t:ALLT + t + 1],
                                             bias=shift_s[:, t:t + 1]).then_inc(S("normed"), 1)
                    if not first and name == ("affine" if last else "square2"):
                        store(ph, tiles, last)

            def store(ph, tiles, last):
                for t in tiles:
                    act.wait_ge(S("shifted"), at(ph, "shifted") + t + 1)
                    dst = out[t, :, :] if last else scratch[2 * ph.layer + ph.part + 1, t, :, :]
                    act.dma_start(dst, xr[:, t, :]).then_inc(S("stored"), 16)

            def rows_of_input(t):
                return x_in[t * P:(t + 1) * P, :] if t < LT else ctx_in[(t - LT) * P:(t - LT + 1) * P, :]

            def load_residual(ph):
                which = 0 if ph.kind == "project" else 1
                for t in range(ph.tiles):
                    src = rows_of_input(t) if ph.layer + which == 0 else scratch[ph.layer * 2 + which, t, :, :]
                    act.dma_start(xr[:, t, :], src).then_inc(S("loaded"), 16)

            def first_norm(ph):
                for t in range(ALLT):
                    if t == ALLT // 2:
                        act.wait_ge(S("first_used"), 1)
                    act.dma_start(xr[:, t, :], rows_of_input(t)).then_inc(S("loaded"), 16)
                norm_steps(ph, first=True)
                for dst, src in consts:
                    act.dma_start(dst, src).then_inc(S("consts"), 16)
                act.dma_start(gain[:, :, :, :].rearrange("p a b c -> p (a b c)"),
                              qk_gain.partition_broadcast(P)).then_inc(S("consts"), 16)
                for s in range(2):
                    split(s, s)
                for b in range(-(-ADA_FIRST // 4)):
                    w = min(4, ADA_FIRST - 4 * b) * P
                    act.wait_ge(S("first_used"), KD)
                    nc.scalar.activation(first_rows[:, 512 * b:512 * b + w], ps[0:2, b, 0:w], ACT.Copy
                                         ).then_inc(S("rows_out"), 1)

            def modulate(ph):
                act.wait_ge(S("mods_ready"), MODS_READY[ph.layer, ph.part])
                if ph.unit:
                    act.wait_ge(S("unit_done"), ph.unit)
                m = 3 * ph.part
                for k in range(KD):
                    slot = 2 * (k % 4)
                    act.wait_ge(S("turned"), at(ph, "turned") + k + 1)
                    if k >= 4:
                        act.wait_ge(S("h_lo"), at(ph, "h_lo") + (k - 4) // 2 + 1)
                        if k % 2:
                            act.wait_ge(S("h_lo_pool"), at(ph, "h_lo_pool") + (k - 4) // 2 + 1)
                    for c, (a, b) in enumerate(((0, LAT), (LAT, TOK))[:1 + (ph.tiles > LT)]):
                        last = nc.scalar.activation(h_tmp[:, k % 4, a:b], span(slot, b - a, a), ACT.Identity,
                                                    scale=mods_v[:, ph.layer, m + 1, k, c:c + 1],
                                                    bias=mods_v[:, ph.layer, m, k, c:c + 1])
                    last.then_inc(S("h_val"), 1)
            def fourier_in(ph):
                with act.Fori(0, KB // 2) as i:
                    for s in range(2):
                        def use():
                            src = ps[:, bass.ds(4 * i + 2 * s, 2), :].rearrange("p a b -> p (a b)")[:, 0:ph.width]
                            dst = u_cols[:, bass.ds(2 * i + s, 1), 0:ph.width].rearrange("p a b -> p (a b)")
                            nc.scalar.activation(dst, src, ACT.Copy).then_inc(S("evacuated"), 1)
                        unit_done(ph.unit + 2 * i + s, s, use)

            def groups(ph):
                if ph.kind == "tokens_a":
                    return ((4, ph.tiles, 512, lambda t: ((tok_a[:, t, 0:512], 0, 512),), 1.0),
                            (2, ALLT, 256, lambda t: ((tok_a[:, t, 512:640], 0, 128), (v_a[:, t, :], 128, 256)), 1.0))
                return ((4, ph.tiles, 512, lambda t: ((tok_b[:, t, 0, :], 0, 512),), QSCALE),
                        (4, ALLT, 512, lambda t: ((tok_b[:, t, 1, :], 0, 512),), 1.0),
                        (4, ALLT, 512, lambda t: ((v_b[:, t, :], 0, 512),), 1.0))

            def piece(ph, h, s, r, bank=7):
                what, a, b = PIECES[r]
                act.wait_ge(S("piece"), at(ph, "piece") + piece_number(ph, h, r) + 1)
                dst = q_st[s][:, a:b] if what == "q" else k_hh[:, s, a:b]
                nc.scalar.activation(dst, ps[:, bank, 0:b - a], ACT.Copy).then_inc(S("piece_hi"), 1)

            def load_bias(ph, h, s):
                act.dma_start(bias_sb[s][:, :], bias[ph.layer, bass.ds(h, 1), :, :]
                              .rearrange("a p c -> p (a c)")).then_inc(bias_ready[s], 16)

            def tokens(ph):
                if ph.kind == "tokens_b":
                    for s in range(2):
                        load_bias(ph, s, s)
                if ph.kind == "tokens_a":
                    act.dma_start(dft_l[:, :, :, :], dft_lat[:, :, :, :]).then_inc(S("dft_loaded"), 16)
                    act.dma_start(dft_x[:, :, :, :], dft_ctx[:, :, :, :]).then_inc(S("dft_loaded"), 16)
                banks, u, n = token_banks(ph), ph.unit, 0
                for units, tiles, cols, dests, scale in groups(ph):
                    values = ph.kind == "tokens_b" and u == ph.unit + 8

                    def use():
                        for t in range(0, tiles, 1 + values):
                            for dst, a, b in dests(t):
                                last = nc.scalar.activation(dst, ps[:, banks[n + t], a:b], ACT.Copy, scale=scale)
                            last.then_inc(S("evacuated"), 1)

                    for j in range(units):
                        unit_done(u + j, j % 2, use if j == units - 1 else None)
                        if values:
                            for r in early_pieces(ph, j + 1):
                                piece(after(ph), 0, 0, r, START_BANKS[1][r])
                    u += units
                    n += tiles

            def fourier(ph):
                for n in range(2 * ph.tiles):
                    g, t = divmod(n, ph.tiles)
                    if n == 0 and ph.layer == 0:
                        act.wait_ge(S("ada_used"), PRIME - ADA_FIRST + ADA_WINDOWS["fourier_in", 0][1])
                    act.wait_ge(S("z_made"), at(ph, "z_made") + n + 1)
                    nc.scalar.activation(z_sb[:, t, 2 * g:2 * g + 2, :].rearrange("p a b -> p (a b)"),
                                         ps[:, z_bank(ph, n), :], ACT.Copy).then_inc(S("evacuated"), 1)
                act.wait_ge(S("var_ready"), at(ph, "var_ready"))
                nc.scalar.activation(std_s[:, :], var_s[:, :], ACT.Sqrt).then_inc(S("std_ready"), 1)
                w = FREQ_L + (FREQ_X if ph.tiles > LT else 0)
                for g in range(KB + 1):
                    if g < KB:
                        act.wait_ge(S("mixed"), at(ph, "mixed") + g + 1)
                        nc.scalar.activation(odd[:, g % 2, 0:w], ps[:, 2 * g + 1, 0:w], ACT.Copy
                                             ).then_inc(S("odd_out"), 1)
                    if g:
                        act.wait_ge(S("mix_made"), at(ph, "mix_made") + g)
                        nc.scalar.activation(o_hi[:, g - 1, 0:ph.width], mix[:, (g - 1) % 2, 0:ph.width], ACT.Copy
                                             ).then_inc(S("o_hi"), 1)

            def merge(ph):
                with act.Fori(0, 2) as i:
                    for half in range(2):
                        for j in range(3):
                            n = 3 * half + j

                            def use():
                                c = 2 * half + j
                                act.wait_ge(S("merged"), at(ph, "merged") + 4 * i + c - 3)
                                nc.scalar.activation(gate[:, c, 0:ph.width], span(2 * j, ph.width), ACT.Sigmoid
                                                     ).then_inc(S("gated"), 1)
                            unit_done(ph.unit + 6 * i + n, n % 2, use if j < 2 else None)

            def attention(ph):
                t_n, rounds, branch = ph.tiles, ROUNDS[ph.tiles], ph.part

                def probs(i, m):
                    n, s, t = 2 * t_n * i + m, m % 2, QUERY_ORDER[t_n][m % t_n]
                    keys = P * len(key_tiles(branch, t))
                    act.wait_ge(S("max_ready"), at(ph, "max_ready") + n + 1)
                    act.wait_ge(S("inverse"), at(ph, "inverse") + n - 1)
                    act.wait_ge(S("turned_p"), at(ph, "turned_p") + n - 1)
                    nc.scalar.activation(p_sb[branch][s][:, 0:keys], span(2 * s, keys), ACT.Exp,
                                         bias=neg_max[:, s:s + 1], accum_out=row_sum[:, s:s + 1]
                                         ).then_inc(S("probs"), 1)

                def copy_turned(i, m):
                    keys = min(512, P * len(key_tiles(branch, QUERY_ORDER[t_n][m % t_n])))
                    act.wait_ge(S("turned_p"), at(ph, "turned_p") + 2 * t_n * i + m + 1)
                    nc.scalar.activation(pt_sb[branch][m % 2][:, 0:keys], span(4, keys), ACT.Copy
                                         ).then_inc(S("pt_act"), 1)

                if branch == 0:
                    for r in range(rounds):
                        piece(ph, 0, 0, r, START_BANKS[0][r])
                load_table(ACT.Exp)
                probs(0, 0)
                probs(0, 1)
                for r in START_PIECES[branch][0]:
                    piece(ph, 1, 1, r)
                copy_turned(0, 0)
                for r in START_PIECES[branch][1][:rounds - 2]:
                    piece(ph, 1, 1, r)

                def pair(i, last):
                    for m in range(1, 2 * t_n + 1 - last):
                        if m + 1 < 2 * t_n or not last:
                            probs(i, m + 1)
                        for h, r in pieces_at(branch, t_n, m, last):
                            piece(ph, 2 * i + h, h % 2, r)
                        copy_turned(i, m)
                        for h in range(2):
                            if branch == 1 and m + 1 == (h + 1) * t_n - 1 and not last:
                                load_bias(ph, 2 * i + 2 + h, h)

                with act.Fori(0, HEADS // 2 - 1) as i:
                    pair(i, False)
                pair(HEADS // 2 - 1, True)
                for j, t in enumerate(QUERY_ORDER[t_n]):
                    act.wait_ge(S("o_turned"), at(ph, "o_turned") + j + 1)
                    nc.scalar.activation(o_hi[:, :, t * P:(t + 1) * P],
                                         ps[:, TURN_BANKS[t_n][j], :].rearrange("p (a b) -> p a b", a=KB), ACT.Copy
                                         ).then_inc(S("o_hi"), 1)

            def project(ph):
                act.wait_ge(S("merged"), at(ph, "merged"))
                act.wait_ge(S("mods_ready"), MODS_READY[ph.layer, 1])

                def chunks(i):
                    for s in range(2):
                        def use():
                            for c, (a, b) in enumerate(((0, LAT), (LAT, TOK))[:1 + (ph.tiles > LT)]):
                                dst = acc[:, bass.ds(2 * i + s, 1), a:b].rearrange("p a b -> p (a b)")
                                last = nc.scalar.activation(dst, span(2 * s, b - a, a), ACT.Copy,
                                                            scale=mods_v[:, ph.layer, 2, bass.ds(2 * i + s, 1), c])
                            last.then_inc(S("projected"), 1)
                        unit_done(ph.unit + 2 * i + s, s, use)

                with act.Fori(0, KD // 4) as i:
                    chunks(i)
                load_residual(ph)
                with act.Fori(KD // 4, KD // 2) as i:
                    chunks(i)

            def residual(ph):
                last = ph.layer == DEPTH - 1 and ph.part == 1
                act.wait_ge(S("unit_done"), ph.unit)
                for n in range(2):
                    act.dma_start(ln_rows[:, n, :], norm_rows[ph.layer, ph.part, n, :].partition_broadcast(P)
                                  ).then_inc(S("rows_loaded"), 16)
                load_table(ACT.Sqrt)
                norm_steps(ph, last=last)
                act.wait_ge(S("stored"), at(ph, "stored") + 16 * ph.tiles)

            def gate_up(ph):
                with act.Fori(0, PARTS[ph.part][1] // 2) as i:
                    for c in range(2):
                        def use():
                            act.wait_ge(S("hidden"), at(ph, "hidden") + 2 * i + c - 1)
                            nc.scalar.activation(silu_g[:, c, 0:ph.width], span(4 * c, ph.width), ACT.Silu
                                                 ).then_inc(S("silu"), 1)
                        unit_done(ph.unit + 4 * i + 2 * c, 0, use)
                        unit_done(ph.unit + 4 * i + 2 * c + 1, 1)

            def down(ph):
                if ph.part == len(PARTS) - 1:
                    load_residual(ph)
                end = ph.unit + KD == n_units
                with act.Fori(0, KD // 2 - end) as i:
                    for s in range(2):
                        unit_done(ph.unit + 2 * i + s, s)

            for ph in phases:
                {"first_norm": first_norm, "modulate": modulate, "fourier_in": fourier_in, "tokens_a": tokens,
                 "tokens_b": tokens, "fourier": fourier, "merge": merge, "attention": attention, "project": project,
                 "residual": residual, "gate_up": gate_up, "down": down}[ph.kind](ph)

        @block.vector
        def _(dve):
            prime(dve, ("branch_read", "merged", "hidden", "summed", "piece_lo", "o_norm", "added", "pt_dve", "inverse",
                        "ada_used"))
            def ada_three(kind, n):
                for s in range(ADA_SLOTS):
                    dve.wait_ge(ada_ready[s], 16 * (n - ADA_FIRST // ADA_SLOTS) + 16)
                    u = ADA_SLOTS * n + s
                    for c, done in enumerate(("ada_half", "ada_used")):
                        if c == 0:
                            dve.wait_ge(S("ada_used"), PRIME + u - ADA_FIRST)
                        else:
                            dve.wait_ge(S("ada_half"), u + 1 - ADA_FIRST)
                        nc.vector.scalar_tensor_tensor(
                            ada_unused[kind][:, :], ada_raw[kind][:, s, :], 1.0, ada_cond[kind][:, c, :],
                            ALU.mult, ALU.mult, accum_out=mods[:, bass.ds(u, 1), c]).then_inc(S(done), 1)

            def ada_biased(first, end, products):
                nc.vector.tensor_tensor(mods[:, first:end, :], products,
                                        ada_bias[:, first:end].unsqueeze(2).broadcast_to([P, end - first, 2]), ALU.add
                                        ).then_inc(S("mods_ready"), 1)

            def ada_window(kind, layer):
                first, end = ADA_WINDOWS[kind, layer]
                n = list(ADA_WINDOWS).index((kind, layer)) + 1
                dve.wait_ge(S("cond_loaded"), 32 + 16 * n)
                with dve.Fori(first // ADA_SLOTS, end // ADA_SLOTS) as i:
                    ada_three(kind, i)
                dve.wait_ge(S("ada_used"), PRIME - ADA_FIRST + end)
                ada_biased(first, end, mods[:, first:end, :])
                dve.wait_ge(S("mods_ready"), n + 1)

            def chain(name, start):
                count = [start]

                def step(instruction):
                    count[0] += 1
                    instruction.then_inc(S(name), 1)
                    dve.wait_ge(S(name), count[0])
                return step

            def inverse_root(step, n, ph):
                dve.wait_ge(S("std_ready"), at(ph, "std_ready") + 1)
                step(nc.vector.reciprocal(inv_s[:, 0:n], std_s[:, 0:n]))
                inv, tmp = inv_s[:, 0:n], tmp_s[:, 0:n]
                step(nc.vector.scalar_tensor_tensor(tmp, inv, -0.5, inv, ALU.mult, ALU.mult))
                step(nc.vector.tensor_tensor(tmp, tmp, var_s[:, 0:n], ALU.mult))
                step(nc.vector.scalar_tensor_tensor(inv, tmp, 1.5, inv, ALU.add, ALU.mult))

            def norms(ph, first=False, last=False):
                step = chain("norm_step", at(ph, "norm_step"))
                seen = dict.fromkeys(("std", "root"), 0)

                def mean(second, t):
                    nc.vector.tensor_scalar(neg_mean[:, second, t:t + 1], sum_s[:, second, t:t + 1], -1.0 / D, None,
                                            ALU.mult).then_inc(S("mean_ready"), 1)

                for name, g in NORM_ORDER:
                    if not in_norms(name, g, ph, first, last):
                        continue
                    tiles = (2 * g, 2 * g + 1)
                    second = int(name.endswith("2"))
                    a = ALLT * second + 2 * g
                    if name == "add":
                        for t in tiles:
                            dve.wait_ge(S("turned"), at(ph, "turned") + t + 1)
                            nc.vector.scalar_tensor_tensor(xr[:, t, :], xr[:, t, :], ALPHA,
                                                           span(2 * ((t + 2) % 4), D),
                                                           ALU.mult, ALU.add, accum_out=sum_s[:, 0, t:t + 1]
                                                           ).then_inc(S("added"), 1)
                        for t in tiles:
                            dve.wait_ge(S("added"), at(ph, "added") + t + 1)
                            mean(0, t)
                    elif name.startswith("var"):
                        squares = 2 * steps_before(("square2" if second else "square", g), ph, first, last)
                        dve.wait_ge(S("squared"), at(ph, "squared") + squares)
                        nc.vector.tensor_scalar(var_s[:, a:a + 2], square_s[:, second, 2 * g:2 * g + 2], 1.0 / D, EPS,
                                                ALU.mult, ALU.add).then_inc(S("var_ready"), 1)
                    elif name.startswith("root"):
                        seen["std"] += 1
                        seen["root"] += 1
                        dve.wait_ge(S("std_ready"), at(ph, "std_ready") + seen["std"])
                        inv, tmp = inv_s[:, a:a + 2], tmp_s[:, a:a + 2]
                        step(nc.vector.reciprocal(inv, std_s[:, a:a + 2]))
                        step(nc.vector.scalar_tensor_tensor(tmp, inv, -0.5, inv, ALU.mult, ALU.mult))
                        step(nc.vector.tensor_tensor(tmp, tmp, var_s[:, a:a + 2], ALU.mult))
                        last_step = nc.vector.scalar_tensor_tensor(inv, tmp, 1.5, inv, ALU.add, ALU.mult)
                        if second:
                            step(last_step)
                            last_step = nc.vector.tensor_tensor(shift_s[:, 2 * g:2 * g + 2],
                                                                neg_mean[:, 1, 2 * g:2 * g + 2], inv, ALU.mult)
                        last_step.then_inc(S("root_ready"), 1)
                    elif name == "affine" and first:
                        for t in tiles:
                            nc.vector.tensor_reduce(sum_s[:, 1, t:t + 1], xr[:, t, :], axis=AX.X, op=ALU.add
                                                    ).then_inc(S("summed_x"), 1)
                        for t in tiles:
                            dve.wait_ge(S("summed_x"), at(ph, "summed_x") + t + 1)
                            mean(1, t)
                    elif name == "affine":
                        if g == 0:
                            dve.wait_ge(S("rows_loaded"), at(ph, "rows_loaded") + 32)
                        dve.wait_ge(S("root_ready"), at(ph, "root_ready") + seen["root"])
                        if g == 0:
                            dve.wait_ge(S("rows_loaded"), at(ph, "rows_loaded") + 32)
                        t = tiles[0]
                        nc.vector.scalar_tensor_tensor(xn[:, t, :], xr[:, t, :], neg_mean[:, 0, t:t + 1],
                                                       ln_rows[:, 0, :], ALU.add, ALU.mult).then_inc(S("scaled"), 1)
                        for t in tiles:
                            name = ("scaled", "scaled_odd")[t % 2]
                            dve.wait_ge(S(name), at(ph, name) + t // 2 + 1)
                            nc.vector.scalar_tensor_tensor(xr[:, t, :], xn[:, t, :], inv_s[:, t:t + 1],
                                                           ln_rows[:, 1, :], ALU.mult, ALU.add,
                                                           accum_out=sum_s[:, 1, t:t + 1]).then_inc(S("shifted"), 1)
                        if not last:
                            dve.wait_ge(S("shifted"), at(ph, "shifted") + 2 * g + 2)
                            for t in tiles:
                                mean(1, t)

                    elif name == "apply":
                        dve.wait_ge(S("root_ready"), at(ph, "root_ready") + seen["root"])
                        t = tiles[1]
                        nc.vector.tensor_scalar(xn[:, t, :], xr[:, t, :], inv_s[:, ALLT + t:ALLT + t + 1],
                                                shift_s[:, t:t + 1], ALU.mult, ALU.add).then_inc(S("normed_odd"), 1)

            def first_norm(ph):
                dve.wait_ge(S("loaded"), 16 * ALLT)
                norms(ph, first=True)
                dve.wait_ge(S("consts"), 16 * 5)
                bias_v = ada_bias[:, :].rearrange("p (l s k) -> p l s k", l=DEPTH, s=6)
                for s in (1, 4):
                    nc.vector.tensor_scalar(bias_v[:, :, s, :], bias_v[:, :, s, :], 1.0, None, ALU.add
                                            ).then_inc(S("bias_raised"), 1)
                dve.wait_ge(S("bias_raised"), 2)
                dve.wait_ge(S("columns"), 1)
                ada_biased(0, ADA_FIRST, ps[:, 7, 0:2 * ADA_FIRST].rearrange("p (a c) -> p a c", c=2))
                dve.wait_ge(S("mods_ready"), 1)

            def modulate(ph):
                w = ph.width
                for k in range(KD):
                    dve.wait_ge(S("h_val"), at(ph, "h_val") + k + 1)
                    nc.vector.tensor_copy(h_hi[:, k, 0:w], h_tmp[:, k % 4, 0:w]).then_inc(S("h_hi"), 1)
                    if k % 2 == 0:
                        dve.wait_ge(S("h_hi"), at(ph, "h_hi") + k + 1)
                        nc.vector.tensor_tensor(h_lo[:, k, 0:w], h_tmp[:, k % 4, 0:w], h_hi[:, k, 0:w].bitcast(F32),
                                                ALU.subtract).then_inc(S("h_lo"), 1)

            def heads_view(ph, a, t):
                n = NH_A if t < ph.tiles else KV_A
                return a[:, (NH_A - n) * HD:].rearrange("p (h d) -> p h d", d=HD), n

            def tokens_a(ph):
                step = chain("rope_step", at(ph, "rope_step"))
                sums = var_s[:, :].rearrange("p (t h) -> p t h", t=ALLT)
                step(nc.vector.memset(var_s[:, :], 1.0))
                for n, (g, scale) in enumerate(((0, QSCALE), (1, QSCALE), (2, 1.0), (3, 1.0))):
                    last = nc.vector.scalar_tensor_tensor(
                        rope_g[:, n, :, :], rope[:, n % 2, :, :], scale,
                        gain[:, ph.layer, g, :].unsqueeze(1).broadcast_to([P, ALLT, HD]), ALU.mult, ALU.mult)
                step(last)
                dve.wait_ge(S("evacuated"), at(ph, "evacuated") + ph.tiles + ALLT)

                for t in range(ALLT):
                    x, n = heads_view(ph, tok_a[:, t, :], t)
                    sq, _ = heads_view(ph, rope_t[t % 2][:, :], t)
                    step(nc.vector.tensor_tensor(sq, x, x, ALU.mult))
                    step(nc.vector.tensor_reduce(sums[:, t, NH_A - n:], sq, axis=AX.X, op=ALU.add))
                step(nc.vector.tensor_scalar(var_s[:, :], var_s[:, :], 1.0 / HD, EPS, ALU.mult, ALU.add))
                nc.vector.tensor_copy(tmp_s[:, :], var_s[:, :]).then_inc(S("var_ready"), 1)

            def rotate(ph):
                step = chain("rope_step", at(ph, "rope_step") - ROTATE_STEPS)
                invs = inv_s[:, :].rearrange("p (t h) -> p t h", t=ALLT)
                inverse_root(step, ALLT * NH_A, ph)
                for t in range(ALLT):
                    x, n = heads_view(ph, tok_a[:, t, :], t)
                    kept, turned = heads_view(ph, rope_t[0][:, :], t)[0], heads_view(ph, rope_t[1][:, :], t)[0]
                    step(nc.vector.tensor_tensor(x, x, invs[:, t, NH_A - n:].unsqueeze(2).broadcast_to([P, n, HD]),
                                                 ALU.mult))
                    parts = ((0, n - KV_A, 0), (n - KV_A, n, 2)) if n > KV_A else ((0, n, 2),)
                    for a, b, g in parts:
                        nc.vector.tensor_tensor(kept[:, a:b, :], x[:, a:b, :],
                                                rope_g[:, g, t, :].unsqueeze(1).broadcast_to([P, b - a, HD]), ALU.mult)
                    for a, b, g in parts:
                        for quarter in range(2):
                            def of(v, q):
                                return v.rearrange("p h (a q d) -> p h a q d", a=2, q=2)[:, :, :, q, :]
                            sin = rope_g[:, g + 1, t, :].rearrange("p (a q d) -> p a q d", a=2, q=2)[:, :, quarter, :]
                            last = nc.vector.tensor_tensor(of(turned[:, a:b, :], quarter), of(x[:, a:b, :], 1 - quarter),
                                                           sin.unsqueeze(1).broadcast_to([P, b - a, 2, HD // 4]), ALU.mult)
                    step(last)
                    step(nc.vector.tensor_tensor(x, kept, turned, ALU.add))

            def fourier(ph):
                for g in range(KB):
                    dve.wait_ge(S("odd_out"), at(ph, "odd_out") + g + 1)
                    if g >= 2:
                        dve.wait_ge(S("o_hi"), at(ph, "o_hi") + g - 1)
                        dve.wait_ge(S("o_lo"), at(ph, "o_lo") + g - 1)
                    runs = [(0, 0, 2 * P, ALU.subtract), (2 * P, P, P, ALU.add), (3 * P, 0, P, ALU.add)]
                    if ph.tiles > LT:
                        runs += [(LAT, FREQ_L, P, ALU.subtract), (LAT + P, FREQ_L, P, ALU.add)]
                    for a, b, n, op in runs:
                        last = nc.vector.tensor_tensor(mix[:, g % 2, a:a + n], ps[:, 2 * g, b:b + n],
                                                       odd[:, g % 2, b:b + n], op)
                    last.then_inc(S("halves_made"), 1)
                    dve.wait_ge(S("halves_made"), at(ph, "halves_made") + g + 1)
                    if ph.tiles > LT:
                        a = FREQ_L + FREQ_X - 1
                        nc.vector.tensor_tensor(mix[:, g % 2, LAT + P:LAT + P + 1], ps[:, 2 * g, a:a + 1],
                                                odd[:, g % 2, a:a + 1], ALU.subtract)
                    nc.vector.tensor_tensor(mix[:, g % 2, 2 * P:4 * P].rearrange("p (a b) -> p a b", b=WIN)[:, :, 0],
                                            ps[:, 2 * g, 2 * P:FREQ_L], odd[:, g % 2, 2 * P:FREQ_L], ALU.subtract
                                            ).then_inc(S("mix_made"), 1)
                rotate(ph)

            def merge(ph):
                w = ph.width
                with dve.Fori(0, 2) as i:
                    for half in range(2):
                        for j in range(2):
                            c = 2 * half + j
                            chunk = acc[:, bass.ds(4 * i + c, 1), 0:w].rearrange("p a b -> p (a b)")
                            dve.wait_ge(S("unit_done"), ph.unit + 6 * i + 3 * half + 3)
                            dve.wait_ge(S("gated"), at(ph, "gated") + 4 * i + c + 1)
                            if ph.part == 2:
                                nc.vector.tensor_tensor(chunk, gate[:, c, 0:w], span(4 + 2 * j, w), ALU.mult
                                                        ).then_inc(S("merged"), 1)
                            else:
                                nc.vector.tensor_tensor(gate[:, c, 0:w], gate[:, c, 0:w], span(4 + 2 * j, w), ALU.mult
                                                        ).then_inc(S("branch_read"), 1)
                                dve.wait_ge(S("branch_read"), at(ph, "branch_read") + 4 * i + c + 1)
                                nc.vector.tensor_tensor(chunk, chunk, gate[:, c, 0:w], ALU.add
                                                        ).then_inc(S("merged"), 1)
                            if ph.part == 1:
                                y = at(ph, "y_split") + 8 * i + 2 * c
                                hi = y_hi[:, bass.ds(4 * i + c, 1), 0:w].rearrange("p a b -> p (a b)")
                                lo = y_lo[:, bass.ds(4 * i + c, 1), 0:w].rearrange("p a b -> p (a b)")
                                dve.wait_ge(S("merged"), at(ph, "merged") + 4 * i + c + 1)
                                nc.vector.tensor_scalar(hi, chunk, 1.0, None, ALU.mult).then_inc(S("y_split"), 1)
                                dve.wait_ge(S("y_split"), y + 1)
                                nc.vector.tensor_tensor(lo, chunk, hi.bitcast(F32), ALU.subtract
                                                        ).then_inc(S("y_split"), 1)

            def piece(ph, h, s, r, bank=7):
                what, a, b = PIECES[r]
                dve.wait_ge(S("piece_hi"), at(ph, "piece_hi") + piece_number(ph, h, r) + 1)
                rows = slice(HD, P) if what == "q" else slice(0, P)
                hi = q_st[s][rows, a:b] if what == "q" else k_hh[rows, s, a:b]
                dst = hi if what == "q" else k_ll[rows, s, a:b]
                nc.vector.tensor_tensor(dst, ps[rows, bank, 0:b - a], hi.bitcast(F32),
                                        ALU.subtract).then_inc(S("piece_lo"), 1)

            def tokens_b(ph):
                for r in range(ROUNDS[ph.tiles]):
                    piece(after(ph), 0, 0, r, START_BANKS[1][r])
                dve.wait_ge(S("unit_done"), ph.unit + 12)
                for t in range(1, ALLT, 2):
                    nc.vector.tensor_copy(v_b[:, t, :], ps[:, VALUE_BANKS[ph.tiles][t], :]
                                          ).then_inc(S("values_out"), 1)

            def attention(ph):
                t_n, rounds, branch = ph.tiles, ROUNDS[ph.tiles], ph.part

                def maximum(i, m):
                    n, s, t, h = 2 * t_n * i + m, m % 2, QUERY_ORDER[t_n][m % t_n], m // t_n
                    keys = P * len(key_tiles(branch, t))
                    dve.wait_ge(S("scored"), at(ph, "scored") + n + 1)
                    dve.wait_ge(S("probs"), at(ph, "probs") + n - 1)
                    if branch == 1 and t < LT:
                        if t == 0:
                            dve.wait_ge(bias_ready[h % 2], 16 * (HEADS // 2) * ph.layer + 16 * (i + h // 2) + 16)
                        nc.vector.tensor_reduce(max_c[:, s:s + 1], span(2 * s, CTX), axis=AX.X, op=ALU.max
                                                ).then_inc(S("max_part"), 1)
                        lat = span(2 * s, keys - CTX, CTX)
                        nc.vector.tensor_tensor_reduce(out=lat, in0=lat,
                                                       in1=bias_sb[h % 2][:, BIAS_AT[t]:BIAS_AT[t] + BIAS_KEYS[t]],
                                                       scale=1.0, scalar=3 * MASKED, op0=ALU.add, op1=ALU.max,
                                                       accum_out=max_a[:, s:s + 1]).then_inc(S("max_bias"), 1)
                        dve.wait_ge(S("max_part"), at(ph, "max_part") + n + 1)
                        dve.wait_ge(S("max_bias"), LT * (HEADS * ph.layer + 2 * i + h) + t + 1)
                        nc.vector.tensor_scalar(neg_max[:, s:s + 1], max_a[:, s:s + 1], max_c[:, s:s + 1], -1.0,
                                                ALU.max, ALU.mult).then_inc(S("max_ready"), 1)
                    else:
                        nc.vector.tensor_reduce(max_c[:, s:s + 1], span(2 * s, keys), axis=AX.X, op=ALU.max
                                                ).then_inc(S("max_part"), 1)
                        dve.wait_ge(S("max_part"), at(ph, "max_part") + n + 1)
                        nc.vector.tensor_scalar(neg_max[:, s:s + 1], max_c[:, s:s + 1], -1.0, None, ALU.mult
                                                ).then_inc(S("max_ready"), 1)

                def copy_turned(i, m):
                    keys = P * len(key_tiles(branch, QUERY_ORDER[t_n][m % t_n]))
                    if keys > 512:
                        dve.wait_ge(S("turned_p"), at(ph, "turned_p") + 2 * t_n * i + m + 1)
                        nc.vector.tensor_scalar(pt_sb[branch][m % 2][:, 512:keys], ps[:, 5, 0:keys - 512], 1.0, None,
                                                ALU.mult).then_inc(S("pt_dve"), 1)

                def invert(i, m):
                    dve.wait_ge(S("probs"), at(ph, "probs") + 2 * t_n * i + m + 1)
                    nc.vector.reciprocal(row_inv[:, m % 4:m % 4 + 1], row_sum[:, m % 2:m % 2 + 1]
                                         ).then_inc(S("inverse"), 1)

                def normalise(i, m):
                    n, t, h = 2 * t_n * i + m, QUERY_ORDER[t_n][m % t_n], m // t_n
                    dve.wait_ge(S("inverse"), at(ph, "inverse") + n + 1)
                    dve.wait_ge(S("attended"), at(ph, "attended") + n + 1)
                    col = HD * (i // 2) if branch == 0 else HD * h
                    nc.vector.tensor_scalar(o_tok[:, t, bass.ds((2 * i + h) * HD, HD)], ps[:, 6, bass.ds(col, HD)],
                                            row_inv[:, m % 4:m % 4 + 1], None, ALU.mult).then_inc(S("o_norm"), 1)

                if branch == 0:
                    for r in range(rounds):
                        piece(ph, 0, 0, r, START_BANKS[0][r])
                maximum(0, 0)
                maximum(0, 1)
                for r in START_PIECES[branch][0]:
                    piece(ph, 1, 1, r)
                copy_turned(0, 0)
                invert(0, 0)
                maximum(0, 2)
                for r in START_PIECES[branch][1][:rounds - 2]:
                    piece(ph, 1, 1, r)

                def pair(i, last):
                    for m in range(1, 2 * t_n + 1 - last):
                        for h, r in pieces_at(branch, t_n, m, last):
                            piece(ph, 2 * i + h, h % 2, r)
                        copy_turned(i, m)
                        invert(i, m)
                        if m + 2 < 2 * t_n or not last:
                            maximum(i, m + 2)
                        normalise(i, m - 1)
                    if last:
                        normalise(i, 2 * t_n - 1)

                with dve.Fori(0, HEADS // 2 - 1) as i:
                    pair(i, False)
                pair(HEADS // 2 - 1, True)
                for j, t in enumerate(QUERY_ORDER[t_n]):
                    dve.wait_ge(S("o_hi"), at(ph, "o_hi") + j + 1)
                    nc.vector.tensor_tensor(o_lo[:, :, t * P:(t + 1) * P],
                                            ps[:, TURN_BANKS[t_n][j], :].rearrange("p (a b) -> p a b", a=KB),
                                            o_hi[:, :, t * P:(t + 1) * P].bitcast(F32), ALU.subtract
                                            ).then_inc(S("o_lo"), 1)

            def residual(ph):
                dve.wait_ge(S("loaded"), at(ph, "loaded"))
                norms(ph, last=ph.layer == DEPTH - 1 and ph.part == 1)

            def gate_up(ph):
                w = ph.width
                beside = ada_beside(ph)
                if beside == ADA_UNITS:
                    dve.wait_ge(S("cond_loaded"), 32 + 16 * (len(ADA_WINDOWS) + 1))
                with dve.Fori(0, PARTS[ph.part][1] // 2) as i:
                    for c in range(2):
                        if c and beside:
                            ada_three("gate_up", beside // ADA_SLOTS + i)
                        n = 2 * i + c
                        hi = hid_hi[:, bass.ds(n, 1), 0:w].rearrange("p a b -> p (a b)")
                        lo = hid_lo[:, bass.ds(n, 1), 0:w].rearrange("p a b -> p (a b)")
                        dve.wait_ge(S("unit_done"), ph.unit + 4 * i + 2 * c + 2)
                        dve.wait_ge(S("silu"), at(ph, "silu") + n + 1)
                        nc.vector.tensor_tensor(hid[:, c, 0:w], silu_g[:, c, 0:w], span(4 * c + 2, w), ALU.mult
                                                ).then_inc(S("hidden"), 1)
                        dve.wait_ge(S("hidden"), at(ph, "hidden") + n + 1)
                        nc.vector.tensor_scalar(hi, hid[:, c, 0:w], 1.0, None, ALU.mult).then_inc(S("hidden_hi"), 1)
                        dve.wait_ge(S("hidden_hi"), at(ph, "hidden_hi") + n + 1)
                        nc.vector.tensor_tensor(lo, hid[:, c, 0:w], hi.bitcast(F32), ALU.subtract
                                                ).then_inc(S("hidden_lo"), 1)

            def down(ph):
                beside = ada_beside(ph)
                with dve.Fori(0, KD // 2) as i:
                    for s in range(2):
                        if s and beside:
                            ada_three("gate_up", beside // ADA_SLOTS + i)
                        n = 2 * i + s
                        dve.wait_ge(S("unit_done"), ph.unit + n + 1)
                        for c, (a, b) in enumerate(((0, LAT), (LAT, TOK))[:1 + (ph.tiles > LT)]):
                            dst = acc[:, bass.ds(n, 1), a:b].rearrange("p a b -> p (a b)")
                            g2 = mods_v[:, ph.layer, 5, bass.ds(n, 1), c]
                            if ph.part == 0:
                                last = nc.vector.tensor_scalar(dst, span(2 * s, b - a, a), g2, None, ALU.mult)
                            else:
                                last = nc.vector.scalar_tensor_tensor(dst, span(2 * s, b - a, a), g2, dst, ALU.mult,
                                                                      ALU.add)
                        last.then_inc(S("summed"), 1)
                if beside and (ph.kind, ph.part) == list(ADA_BESIDE)[-1]:
                    end = DEPTH * ADA_UNITS
                    dve.wait_ge(S("ada_used"), PRIME + end - ADA_FIRST)
                    ada_biased(ADA_UNITS, end, mods[:, ADA_UNITS:end, :])
                    dve.wait_ge(S("mods_ready"), MODS_READY[1, 0])

            for ph in phases:
                if (ph.kind, ph.layer) in ADA_WINDOWS:
                    ada_window(ph.kind, ph.layer)
                work = {"first_norm": first_norm, "modulate": modulate, "tokens_a": tokens_a, "tokens_b": tokens_b,
                        "fourier": fourier, "merge": merge, "attention": attention, "residual": residual, "gate_up": gate_up,
                        "down": down}.get(ph.kind)
                if work:
                    work(ph)

        @block.tensor
        def _(pe):
            prime(pe, ("piece", "attended", "scored", "turned_p"))

            def first_norm(ph):
                pe.wait_ge(S("cond_ready"), 1)
                for k in range(KD):
                    pe.wait_ge(first_ready[k % 2], 16 * (k // 2) + 16)
                    for b in range(-(-ADA_FIRST // 4)):
                        w = min(4, ADA_FIRST - 4 * b) * P
                        last = nc.tensor.matmul(ps[0:2, b, 0:w], cond_act[:, k, :],
                                                first_raw[:, k % 2, 512 * b:512 * b + w],
                                                start=k == 0, stop=k == KD - 1)
                    last.then_inc(S("first_used"), 1)
                pe.wait_ge(S("consts"), 16 * 5)
                for j in range(ADA_FIRST):
                    pe.wait_ge(S("rows_out"), j // 4 + 1)
                    last = nc.tensor.transpose(ps[:, 7, 2 * j:2 * j + 2], first_rows[:, j * P:(j + 1) * P],
                                               ident[0:2, 0:2])
                last.then_inc(S("columns"), 1)

            def columns(ph, u, s, bank, x_hi, x_lo, k_tiles, first=0, ready=lambda k: None):
                pe.wait_ge(S("lo_made"), u + 1)
                wide = ph.width > LAT
                for k in range(k_tiles):
                    ready(k)
                    for name in TERMS:
                        w, x = term(name, s, x_hi, x_lo)
                        tile = w[:, s, (first + k) * P:(first + k + 1) * P]
                        start = k == 0 and name == TERMS[0]
                        stop = k == k_tiles - 1 and name == TERMS[-1]
                        last = nc.tensor.matmul(bank(0), tile, x[:, k, 0:LAT], start=start, stop=stop)
                        if wide:
                            last = nc.tensor.matmul(bank(1), tile, x[:, k, LAT:TOK], start=start, stop=stop)
                return last

            def fixed(b):
                return lambda half: ps[:, b, :] if half == 0 else ps[:, b + 1, 0:CTX]

            def modulate(ph):
                pe.wait_ge(S("consts"), 16 * 5)
                if ph.unit:
                    pe.wait_ge(S("added"), at(ph, "added"))
                else:
                    pe.wait_ge(S("mods_ready"), 1)
                for t in range(ph.tiles):
                    name = ("normed", "normed_odd")[t % 2]
                    pe.wait_ge(S(name), at(ph, name) - ph.tiles // 2 + t // 2 + 1)
                    for k in range(4):
                        last = nc.tensor.transpose(span(2 * k, P, t * P), xn[:, t, k * P:(k + 1) * P], ident[:, :])
                        if t == ph.tiles - 1:
                            last.then_inc(S("turned"), 1)
                for k in range(4, KD):
                    pe.wait_ge(S("h_val"), at(ph, "h_val") + k - 3)
                    for t in range(ph.tiles):
                        last = nc.tensor.transpose(span(2 * (k % 4), P, t * P), xn[:, t, k * P:(k + 1) * P], ident[:, :])
                    last.then_inc(S("turned"), 1)

            def h_ready(ph):
                def ready(k):
                    name = ("h_lo", "h_lo_pool")[k % 2]
                    pe.wait_ge(S(name), at(ph, name) - KD // 2 + k // 2 + 1)
                return ready

            def fourier_in(ph):
                pe.wait_ge(S("h_val"), at(ph, "h_val") - 3)
                with pe.Fori(0, KB // 2) as i:
                    for s in range(2):
                        def bank(half):
                            b = ps[:, bass.ds(4 * i + 2 * s + half, 1), :].rearrange("p a b -> p (a b)")
                            return b if half == 0 else b[:, 0:CTX]
                        columns(ph, ph.unit + 2 * i + s, s, bank, h_hi, h_lo, KD, ready=h_ready(ph)
                                ).then_inc(S("unit_done"), 1)

            def piece(ph, h, s, r, bank=7):
                what, a, b = PIECES[r]
                if r == 0 or (what == "k" and ph.part == 0):
                    pe.wait_ge(S("staged"), at(ph, "staged") + (2 * h + 2 if ph.part == 1 or what == "k" else
                                                                staged_before(ph, h) + 1))
                if bank == 7:
                    pe.wait_ge(S("piece_lo"), at(ph, "piece_lo") + piece_number(ph, h, r))
                elif ph.part == 1 and r >= 2:
                    pe.wait_ge(S("piece_lo"), at(ph, "piece_lo") + r - 1)
                src = stage_q[ph.part][s] if what == "q" else stage_k[ph.part][s]
                for t in range(a // P, b // P):
                    last = nc.tensor.transpose(ps[:, bank, t * P - a:(t + 1) * P - a],
                                               src[:, t, :, :].rearrange("p a b -> p (a b)"), ident[:, :])
                last.then_inc(S("piece"), 1)

            def tokens(ph):
                if ph.kind == "tokens_a":
                    groups = ((4, ph.tiles, 512), (2, ALLT, 256))
                else:
                    groups = ((4, ph.tiles, 512), (4, ALLT, 512), (4, ALLT, 512))
                    pe.wait_ge(S("gated"), at(ph, "gated"))
                banks, u, first = token_banks(ph), ph.unit, 0
                for units, tiles, cols in groups:
                    per = UNIT * P // cols
                    for j in range(units):
                        s = j % 2
                        if ph.kind == "tokens_b" and u == ph.unit + 8:
                            for r in early_pieces(ph, j):
                                piece(after(ph), 0, 0, r, START_BANKS[1][r])
                        pe.wait_ge(S("lo_made"), u + j + 1)
                        for kk in range(per):
                            k = j * per + kk
                            for t in range(tiles):
                                n = first + t
                                if k == 0 and banks[n] in banks[:n]:
                                    held = max(m for m in range(n) if banks[m] == banks[n])
                                    pe.wait_ge(S("evacuated"), at(ph, "evacuated") + held + 1)
                                elif k == 0 and ph.kind == "tokens_a":
                                    pe.wait_ge(S("evacuated"), at(ph, "evacuated") - KB + banks[n] // 2 + 1)
                                elif k == 0 and banks[n] >= 4:
                                    pe.wait_ge(S("merged"), at(ph, "merged") - 1 + (banks[n] - 4) // 2)
                                for name in TERMS:
                                    w, x = {"lo_hi": (w_lo, h_hi), "hi_lo": (w_hi, h_lo), "hi_hi": (w_hi, h_hi)}[name]
                                    last = nc.tensor.matmul(ps[:, banks[n], 0:cols], x[:, k, t * P:(t + 1) * P],
                                                            w[:, s, kk * cols:(kk + 1) * cols],
                                                            start=k == 0 and name == TERMS[0],
                                                            stop=k == KD - 1 and name == TERMS[-1])
                        last.then_inc(S("unit_done"), 1)
                    u += units
                    first += tiles

            def fourier(ph):
                for n in range(2 * ph.tiles):
                    g, t = divmod(n, ph.tiles)
                    pe.wait_ge(S("evacuated"), at(ph, "evacuated") + n - 7)
                    for j in range(2):
                        last = nc.tensor.matmul(ps[:, z_bank(ph, n), 256 * j:256 * j + 256],
                                                u_cols[:, 2 * g + j, t * P:(t + 1) * P], dft_c[:, :],
                                                start=True, stop=True)
                    last.then_inc(S("z_made"), 1)
                pe.wait_ge(S("dft_loaded"), 32 * (ph.layer + 1))
                for g in range(KB):
                    held = [n for n in range(2 * ph.tiles) if z_bank(ph, n) in (2 * g, 2 * g + 1)]
                    pe.wait_ge(S("evacuated"), at(ph, "evacuated") + max(max(held) + 1, (g // 2 + 1) * ph.tiles))
                    for part in range(2):
                        for t in range(LT):
                            last = nc.tensor.matmul(ps[:, 2 * g + part, 0:FREQ_L],
                                                    z_sb[:, t, g, part * P:(part + 1) * P], dft_l[:, t, part, :],
                                                    start=t == 0, stop=t == LT - 1)
                        for t in range(ph.tiles - LT):
                            last = nc.tensor.matmul(ps[:, 2 * g + part, FREQ_L:FREQ_L + FREQ_X],
                                                    z_sb[:, LT + t, g, part * P:(part + 1) * P], dft_x[:, t, part, :],
                                                    start=t == 0, stop=t == CT - 1)
                    last.then_inc(S("mixed"), 1)

            def merge(ph):
                read = "merged" if ph.part == 2 else "branch_read"
                with pe.Fori(0, 2) as i:
                    for half in range(2):
                        for j in range(3):
                            n = 3 * half + j
                            u = ph.unit + 6 * i + n
                            if j < 2:
                                if ph.part == 2:
                                    pe.wait_ge(S("mix_made"), at(ph, "mix_made") - KB + 1 + j)
                                elif j:
                                    pe.wait_ge(S("o_lo"), at(ph, "o_lo") - 1)
                                pe.wait_ge(S("gated"), at(ph, "gated") + 4 * i + 2 * half + j - 1)
                                columns(ph, u, n % 2, fixed(2 * j), h_hi, h_lo, KD).then_inc(S("unit_done"), 1)
                            else:
                                pe.wait_ge(S("o_lo"), at(ph, "o_lo"))
                                for c in range(2):
                                    pe.wait_ge(S(read), at(ph, read) + 4 * i + 2 * half + c - 1)
                                    last = columns(ph, u, n % 2, fixed(4 + 2 * c), o_hi, o_lo, KB, first=KB * c)
                                last.then_inc(S("unit_done"), 1)

            def attention(ph):
                t_n, rounds, branch = ph.tiles, ROUNDS[ph.tiles], ph.part

                def score(i, m):
                    n, s, t, h = 2 * t_n * i + m, m % 2, QUERY_ORDER[t_n][m % t_n], m // t_n
                    if t == 0:
                        start = isinstance(i, int) and 2 * i + h == 0
                        pe.wait_ge(S("piece_lo"), at(ph, "piece_lo")
                                   + (rounds if start else pieces_before(ph, 2 * i + h + 1)))
                    pe.wait_ge(S("probs"), at(ph, "probs") + n - 1)
                    keys = h % 2 if branch == 1 else (i + h // 2) // 2
                    for part, kk in enumerate((k_hh, k_ll)):
                        for a, b, at_col in key_runs(branch, t):
                            last = nc.tensor.matmul(span(2 * s, b - a, at_col) if at_col < 512 else
                                                    ps[:, 2 * s + 1, at_col - 512:at_col - 512 + b - a],
                                                    q_st[h % 2][:, t * P:(t + 1) * P],
                                                    kk[:, bass.ds(keys, 1), a:b].rearrange("p a b -> p (a b)"),
                                                    start=part == 0 and at_col in (0, 512), stop=part == 1,
                                                    skip_group_check=True)
                    last.then_inc(S("scored"), 1)

                def turn(i, m):
                    n, t, h = 2 * t_n * i + m, QUERY_ORDER[t_n][m % t_n], m // t_n
                    pe.wait_ge(S("probs"), at(ph, "probs") + n + 1)
                    pe.wait_ge(S("pt_act"), at(ph, "pt_act") + n)
                    pe.wait_ge(S("pt_dve"), at(ph, "pt_dve") + wide_tiles(branch, t_n, t_n) * (2 * i + h)
                               + wide_tiles(branch, t_n, m % t_n))
                    for kk in range(len(key_tiles(branch, t))):
                        last = nc.tensor.transpose(ps[:, 4 + kk // 4, (kk % 4) * P:(kk % 4 + 1) * P],
                                                   p_sb[branch][m % 2][:, kk * P:(kk + 1) * P], ident[:, :])
                    last.then_inc(S("turned_p"), 1)

                def attend(i, m):
                    n, t, h = 2 * t_n * i + m, QUERY_ORDER[t_n][m % t_n], m // t_n
                    pe.wait_ge(S("pt_act"), at(ph, "pt_act") + n + 1)
                    pe.wait_ge(S("pt_dve"), at(ph, "pt_dve") + wide_tiles(branch, t_n, t_n) * (2 * i + h)
                               + wide_tiles(branch, t_n, m % t_n + 1))
                    pe.wait_ge(S("o_norm"), at(ph, "o_norm") + n)
                    tiles = key_tiles(branch, t)
                    for kk, kt in enumerate(tiles):
                        values = v_a[:, kt, :] if branch == 0 else v_b[:, kt, bass.ds(2 * HD * i, 2 * HD)]
                        last = nc.tensor.matmul(ps[:, 6, 0:2 * HD], pt_sb[branch][m % 2][:, kk * P:(kk + 1) * P],
                                                values, start=kk == 0, stop=kk == len(tiles) - 1)
                    last.then_inc(S("attended"), 1)

                def values_out(banks):
                    for t in (VALUE_BANKS[t_n].index(b) for b in banks if b in VALUE_BANKS[t_n]):
                        name = ("evacuated", "values_out")[t % 2]
                        pe.wait_ge(S(name), at(ph, name) - ALLT // 2 + t // 2 + 1)

                if branch == 0:
                    pe.wait_ge(S("gated"), at(ph, "gated"))
                    for r in range(rounds):
                        piece(ph, 0, 0, r, START_BANKS[0][r])
                else:
                    values_out((0, 1))
                score(0, 0)
                if branch == 1:
                    values_out((2, 3))
                score(0, 1)
                if branch == 0:
                    pe.wait_ge(S("merged"), at(ph, "merged"))
                else:
                    values_out((4, 5, 6, 7))
                for r in START_PIECES[branch][0]:
                    piece(ph, 1, 1, r)
                turn(0, 0)
                score(0, 2)
                for r in START_PIECES[branch][1][:rounds - 2]:
                    piece(ph, 1, 1, r)

                def pair(i, last):
                    for m in range(1, 2 * t_n + 1 - last):
                        for h, r in pieces_at(branch, t_n, m, last):
                            piece(ph, 2 * i + h, h % 2, r)
                        turn(i, m)
                        if m + 2 < 2 * t_n or not last:
                            score(i, m + 2)
                        attend(i, m - 1)
                    if last:
                        attend(i, 2 * t_n - 1)

                with pe.Fori(0, HEADS // 2 - 1) as i:
                    pair(i, False)
                pair(HEADS // 2 - 1, True)
                for j, t in enumerate(QUERY_ORDER[t_n]):
                    pe.wait_ge(S("o_norm"), at(ph, "o_norm") + (HEADS - 1) * t_n + j + 1)
                    for c in range(KB):
                        last = nc.tensor.transpose(ps[:, TURN_BANKS[t_n][j], c * P:(c + 1) * P], o_tok[:, t, c * P:(c + 1) * P],
                                                   ident[:, :])
                    last.then_inc(S("o_turned"), 1)

            def project(ph):
                def ready(k):
                    pe.wait_ge(S("y_split"), at(ph, "y_split") - 2 * KD + 2 * k + 2)
                pe.wait_ge(S("gated"), at(ph, "gated"))
                with pe.Fori(0, KD // 2) as i:
                    for s in range(2):
                        pe.wait_ge(S("projected"), at(ph, "projected") + 2 * i + s - 1)
                        columns(ph, ph.unit + 2 * i + s, s, fixed(2 * s), y_hi, y_lo, KD, ready=ready
                                ).then_inc(S("unit_done"), 1)

            def residual(ph):
                chunks = ("projected", "summed")[ph.part]
                for t in range(ph.tiles):
                    if t >= 4:
                        pe.wait_ge(S("added"), at(ph, "added") + t - 3)
                    bank = 2 * ((t + 2) % 4)
                    for j in range(KD):
                        if t == 0:
                            pe.wait_ge(S(chunks), at(ph, chunks) - KD + j + 1)
                        last = nc.tensor.transpose(span(bank, P, j * P) if j < 4 else
                                                   ps[:, bank + 1, (j - 4) * P:(j - 3) * P],
                                                   acc[:, j, t * P:(t + 1) * P], ident[:, :])
                    last.then_inc(S("turned"), 1)

            def gate_up(ph):
                pe.wait_ge(S("h_val"), at(ph, "h_val") - 3)
                pe.wait_ge(S("summed"), at(ph, "summed") - 1)
                with pe.Fori(0, PARTS[ph.part][1] // 2) as i:
                    for c in range(2):
                        u = ph.unit + 4 * i + 2 * c
                        pe.wait_ge(S("silu"), at(ph, "silu") + 2 * i + c - 1)
                        columns(ph, u, 0, fixed(4 * c), h_hi, h_lo, KD, ready=h_ready(ph)).then_inc(S("unit_done"), 1)
                        pe.wait_ge(S("summed"), at(ph, "summed"))
                        pe.wait_ge(S("hidden"), at(ph, "hidden") + 2 * i + c - 1)
                        columns(ph, u + 1, 1, fixed(4 * c + 2), h_hi, h_lo, KD).then_inc(S("unit_done"), 1)

            def down(ph):
                chunks = PARTS[ph.part][1]

                def ready(k):
                    pe.wait_ge(S("hidden_lo"), at(ph, "hidden_lo") - chunks + k + 1)

                with pe.Fori(0, KD // 2) as i:
                    for s in range(2):
                        pe.wait_ge(S("summed"), at(ph, "summed") + 2 * i + s - 1)
                        columns(ph, ph.unit + 2 * i + s, s, fixed(2 * s), hid_hi, hid_lo, chunks,
                                ready=ready).then_inc(S("unit_done"), 1)

            for ph in phases:
                work = {"first_norm": first_norm, "modulate": modulate, "fourier_in": fourier_in, "tokens_a": tokens, "tokens_b": tokens,
                        "fourier": fourier, "merge": merge, "attention": attention, "project": project,
                        "residual": residual, "gate_up": gate_up, "down": down}.get(ph.kind)
                if work:
                    work(ph)


MODS_READY = {(0, 0): 1, (0, 1): 2, (1, 0): 4, (1, 1): 4}


def in_norms(name, g, ph, first, last):
    if g >= ph.tiles // 2:
        return False
    of_second = name in ("square2", "var2", "std2", "root2", "apply")
    return name == "affine" or (of_second and not last) or (not of_second and not first)


def steps_before(step, ph, first, last):
    kind = step[0].rstrip("2")
    steps = [s for s in NORM_ORDER if s[0].rstrip("2") == kind and in_norms(*s, ph, first, last)]
    return steps.index(step) + 1


START_BANKS = ((0, 1, 2, 3), (5, 6, 5, 6))
TURN_BANKS = {ALLT: (4, 5, 7, 3, 2, 6), LT: (4, 5, 7, 6)}


def token_banks(ph):
    if ph.kind == "tokens_a":
        return [n % 8 for n in range(ph.tiles + ALLT)]
    keys = [(ph.tiles + n) % 8 for n in range(ALLT)]
    return list(range(ph.tiles)) + keys + list(VALUE_BANKS[ph.tiles])


VALUE_BANKS = {ALLT: (4, 0, 1, 2, 3, 7), LT: (2, 3, 0, 1, 4, 7)}


def early_pieces(ph, unit):
    return {2: (0, 1), 3: tuple(range(2, ROUNDS[ph.tiles]))}.get(unit, ())


def z_bank(ph, n):
    return (n + ph.tiles + ALLT) % 8


PIECES = (("q", 0, LAT), ("k", 0, LAT), ("k", LAT, TOK), ("q", LAT, TOK))


START_PIECES = (((1, 2), (0, 3)), ((0, 1), ()))


def pieces_before(ph, h):
    rounds = ROUNDS[ph.tiles]
    return rounds * h if ph.part == 1 else rounds + 2 + (rounds - 2) * (h - 1)


def piece_number(ph, h, r):
    rounds = ROUNDS[ph.tiles]
    if ph.part == 1:
        return rounds * h + r
    if isinstance(h, int) and h == 0:
        return r
    if PIECES[r][0] == "k":
        return rounds + r - 1
    return pieces_before(ph, h) + (r == 3)


def staged_before(ph, h):
    if ph.part == 1:
        return 2 * h
    return 2 * h if isinstance(h, int) and h < 2 else h + 2


def pieces_at(branch, t_n, m, last):
    if branch == 0:
        steps = {5: ((2, 0),), 6: ((2, 3),), 11: ((3, 0),), 12: ((3, 3),)} if t_n == ALLT else {4: ((2, 0),), 7: ((3, 0),)}
    elif t_n == ALLT:
        steps = {1: ((1, 2),), 2: ((1, 3),), 5: ((2, 0),), 6: ((2, 1),), 7: ((2, 2),), 8: ((2, 3),), 11: ((3, 0),),
                 12: ((3, 1),)}
    else:
        steps = {1: ((1, 2),), 3: ((2, 0),), 4: ((2, 1),), 5: ((2, 2),), 7: ((3, 0),), 8: ((3, 1),)}
    return [(h, r) for h, r in steps.get(m, ()) if h == 1 or not last]


QUERY_ORDER = {ALLT: (0, 4, 1, 5, 2, 3), LT: (0, 1, 2, 3)}


def key_tiles(branch, t):
    ctx = [LT + c for c in range(CT)]
    if t >= LT:
        return ctx
    if branch == 0:
        return ctx + list(range(LT))
    return ctx + [FIRST_BLOCK[t] + b for b in range(BIAS_KEYS[t] // P)]


def wide_tiles(branch, t_n, n):
    return sum(P * len(key_tiles(branch, t)) > 512 for t in QUERY_ORDER[t_n][:n])


def key_runs(branch, t):
    runs = [(LAT, TOK, 0)]
    lat = key_tiles(branch, t)[CT:]
    if lat:
        a = lat[0] * P
        runs.append((a, a + 256, 256))
        if len(lat) > 2:
            runs.append((a + 256, a + 512, 512))
    return runs


def latent_order():
    row, col = np.divmod(np.arange(P), WIN)
    tiles = [row * GRID_W + block * WIN + col for block in range(GRID_W // WIN)]
    for block in (2, 3):
        tiles[block] = np.where(col == 0, tiles[block], LAT - tiles[3 - block])
    return np.concatenate(tiles)


def context_order():
    first = np.arange(P)
    return np.concatenate([first, np.where(first == 0, P, CTX - first)])


def feature_units(w):
    k, n = w.shape
    return w.reshape(k // P, P, n // P, P).transpose(2, 1, 0, 3).reshape(n // P, P, k)


def token_units(w, cols):
    per = UNIT * P // cols
    return w.reshape(KD // per, per, P, cols).transpose(0, 2, 1, 3).reshape(KD // per, P, per * cols)


def lay_stream(w_in, w_branch, w_out, w_gu, w_down):
    units = []
    for l in range(DEPTH):
        w = w_in[l]
        qa, ka, va, qb, kb, vb, uc, gz = np.split(w, np.cumsum((512, 128, 128, 512, 512, 512, 512)), axis=1)

        def merge(b):
            gates = feature_units(gz[:, b * D:(b + 1) * D])
            wb = w_branch[l, b].reshape(KB, P, KD // 2, 2, P).transpose(2, 1, 3, 0, 4).reshape(KD // 2, P, UNIT * P)
            for j in range(KD // 2):
                units.extend((gates[2 * j][None], gates[2 * j + 1][None], wb[j][None]))

        units.append(feature_units(uc))
        units.append(token_units(qa, 512))
        units.append(token_units(np.concatenate([ka, va], 1), 256))
        merge(2)
        merge(0)
        for m in (qb, kb, vb):
            units.append(token_units(m, 512))
        merge(1)
        units.append(feature_units(w_out[l]))
        gate, up = feature_units(w_gu[l][:, :D_FF]), feature_units(w_gu[l][:, D_FF:])
        for first, count in PARTS:
            for c in range(first, first + count):
                units.extend((gate[c][None], up[c][None]))
            rows = w_down[l][first * P:(first + count) * P]
            part = np.zeros((KD, P, UNIT * P), w_down.dtype)
            part[:, :, :count * P] = feature_units(rows)
            units.append(part)
    return np.concatenate(units, 0)


def lay_bias(rpb):
    out = np.full((DEPTH, HEADS, P, BIAS_W), MASKED, rpb.dtype)
    rows, cols = np.divmod(latent_order().reshape(LT, P), GRID_W)
    for block in range(GRID_W // WIN):
        start = np.clip(cols[block] - WIN // 2, 0, GRID_W - WIN)
        for b in range(BIAS_KEYS[block] // P):
            k_row, k_col = rows[FIRST_BLOCK[block] + b], cols[FIRST_BLOCK[block] + b]
            dr = k_row[None, :] - rows[block][:, None] + ROWS - 1
            dc = k_col[None, :] - cols[block][:, None] + WIN - 1
            seen = (k_col[None, :] >= start[:, None]) & (k_col[None, :] < start[:, None] + WIN)
            at = BIAS_AT[block] + b * P
            got = rpb[:, :, dr, np.clip(dc, 0, 2 * WIN - 2)]
            out[:, :, :, at:at + P] = np.where(seen, got, out[:, :, :, at:at + P])
    return out


def shape_tables():
    ident = np.eye(P, dtype=np.float32)
    quarter = HD // 4
    freqs = (10000.0 ** (-np.arange(quarter, dtype=np.float32) / np.float32(quarter))).astype(np.float32)
    pos, ctx_pos = latent_order(), context_order()
    rope = np.zeros((2, TOK, HD), np.float32)
    rope[0] = 1.0
    for half, where in enumerate((pos // GRID_W, pos % GRID_W)):
        ang = (where.astype(np.float32)[:, None] * freqs).astype(np.float32)
        for q in range(2):
            sl = slice(half * 2 * quarter + q * quarter, half * 2 * quarter + (q + 1) * quarter)
            rope[0, :LAT, sl] = np.cos(ang)
            rope[1, :LAT, sl] = (-1.0, 1.0)[q] * np.sin(ang)
    rope = rope.reshape(2, ALLT, P, HD).transpose(2, 0, 1, 3)

    def angles(n, i, j):
        return 2.0 * np.pi * ((i[:, None] * j[None, :]) % n) / n

    ch = angles(P, np.arange(P), np.arange(P))
    dft_ch = np.concatenate([np.cos(ch), np.sin(ch)], 1)
    lat = angles(LAT, pos, np.concatenate([pos[:2 * P], pos[2 * P::WIN]]))
    dft_lat = np.stack([np.cos(lat), np.sin(lat)], 1) / np.sqrt(LAT * P)
    ctx = angles(CTX, ctx_pos, ctx_pos[:P + 1])
    dft_ctx = np.stack([np.cos(ctx), np.sin(ctx)], 1) / np.sqrt(CTX * P)
    dft_lat = dft_lat.reshape(LT, P, 2, FREQ_L).transpose(1, 0, 2, 3)
    dft_ctx = dft_ctx.reshape(CT, P, 2, FREQ_X).transpose(1, 0, 2, 3)
    return [np.ascontiguousarray(a, np.float32) for a in (ident, rope, dft_ch, dft_lat, dft_ctx)]


def lay_out(x, c, ctx, c_ctx, w_ada, b_ada, w_in, q_norm, k_norm, rpb, w_branch, w_out, ln1_g, ln1_b, w_gu, w_down,
            ln2_g, ln2_b):
    swap = np.arange(HD).reshape(2, 2, HD // 4)[:, ::-1].reshape(HD)
    ident, rope, dft_ch, dft_lat, dft_ctx = shape_tables()
    return {
        "x_in": x[0][latent_order()],
        "ctx_in": ctx[0][context_order()],
        "cond": np.stack([c[0], c_ctx], 0),
        "cond_cols": np.stack([c[0].reshape(KD, P).T, c_ctx.reshape(KD, P).T], 2),
        "w_first": w_ada[0][:, :ADA_FIRST * P].reshape(KD, P, ADA_FIRST * P),
        "w_ada": w_ada.swapaxes(1, 2).reshape(DEPTH * ADA_UNITS, P, D),
        "b_ada": b_ada.reshape(DEPTH * ADA_UNITS, P).T,
        "stream": lay_stream(w_in, w_branch, w_out, w_gu, w_down),
        "qk_gain": np.stack([q_norm, q_norm[:, swap], k_norm, k_norm[:, swap]], 1).reshape(-1),
        "norm_rows": np.stack([np.stack([ln1_g, ln1_b], 1), np.stack([ln2_g, ln2_b], 1)], 1),
        "bias": lay_bias(rpb),
        "ident_in": ident, "rope_in": rope, "dft_ch": dft_ch, "dft_lat": dft_lat, "dft_ctx": dft_ctx,
    }


def program(nc, arrays):
    args = [nc.dram_tensor(f"in_{n}", a.shape, mybir.dt.from_np(a.dtype), kind="ExternalInput").ap()
            for n, a in arrays.items()]
    scratch = nc.dram_tensor("scratch", (2 * DEPTH, ALLT, P, D), F32, kind="Internal").ap()
    out = nc.dram_tensor("out_x", (LT, P, D), F32, kind="ExternalOutput").ap()
    cond_scratch = nc.dram_tensor("cond_scratch", (2, D), F32, kind="Internal").ap()
    build(nc, *args, scratch, cond_scratch, out)


def kernel(**inputs):
    import concourse.bacc as bacc
    from concourse.bass_utils import run_bass_kernel_spmd

    arrays = {n: np.ascontiguousarray(a) for n, a in
              lay_out(**{n: np.asarray(a) for n, a in inputs.items()}).items()}
    nc = bacc.Bacc("TRN2", target_bir_lowering=False, num_devices=1)
    program(nc, arrays)
    r = run_bass_kernel_spmd(nc, [{f"in_{n}": a for n, a in arrays.items()}], core_ids=[0])
    got = np.empty((1, LAT, D), np.float32)
    got[0, latent_order()] = r.results[0]["out_x"].reshape(LAT, D)
    return got
```
